# Optimizing a Trainium2 kernel written in Bass

```python
import math
import jax, jax.numpy as jnp
from jax import lax
import numpy as np

D_MODEL = 1024
BATCH = 1
SEQ = 256
DEPTH = 2

GRID_W = 64
CTX_LEN = 256
HEAD_DIM = 64
BLK = 128
WINDOW = 128
ROPE_THETA = 10000.0
EPS = 1e-6
NEG = -1e30
N_HEADS_A = 8
N_KV_A = 2
GROUP_A = N_HEADS_A // N_KV_A
N_HEADS_B = 8
N_KV_B = 2
GROUP_B = N_HEADS_B // N_KV_B
QA_W = N_HEADS_A * HEAD_DIM
KVA_W = N_KV_A * HEAD_DIM
QB_W = N_HEADS_B * HEAD_DIM
KVB_W = N_KV_B * HEAD_DIM
IN_AB = QA_W + 2 * KVA_W + QB_W + 2 * KVB_W
AB_SPLITS = (QA_W, QA_W + KVA_W, QA_W + 2 * KVA_W, QA_W + 2 * KVA_W + QB_W, QA_W + 2 * KVA_W + QB_W + KVB_W)
MIX_AB = QA_W + QB_W
N_HEADS_C = 8
DV_C = 2 * HEAD_DIM
IN_C = 3 * N_HEADS_C * DV_C
MIX_C = N_HEADS_C * DV_C
N_GROUPS = 4
EXPERTS_PER_GROUP = 8
N_EXPERTS = N_GROUPS * EXPERTS_PER_GROUP
TOP_K = 2
D_EXPERT = 512
N_EVEN = (DEPTH + 1) // 2
N_ODD = DEPTH // 2


def rms_norm(x, g):
    xf = x.astype(jnp.float32)
    y = xf * lax.rsqrt(jnp.mean(xf * xf, axis=-1, keepdims=True) + EPS)
    return (y * g.astype(jnp.float32)).astype(x.dtype)

def modulate(x, g, shift, scale):
    return rms_norm(x, g) * (1 + scale) + shift

def axial_rope_tables(rows_n):
    rows = jnp.broadcast_to(jnp.arange(rows_n, dtype=jnp.float32)[:, None], (rows_n, GRID_W)).reshape(-1)
    cols = jnp.broadcast_to(jnp.arange(GRID_W, dtype=jnp.float32)[None, :], (rows_n, GRID_W)).reshape(-1)
    half = HEAD_DIM // 2
    inv = ROPE_THETA ** (-jnp.arange(0, half, 2, dtype=jnp.float32) / half)
    ang = jnp.concatenate([rows[:, None] * inv, cols[:, None] * inv], axis=-1)
    return jnp.cos(ang), jnp.sin(ang)

def apply_rope(x, cos, sin):
    shp = (1, cos.shape[0]) + (1,) * (x.ndim - 3) + (cos.shape[1],)
    cos = cos.reshape(shp)
    sin = sin.reshape(shp)
    x1, x2 = jnp.split(x.astype(jnp.float32), 2, axis=-1)
    return jnp.concatenate([x1 * cos - x2 * sin, x2 * cos + x1 * sin], axis=-1).astype(x.dtype)

def gqa_sweep(q, k, v):
    b, l, hkv, g, d = q.shape
    qb = q.reshape(b, l // BLK, BLK, hkv, g, d).transpose(1, 0, 2, 3, 4, 5)
    scale = d ** -0.5

    def one_block(qi):
        s = jnp.einsum('bqhgd,bkhd->bhgqk', qi, k).astype(jnp.float32) * scale
        p = jax.nn.softmax(s, axis=-1).astype(v.dtype)
        return jnp.einsum('bhgqk,bkhd->bqhgd', p, v)

    o = lax.map(one_block, qb)
    return o.transpose(1, 0, 2, 3, 4, 5).reshape(b, l, hkv, g, d)

def window_sink_attention(q, k, v, kc, vc, sink):
    b, seq, hkv, g, d = q.shape
    nb = seq // BLK
    qb = q.reshape(b, nb, BLK, hkv, g, d)

    def bands(t):
        tp = jnp.pad(t, ((0, 0), (BLK, BLK), (0, 0), (0, 0))).reshape(b, nb + 2, BLK, hkv, d)
        return jnp.concatenate([tp[:, :-2], tp[:, 1:-1], tp[:, 2:]], axis=2)

    kw, vw = bands(k), bands(v)
    qi = jnp.arange(BLK)[:, None]
    ki = jnp.arange(3 * BLK)[None, :]
    rel = ki - BLK - qi
    kpos = jnp.arange(nb)[:, None, None] * BLK + ki[None] - BLK
    mask = (jnp.abs(rel)[None] <= WINDOW) & (kpos >= 0) & (kpos < seq)
    scale = d ** -0.5
    s_loc = jnp.einsum('bnqhgd,bnkhd->bnhgqk', qb, kw).astype(jnp.float32) * scale
    s_loc = jnp.where(mask[None, :, None, None], s_loc, NEG)
    s_ctx = jnp.einsum('bnqhgd,bchd->bnhgqc', qb, kc).astype(jnp.float32) * scale
    sink_col = jnp.broadcast_to(sink.astype(jnp.float32)[None, None, :, :, None, None], s_loc.shape[:-1] + (1,))
    p = jax.nn.softmax(jnp.concatenate([s_loc, s_ctx, sink_col], axis=-1), axis=-1).astype(v.dtype)
    o = (jnp.einsum('bnhgqk,bnkhd->bnqhgd', p[..., :3 * BLK], vw)
         + jnp.einsum('bnhgqc,bchd->bnqhgd', p[..., 3 * BLK:-1], vc))
    return o.reshape(b, seq, hkv, g, d)

def ctx_sink_attention(q, k, v, sink):
    scale = q.shape[-1] ** -0.5
    s = jnp.einsum('bqhgd,bkhd->bhgqk', q, k).astype(jnp.float32) * scale
    sink_col = jnp.broadcast_to(sink.astype(jnp.float32)[None, :, :, None, None], s.shape[:-1] + (1,))
    p = jax.nn.softmax(jnp.concatenate([s, sink_col], axis=-1), axis=-1)[..., :-1].astype(v.dtype)
    return jnp.einsum('bhgqk,bkhd->bqhgd', p, v)

def diff_sweep(q, k, v, lam):
    b, l, h, _, d = q.shape
    qb = q.reshape(b, l // BLK, BLK, h, 2, d).transpose(1, 0, 2, 3, 4, 5)
    scale = d ** -0.5

    def one_block(qi):
        s = jnp.einsum('bqhcd,bkhcd->bhcqk', qi, k).astype(jnp.float32) * scale
        p = jax.nn.softmax(s, axis=-1)
        a = p[:, :, 0] - lam * p[:, :, 1]
        return jnp.einsum('bhqk,bkhe->bqhe', a.astype(v.dtype), v)

    o = lax.map(one_block, qb)
    return o.transpose(1, 0, 2, 3, 4).reshape(b, l, h, v.shape[-1])

def mixer_ab(h_lat, h_ctx, cos, sin, w_in, w_out, qn_a, kn_a, sink_a, qn_b, kn_b, with_ctx_out):
    def project(h, rope):
        bb, ll, _ = h.shape
        qa, ka, va, qb, kb, vb = jnp.split(h @ w_in, AB_SPLITS, axis=-1)
        qa = rms_norm(qa.reshape(bb, ll, N_KV_A, GROUP_A, HEAD_DIM), qn_a)
        ka = rms_norm(ka.reshape(bb, ll, N_KV_A, HEAD_DIM), kn_a)
        va = va.reshape(bb, ll, N_KV_A, HEAD_DIM)
        qb = rms_norm(qb.reshape(bb, ll, N_KV_B, GROUP_B, HEAD_DIM), qn_b)
        kb = rms_norm(kb.reshape(bb, ll, N_KV_B, HEAD_DIM), kn_b)
        vb = vb.reshape(bb, ll, N_KV_B, HEAD_DIM)
        if rope:
            qa, ka = apply_rope(qa, cos, sin), apply_rope(ka, cos, sin)
            qb, kb = apply_rope(qb, cos, sin), apply_rope(kb, cos, sin)
        return qa, ka, va, qb, kb, vb

    b, seq, _ = h_lat.shape
    qa, ka, va, qb, kb, vb = project(h_lat, True)
    cqa, cka, cva, cqb, ckb, cvb = project(h_ctx, False)
    sink = sink_a.reshape(N_KV_A, GROUP_A)
    oa = window_sink_attention(qa, ka, va, cka, cva, sink)
    ob = gqa_sweep(qb, jnp.concatenate([kb, ckb], axis=1), jnp.concatenate([vb, cvb], axis=1))
    o_lat = jnp.concatenate([oa.reshape(b, seq, QA_W), ob.reshape(b, seq, QB_W)], axis=-1) @ w_out
    o_ctx = None
    if with_ctx_out:
        cl = h_ctx.shape[1]
        oca = ctx_sink_attention(cqa, cka, cva, sink)
        ocb = gqa_sweep(cqb, ckb, cvb)
        o_ctx = jnp.concatenate([oca.reshape(b, cl, QA_W), ocb.reshape(b, cl, QB_W)], axis=-1) @ w_out
    return o_lat, o_ctx

def mixer_c(h_lat, h_ctx, cos, sin, w_in, w_out, qn, kn, lam_p, subln, lam_init, with_ctx_out):
    lp = lam_p.astype(jnp.float32)
    lam = jnp.exp(jnp.sum(lp[0] * lp[1])) - jnp.exp(jnp.sum(lp[2] * lp[3])) + lam_init

    def project(h, rope):
        bb, ll, _ = h.shape
        q, k, v = jnp.split(h @ w_in, 3, axis=-1)
        q = rms_norm(q.reshape(bb, ll, N_HEADS_C, 2, HEAD_DIM), qn)
        k = rms_norm(k.reshape(bb, ll, N_HEADS_C, 2, HEAD_DIM), kn)
        v = v.reshape(bb, ll, N_HEADS_C, DV_C)
        if rope:
            q, k = apply_rope(q, cos, sin), apply_rope(k, cos, sin)
        return q, k, v

    def finish(o):
        o = rms_norm(o, subln) * (1 - lam_init)
        return o.reshape(o.shape[0], o.shape[1], MIX_C) @ w_out

    q_l, k_l, v_l = project(h_lat, True)
    q_c, k_c, v_c = project(h_ctx, False)
    o_lat = finish(diff_sweep(q_l, jnp.concatenate([k_l, k_c], axis=1), jnp.concatenate([v_l, v_c], axis=1), lam))
    o_ctx = finish(diff_sweep(q_c, k_c, v_c, lam)) if with_ctx_out else None
    return o_lat, o_ctx

def hier_moe(h, w_group, b_group, w_expert, b_expert, w1, w3, w2):
    t, d = h.shape
    pg = jax.nn.softmax((h @ w_group).astype(jnp.float32) + b_group.astype(jnp.float32), axis=-1)
    g_prob, g_idx = lax.top_k(pg, 1)
    le = ((h @ w_expert).astype(jnp.float32) + b_expert.astype(jnp.float32)).reshape(t, N_GROUPS, EXPERTS_PER_GROUP)
    le = jnp.take_along_axis(le, g_idx[:, :, None], axis=1)[:, 0]
    e_prob, e_idx = lax.top_k(jax.nn.softmax(le, axis=-1), TOP_K)
    weights = g_prob * e_prob / jnp.sum(e_prob, axis=-1, keepdims=True)
    expert_id = g_idx * EXPERTS_PER_GROUP + e_idx
    flat_e = expert_id.reshape(-1)
    flat_tok = jnp.repeat(jnp.arange(t), TOP_K)
    flat_w = weights.reshape(-1)
    order = jnp.argsort(flat_e)
    se, stok, sw = flat_e[order], flat_tok[order], flat_w[order]
    counts = jnp.bincount(flat_e, length=N_EXPERTS)
    padded = (counts + BLK - 1) // BLK * BLK
    start = jnp.cumsum(counts) - counts
    pend = jnp.cumsum(padded)
    dest = (pend - padded)[se] + jnp.arange(flat_e.shape[0]) - start[se]
    n_rows = (t * TOP_K + BLK - 1) // BLK * BLK + N_EXPERTS * BLK
    n_blk = n_rows // BLK
    buf = jnp.zeros((n_rows, d), h.dtype).at[dest].set(h[stok])
    blk_e = jnp.minimum(jnp.searchsorted(pend, jnp.arange(n_blk) * BLK, side='right'), N_EXPERTS - 1)

    def expert_block(args):
        xb, e = args
        return (jax.nn.silu(xb @ w1[e]) * (xb @ w3[e])) @ w2[e]

    yb = lax.map(expert_block, (buf.reshape(n_blk, BLK, d), blk_e))
    y = yb.reshape(n_rows, d)[dest] * sw[:, None].astype(h.dtype)
    return jnp.zeros_like(h).at[stok].add(y)

def first_inputs(seed: int = 0) -> dict:
    key = jax.random.key(seed)
    ks = iter(jax.random.split(key, 40))

    def nrm(shape, scale):
        return jax.random.normal(next(ks), shape, jnp.float32) * scale

    D = D_MODEL
    return {
        'x': nrm((BATCH, SEQ, D), 1.0),
        'c': nrm((BATCH, D), 1.0),
        'ctx': nrm((BATCH, CTX_LEN, D), 1.0),
        'c_ctx': nrm((D,), 1.0),
        'w_mod': nrm((DEPTH, D, 6 * D), 0.5 * D ** -0.5),
        'b_mod': nrm((DEPTH, 6 * D), 0.01),
        'norm_mix': 1.0 + nrm((DEPTH, D), 0.05),
        'norm_ffn': 1.0 + nrm((DEPTH, D), 0.05),
        'w_in_ab': nrm((N_EVEN, D, IN_AB), D ** -0.5),
        'w_out_ab': nrm((N_EVEN, MIX_AB, D), MIX_AB ** -0.5),
        'qn_a': 1.0 + nrm((N_EVEN, HEAD_DIM), 0.05),
        'kn_a': 1.0 + nrm((N_EVEN, HEAD_DIM), 0.05),
        'sink_a': nrm((N_EVEN, N_HEADS_A), 0.5),
        'qn_b': 1.0 + nrm((N_EVEN, HEAD_DIM), 0.05),
        'kn_b': 1.0 + nrm((N_EVEN, HEAD_DIM), 0.05),
        'w_in_c': nrm((N_ODD, D, IN_C), D ** -0.5),
        'w_out_c': nrm((N_ODD, MIX_C, D), MIX_C ** -0.5),
        'qn_c': 1.0 + nrm((N_ODD, HEAD_DIM), 0.05),
        'kn_c': 1.0 + nrm((N_ODD, HEAD_DIM), 0.05),
        'lam_c': nrm((N_ODD, 4, HEAD_DIM), 0.1),
        'subln_c': 1.0 + nrm((N_ODD, DV_C), 0.05),
        'w_group': nrm((DEPTH, D, N_GROUPS), D ** -0.5),
        'b_group': nrm((DEPTH, N_GROUPS), 0.01),
        'w_expert': nrm((DEPTH, D, N_EXPERTS), D ** -0.5),
        'b_expert': nrm((DEPTH, N_EXPERTS), 0.01),
        'w1': nrm((DEPTH, N_EXPERTS, D, D_EXPERT), D ** -0.5),
        'w3': nrm((DEPTH, N_EXPERTS, D, D_EXPERT), D ** -0.5),
        'w2': nrm((DEPTH, N_EXPERTS, D_EXPERT, D), D_EXPERT ** -0.5),
    }

def first_block(x, c, ctx, c_ctx, w_mod, b_mod, norm_mix, norm_ffn, w_in_ab, w_out_ab, qn_a, kn_a, sink_a,
              qn_b, kn_b, w_in_c, w_out_c, qn_c, kn_c, lam_c, subln_c, w_group, b_group, w_expert, b_expert,
              w1, w3, w2):
    b, s_lat, d = x.shape
    c_len = ctx.shape[1]
    rows_n = s_lat // GRID_W
    cos, sin = axial_rope_tables(rows_n)
    for l in range(DEPTH):
        last = l == DEPTH - 1
        i = l // 2
        mod = jax.nn.silu(c) @ w_mod[l] + b_mod[l]
        mod_c = jax.nn.silu(c_ctx) @ w_mod[l] + b_mod[l]
        sh1, sc1, gt1, sh2, sc2, gt2 = jnp.split(mod[:, None, :], 6, axis=-1)
        csh1, csc1, cgt1, csh2, csc2, cgt2 = jnp.split(mod_c, 6, axis=-1)
        h_lat = modulate(x, norm_mix[l], sh1, sc1)
        h_ctx = modulate(ctx, norm_mix[l], csh1, csc1)
        if l % 2 == 0:
            o_lat, o_ctx = mixer_ab(h_lat, h_ctx, cos, sin, w_in_ab[i], w_out_ab[i], qn_a[i], kn_a[i], sink_a[i],
                                    qn_b[i], kn_b[i], not last)
        else:
            lam_init = 0.8 - 0.6 * math.exp(-0.3 * l)
            o_lat, o_ctx = mixer_c(h_lat, h_ctx, cos, sin, w_in_c[i], w_out_c[i], qn_c[i], kn_c[i], lam_c[i],
                                   subln_c[i], lam_init, not last)
        x = x + gt1 * o_lat
        if not last:
            ctx = ctx + cgt1 * o_ctx
            tokens = jnp.concatenate([modulate(ctx, norm_ffn[l], csh2, csc2),
                                      modulate(x, norm_ffn[l], sh2, sc2)], axis=1).reshape(-1, d)
            f = hier_moe(tokens, w_group[l], b_group[l], w_expert[l], b_expert[l], w1[l], w3[l], w2[l])
            f = f.reshape(b, c_len + s_lat, d)
            ctx = ctx + cgt2 * f[:, :c_len]
            x = x + gt2 * f[:, c_len:]
        else:
            tokens = modulate(x, norm_ffn[l], sh2, sc2).reshape(-1, d)
            f = hier_moe(tokens, w_group[l], b_group[l], w_expert[l], b_expert[l], w1[l], w3[l], w2[l])
            x = x + gt2 * f.reshape(b, s_lat, d)
    return x


NSA_HEADS = 8
NSA_KV_GROUPS = 2
NSA_HEAD_DIM = 64
NSA_BRANCHES = 3
CMP_BLOCK = 32
CMP_STRIDE = 16
CMP_HIDDEN = 256
SEL_BLOCK = 64
N_SELECT = 16
N_LOCAL = 2
WINDOW_2 = 512
NSA_Q_CHUNK = 64

MLA_HEADS = 8
MLA_NOPE_DIM = 64
MLA_ROPE_DIM = 32
MLA_V_DIM = 64
Q_LORA_RANK = 256
KV_LORA_RANK = 128
ATTN_BLOCK = 128

D_FF = 4 * D_MODEL
NORM_EPS = 1e-6
NEG_INF = -1e30
FORCE_BONUS = 1e4

NSA_WIDTH = NSA_HEADS * NSA_HEAD_DIM
NSA_KV_WIDTH = NSA_KV_GROUPS * NSA_HEAD_DIM
MLA_WIDTH = MLA_HEADS * MLA_V_DIM
MIX_WIDTH = NSA_WIDTH + MLA_WIDTH
IN_SIZES = (NSA_WIDTH, NSA_KV_WIDTH, NSA_KV_WIDTH, NSA_KV_WIDTH, NSA_KV_WIDTH,
            NSA_KV_WIDTH, NSA_KV_WIDTH, NSA_BRANCHES * NSA_HEADS,
            Q_LORA_RANK, KV_LORA_RANK, MLA_ROPE_DIM)
IN_WIDTH = sum(IN_SIZES)


def _rms_norm(x, gain):
    xf = x.astype(jnp.float32)
    y = xf * lax.rsqrt(jnp.mean(xf * xf, axis=-1, keepdims=True) + NORM_EPS)
    return (y * gain.astype(jnp.float32)).astype(x.dtype)

def _rope_tables(seq, dim, dtype):
    inv_freq = 1.0 / (ROPE_THETA ** (jnp.arange(0, dim, 2, dtype=jnp.float32) / dim))
    ang = jnp.arange(seq, dtype=jnp.float32)[:, None] * inv_freq[None, :]
    ang = jnp.concatenate([ang, ang], axis=-1)
    return jnp.cos(ang).astype(dtype), jnp.sin(ang).astype(dtype)

def _rope(x, cos, sin):
    half = x.shape[-1] // 2
    rot = jnp.concatenate([-x[..., half:], x[..., :half]], axis=-1)
    return x * cos[:, None, :] + rot * sin[:, None, :]

def _masked_softmax(s, mask):
    s = jnp.where(mask, s, NEG_INF)
    m = jnp.max(s, axis=-1, keepdims=True)
    e = jnp.where(mask, jnp.exp(s - m), 0.0)
    return e / jnp.maximum(jnp.sum(e, axis=-1, keepdims=True), 1e-30)

def _heads(t, n):
    b, s, w = t.shape
    return t.reshape(b, s, n, w // n)

def _compress(kv, pos_emb, w1, w2):
    B, S, G, dk = kv.shape
    ratio = CMP_BLOCK // CMP_STRIDE
    n_cmp = S // CMP_STRIDE - ratio + 1
    chunks = kv.reshape(B, S // CMP_STRIDE, CMP_STRIDE, G, dk)
    blocks = jnp.concatenate([chunks[:, i:i + n_cmp] for i in range(ratio)], axis=2)
    blocks = blocks + pos_emb[None, None, :, None, :]
    flat = jnp.swapaxes(blocks, 2, 3).reshape(B, n_cmp, G, CMP_BLOCK * dk)
    return jax.nn.silu(flat @ w1) @ w2

def _nsa(q, k_cmp, v_cmp, k_sel, v_sel, k_win, v_win, gates):
    B, S, H, dk = q.shape
    G = k_sel.shape[2]
    R = H // G
    n_cmp = k_cmp.shape[1]
    n_blk = S // SEL_BLOCK
    n_sel = min(N_SELECT, n_blk)
    QC = NSA_Q_CHUNK
    scale = dk ** -0.5
    qg = q.reshape(B, S, G, R, dk)
    gg = gates.reshape(B, S, G, R, NSA_BRANCHES)
    k_blocks = k_sel.reshape(B, n_blk, SEL_BLOCK, G, dk).transpose(0, 3, 1, 2, 4)
    v_blocks = v_sel.reshape(B, n_blk, SEL_BLOCK, G, dk).transpose(0, 3, 1, 2, 4)
    pad = ((0, 0), (WINDOW_2, 0), (0, 0), (0, 0))
    k_win_pad = jnp.pad(k_win, pad)
    v_win_pad = jnp.pad(v_win, pad)
    cmp_end = jnp.arange(n_cmp) * CMP_STRIDE + CMP_BLOCK - 1
    blk_ids = jnp.arange(n_blk)
    a = SEL_BLOCK // CMP_STRIDE
    b = CMP_BLOCK // CMP_STRIDE
    overlap = np.convolve(np.ones(a), np.ones(b))
    bi = jnp.arange(B)[:, None, None, None]
    gi = jnp.arange(G)[None, :, None, None]

    def chunk(c):
        s0 = c * QC
        t = s0 + jnp.arange(QC)
        qc = lax.dynamic_slice_in_dim(qg, s0, QC, axis=1)
        gc = lax.dynamic_slice_in_dim(gg, s0, QC, axis=1)
        s_cmp = jnp.einsum('bqgrd,bngd->bgrqn', qc, k_cmp, preferred_element_type=jnp.float32) * scale
        p_cmp = _masked_softmax(s_cmp, cmp_end[None, :] <= t[:, None])
        o_cmp = jnp.einsum('bgrqn,bngd->bqgrd', p_cmp.astype(v_cmp.dtype), v_cmp)
        imp = jnp.pad(p_cmp.sum(axis=2), ((0, 0), (0, 0), (0, 0), (b - 1, b - 1)))
        imp_blk = sum(float(overlap[j]) * imp[..., j:j + a * (n_blk - 1) + 1:a] for j in range(a + b - 1))
        cur = t // SEL_BLOCK
        valid = blk_ids[None, :] <= cur[:, None]
        forced = valid & ((blk_ids[None, :] == 0) | (blk_ids[None, :] > cur[:, None] - N_LOCAL))
        score = jnp.where(forced, FORCE_BONUS, jnp.where(valid, imp_blk, -1.0))
        _, idx = lax.top_k(score, n_sel)
        k_g = k_blocks[bi, gi, idx]
        v_g = v_blocks[bi, gi, idx]
        key_pos = idx[..., None] * SEL_BLOCK + jnp.arange(SEL_BLOCK)
        m_sel = (key_pos <= t[:, None, None]).reshape(B, G, 1, QC, n_sel * SEL_BLOCK)
        s_sel = jnp.einsum('bqgrd,bgqnkd->bgrqnk', qc, k_g, preferred_element_type=jnp.float32) * scale
        p_sel = _masked_softmax(s_sel.reshape(B, G, R, QC, n_sel * SEL_BLOCK), m_sel)
        o_sel = jnp.einsum('bgrqj,bgqjd->bqgrd', p_sel.astype(v_g.dtype),
                           v_g.reshape(B, G, QC, n_sel * SEL_BLOCK, dk))
        kw = lax.dynamic_slice_in_dim(k_win_pad, s0, WINDOW_2 + QC, axis=1)
        vw = lax.dynamic_slice_in_dim(v_win_pad, s0, WINDOW_2 + QC, axis=1)
        win_pos = s0 - WINDOW_2 + jnp.arange(WINDOW_2 + QC)
        m_win = ((win_pos[None, :] <= t[:, None]) & (win_pos[None, :] > t[:, None] - WINDOW_2)
                 & (win_pos[None, :] >= 0))
        s_win = jnp.einsum('bqgrd,bkgd->bgrqk', qc, kw, preferred_element_type=jnp.float32) * scale
        p_win = _masked_softmax(s_win, m_win)
        o_win = jnp.einsum('bgrqk,bkgd->bqgrd', p_win.astype(vw.dtype), vw)
        return gc[..., 0:1] * o_cmp + gc[..., 1:2] * o_sel + gc[..., 2:3] * o_win

    out = lax.map(chunk, jnp.arange(S // QC))
    return jnp.swapaxes(out, 0, 1).reshape(B, S, H * dk)

def _causal_attention(q, k, v):
    B, S, H, dk = q.shape
    dv = v.shape[-1]
    scale = dk ** -0.5
    kpos = jnp.arange(S)

    def block(c):
        s0 = c * ATTN_BLOCK
        qb = lax.dynamic_slice_in_dim(q, s0, ATTN_BLOCK, axis=1)
        s = jnp.einsum('bqhd,bkhd->bhqk', qb, k, preferred_element_type=jnp.float32) * scale
        mask = kpos[None, :] <= (s0 + jnp.arange(ATTN_BLOCK))[:, None]
        p = _masked_softmax(s, mask)
        return jnp.einsum('bhqk,bkhd->bqhd', p.astype(v.dtype), v)

    out = lax.map(block, jnp.arange(S // ATTN_BLOCK))
    return jnp.swapaxes(out, 0, 1).reshape(B, S, H, dv)

def _mla(c_q, c_kv, k_rope, q_norm, w_q_up, kv_norm, w_kv_up, cos, sin):
    B, S, _ = c_q.shape
    q = (_rms_norm(c_q, q_norm) @ w_q_up).reshape(B, S, MLA_HEADS, MLA_NOPE_DIM + MLA_ROPE_DIM)
    q = jnp.concatenate([q[..., :MLA_NOPE_DIM], _rope(q[..., MLA_NOPE_DIM:], cos, sin)], axis=-1)
    kv = (_rms_norm(c_kv, kv_norm) @ w_kv_up).reshape(B, S, MLA_HEADS, MLA_NOPE_DIM + MLA_V_DIM)
    k_nope, v = kv[..., :MLA_NOPE_DIM], kv[..., MLA_NOPE_DIM:]
    k_pe = _rope(k_rope[:, :, None, :], cos, sin)
    k = jnp.concatenate([k_nope, jnp.broadcast_to(k_pe, (B, S, MLA_HEADS, MLA_ROPE_DIM))], axis=-1)
    return _causal_attention(q, k, v).reshape(B, S, MLA_WIDTH)

def second_inputs(seed: int = 0) -> dict:
    key = jax.random.key(seed)
    ks = jax.random.split(key, 20)
    L = DEPTH
    dk = NSA_HEAD_DIM

    def dense(k, shape, fan_in):
        return jax.random.normal(k, shape, jnp.float32) * fan_in ** -0.5

    def gain(k, shape):
        return 1.0 + 0.02 * jax.random.normal(k, shape, jnp.float32)

    return {
        "x": jax.random.normal(ks[0], (BATCH, SEQ, D_MODEL), jnp.float32),
        "attn_norm": gain(ks[1], (L, D_MODEL)),
        "w_in": dense(ks[2], (L, D_MODEL, IN_WIDTH), D_MODEL),
        "cmp_pos_k": 0.1 * jax.random.normal(ks[3], (L, CMP_BLOCK, dk), jnp.float32),
        "cmp_w1_k": dense(ks[4], (L, CMP_BLOCK * dk, CMP_HIDDEN), CMP_BLOCK * dk),
        "cmp_w2_k": dense(ks[5], (L, CMP_HIDDEN, dk), CMP_HIDDEN),
        "cmp_pos_v": 0.1 * jax.random.normal(ks[6], (L, CMP_BLOCK, dk), jnp.float32),
        "cmp_w1_v": dense(ks[7], (L, CMP_BLOCK * dk, CMP_HIDDEN), CMP_BLOCK * dk),
        "cmp_w2_v": dense(ks[8], (L, CMP_HIDDEN, dk), CMP_HIDDEN),
        "mla_q_norm": gain(ks[9], (L, Q_LORA_RANK)),
        "w_q_up": dense(ks[10], (L, Q_LORA_RANK, MLA_HEADS * (MLA_NOPE_DIM + MLA_ROPE_DIM)), Q_LORA_RANK),
        "mla_kv_norm": gain(ks[11], (L, KV_LORA_RANK)),
        "w_kv_up": dense(ks[12], (L, KV_LORA_RANK, MLA_HEADS * (MLA_NOPE_DIM + MLA_V_DIM)), KV_LORA_RANK),
        "nsa_out_norm": gain(ks[13], (L, NSA_WIDTH)),
        "mla_out_norm": gain(ks[14], (L, MLA_WIDTH)),
        "w_out": dense(ks[15], (L, MIX_WIDTH, D_MODEL), MIX_WIDTH),
        "mlp_norm": gain(ks[16], (L, D_MODEL)),
        "w_ff1": dense(ks[17], (L, D_MODEL, D_FF), D_MODEL),
        "w_ff2": dense(ks[18], (L, D_FF, D_MODEL), D_FF),
        "final_norm": gain(ks[19], (D_MODEL,)),
    }

def second_block(x, attn_norm, w_in, cmp_pos_k, cmp_w1_k, cmp_w2_k, cmp_pos_v, cmp_w1_v, cmp_w2_v,
              mla_q_norm, w_q_up, mla_kv_norm, w_kv_up, nsa_out_norm, mla_out_norm, w_out,
              mlp_norm, w_ff1, w_ff2, final_norm):
    B, S, _ = x.shape
    cos_a, sin_a = _rope_tables(S, NSA_HEAD_DIM, x.dtype)
    cos_b, sin_b = _rope_tables(S, MLA_ROPE_DIM, x.dtype)
    offsets = [int(o) for o in np.cumsum(IN_SIZES)[:-1]]
    G = NSA_KV_GROUPS
    for l in range(DEPTH):
        h = _rms_norm(x, attn_norm[l])
        proj = h @ w_in[l]
        (q_a, k_c, v_c, k_s, v_s, k_w, v_w, g_a, c_q, c_kv, k_r) = jnp.split(proj, offsets, axis=-1)
        q_a = _rope(_heads(q_a, NSA_HEADS), cos_a, sin_a)
        k_cmp = _compress(_rope(_heads(k_c, G), cos_a, sin_a), cmp_pos_k[l], cmp_w1_k[l], cmp_w2_k[l])
        v_cmp = _compress(_heads(v_c, G), cmp_pos_v[l], cmp_w1_v[l], cmp_w2_v[l])
        gates = jax.nn.sigmoid(g_a).reshape(B, S, NSA_HEADS, NSA_BRANCHES)
        o_a = _nsa(q_a, k_cmp, v_cmp,
                   _rope(_heads(k_s, G), cos_a, sin_a), _heads(v_s, G),
                   _rope(_heads(k_w, G), cos_a, sin_a), _heads(v_w, G), gates)
        o_b = _mla(c_q, c_kv, k_r, mla_q_norm[l], w_q_up[l], mla_kv_norm[l], w_kv_up[l], cos_b, sin_b)
        mixed = jnp.concatenate([_rms_norm(o_a, nsa_out_norm[l]), _rms_norm(o_b, mla_out_norm[l])], axis=-1)
        x = x + mixed @ w_out[l]
        h = _rms_norm(x, mlp_norm[l])
        x = x + jnp.square(jax.nn.relu(h @ w_ff1[l])) @ w_ff2[l]
    return _rms_norm(x, final_norm)


def setup_inputs(seed=0):
    out = dict(first_inputs(seed))
    for name, value in second_inputs(seed + 1).items():
        if name != "x":
            out[name + "_2"] = value
    return out


def reference(
    x, c, ctx, c_ctx, w_mod, b_mod, norm_mix, norm_ffn, w_in_ab, w_out_ab, qn_a, kn_a, sink_a,
    qn_b, kn_b, w_in_c, w_out_c, qn_c, kn_c, lam_c, subln_c, w_group, b_group, w_expert,
    b_expert, w1, w3, w2, attn_norm_2, w_in_2, cmp_pos_k_2, cmp_w1_k_2, cmp_w2_k_2, cmp_pos_v_2,
    cmp_w1_v_2, cmp_w2_v_2, mla_q_norm_2, w_q_up_2, mla_kv_norm_2, w_kv_up_2, nsa_out_norm_2,
    mla_out_norm_2, w_out_2, mlp_norm_2, w_ff1_2, w_ff2_2, final_norm_2,
):
    x = first_block(
        x, c, ctx, c_ctx, w_mod, b_mod, norm_mix, norm_ffn, w_in_ab, w_out_ab, qn_a, kn_a,
        sink_a, qn_b, kn_b, w_in_c, w_out_c, qn_c, kn_c, lam_c, subln_c, w_group, b_group,
        w_expert, b_expert, w1, w3, w2,
    )
    return second_block(
        x, attn_norm_2, w_in_2, cmp_pos_k_2, cmp_w1_k_2, cmp_w2_k_2, cmp_pos_v_2, cmp_w1_v_2,
        cmp_w2_v_2, mla_q_norm_2, w_q_up_2, mla_kv_norm_2, w_kv_up_2, nsa_out_norm_2,
        mla_out_norm_2, w_out_2, mlp_norm_2, w_ff1_2, w_ff2_2, final_norm_2,
    )


_drawn_inputs = setup_inputs


def setup_inputs(seed=0):
    import zlib

    import numpy as np

    out = dict(_drawn_inputs(seed))
    spreads = {}
    factors = {'norm_mix': 3.235,
     'qn_a': 8.0,
     'kn_a': 8.0,
     'sink_a': 8.0,
     'qn_b': 8.0,
     'kn_b': 8.0,
     'qn_c': 6.568,
     'kn_c': 6.87,
     'lam_c': 2.722,
     'b_group': 5.61,
     'b_expert': 8.0,
     'cmp_pos_k_2': 7.8,
     'mla_q_norm_2': 8.0,
     'mla_kv_norm_2': 3.194,
     'nsa_out_norm_2': 4.353,
     'mla_out_norm_2': 4.192,
     'mlp_norm_2': 2.843}
    for name, (base, spread) in spreads.items():
        noise = np.random.default_rng([zlib.crc32(name.encode()), seed]).standard_normal(out[name].shape)
        drawn = base * np.exp(spread * noise) if base else spread * noise
        out[name] = __import__('jax').numpy.asarray(drawn.astype(out[name].dtype))
    for name, factor in factors.items():
        out[name] = (out[name] * factor).astype(out[name].dtype)
    return out
```

```python
from contextlib import ExitStack, contextmanager

import numpy as np

import concourse.bass as bass
from concourse import mybir

P = 128
D = 1024
KB = D // P
DEPTH = 2
SEQ = 256
CTX = 256
TOK = SEQ + CTX
HD = 64
NEG = -1e30
EPS = 1e-6
GROUPS, PER_GROUP, EXPERTS = 4, 8, 32
ROUTES = GROUPS + EXPERTS
SLOTS = 64
PAIRS = EXPERTS // 2
DFF = 4096
SCALE = HD ** -0.5
MLA_D = 96
MLA_SCALE = MLA_D ** -0.5
LAM_INIT = 0.8 - 0.6 * float(np.exp(-0.3))
IN2 = 1720
IN2_PAD = 2048
Q2, KC2, VC2, KS2, VS2, KW2, VW2, GA2, CQ2, CKV2, KR2 = 0, 512, 640, 768, 896, 1024, 1152, 1280, 1304, 1560, 1688
RING = 6
CHUNK = 4 * 512

PARAMS = [
    ("c", 2 * KB), ("norm_mix", 2 * KB), ("norm_ffn", 2 * KB), ("head_gain", 6 * HD), ("sink", 8), ("lam", 4 * HD),
    ("subln", 128), ("w_route", 2 * KB * ROUTES), ("b_route", 2 * ROUTES), ("attn_norm", 2 * KB), ("q_norm", 4),
    ("kv_norm", 2), ("mix_norm", 2 * KB), ("mlp_norm", 2 * KB), ("pos_k", 32), ("pos_v", 32),
    ("cmp_w2k", 2 * 2 * 128), ("cmp_w2v", 2 * 2 * 64),
]
CONSTS = [
    ("ident", 128), ("cos_ax", 128), ("sin_ax", 128), ("cos_a", 128), ("sin_a", 128), ("cos_b", 64), ("sin_b", 64),
    ("window", 512), ("causal", 128), ("cmp_add", 32), ("cmp_keep", 32), ("before", 128), ("ones", 128),
    ("slot", P), ("rank_e", EXPERTS), ("rank_g", GROUPS), ("fold", 2), ("spread", 256), ("block_diag", 8),
]


def offsets(spec):
    at, out = 0, {}
    for name, width in spec:
        out[name] = (at, width)
        at += width
    return out, at


def constants():
    c = {}
    part = np.arange(P)
    c["ident"] = np.eye(P)

    def rope(cos, sin):
        cc, ss = np.concatenate([cos, cos], -1), np.concatenate([-sin, sin], -1)
        return [t.reshape(2, P, -1).transpose(1, 0, 2).reshape(P, -1) for t in (cc, ss)]

    half = HD // 2
    inv = (np.float32(10000.0) ** (-np.arange(0, half, 2, dtype=np.float32) / half)).astype(np.float32)
    rows, cols = np.repeat(np.arange(4, dtype=np.float32), 64), np.tile(np.arange(64, dtype=np.float32), 4)
    ang = np.concatenate([rows[:, None] * inv, cols[:, None] * inv], -1)
    c["cos_ax"], c["sin_ax"] = rope(np.cos(ang), np.sin(ang))
    for name, dim in (("a", HD), ("b", 32)):
        inv = (np.float32(1.0) / (np.float32(10000.0) ** (np.arange(0, dim, 2, dtype=np.float32) / dim))).astype(np.float32)
        ang = np.arange(SEQ, dtype=np.float32)[:, None] * inv[None, :]
        c["cos_" + name], c["sin_" + name] = rope(np.cos(ang), np.sin(ang))
    q = np.arange(SEQ).reshape(2, P)
    k = np.arange(SEQ)
    c["window"] = np.concatenate([np.where(np.abs(k[None] - q[t][:, None]) <= 128, 0.0, NEG) for t in range(2)], 1)
    c["causal"] = np.where(part[None] <= part[:, None], 0.0, NEG)
    end = np.where(np.arange(16) < 15, np.arange(16) * 16 + 31, 1 << 20)
    keep = np.concatenate([(end[None] <= q[t][:, None]) for t in range(2)], 1)
    c["cmp_add"], c["cmp_keep"] = np.where(keep, 0.0, NEG), keep * 1.0
    c["before"] = (part[:, None] < part[None]) * 1.0
    c["ones"] = np.ones((P, P))
    c["slot"] = np.broadcast_to(np.arange(P), (P, P))
    c["rank_e"] = np.broadcast_to(EXPERTS - np.arange(EXPERTS), (P, EXPERTS))
    c["rank_g"] = np.broadcast_to(GROUPS - np.arange(GROUPS), (P, GROUPS))
    c["fold"] = np.stack([part % 32 == r for r in range(2)], 1) * 1.0
    c["spread"] = np.concatenate([np.broadcast_to((part % 32 == r)[:, None], (P, P)) for r in range(2)], 1) * 1.0
    c["block_diag"] = (part[:, None] // 16 == np.arange(8)[None]) * 1.0
    return np.concatenate([c[n].astype(np.float32).reshape(P, w) for n, w in CONSTS], 1)


class Tally:

    def __init__(self, sem, unit=1):
        self.sem, self.unit, self.n, self.laps = sem, unit, 0, []

    def value(self, back=0):
        value = (self.n - back) * self.unit
        if not self.laps:
            return max(value, 0)
        for i, per in self.laps:
            if per:
                value = value + i * (per * self.unit)
        return value

    def next(self, more=1):
        self.n += more
        return self.value()


@contextmanager
def laps(eng, trips, per):
    with eng.Fori(0, trips) as i:
        start = {t: t.n for t in per}
        for t, m in per.items():
            t.laps.append((i, m))
        yield i
        for t, m in per.items():
            assert t.n - start[t] == m, (t.sem, t.n - start[t], m)
            t.laps.pop()
    for t, m in per.items():
        t.n = start[t] + m * trips


def build(nc, t):
    f32, i32 = mybir.dt.float32, mybir.dt.int32
    ALU, ACT, AX = mybir.AluOpType, mybir.ActivationFunctionType, mybir.AxisListType.X
    par_at, par_w = offsets(PARAMS)
    con_at, con_w = offsets(CONSTS)

    ctx = ExitStack()
    with ctx:
        def sb(name, shape, dt=f32):
            return ctx.enter_context(nc.sbuf_tensor(name, shape, dt))

        def sem(name):
            return ctx.enter_context(nc.semaphore(name))

        par, con = sb("par", [P, par_w]), sb("con", [P, con_w])
        ring = sb("ring", [P, RING, CHUNK])
        X = sb("X", [P, 4, D])
        hT = sb("hT", [P, KB, TOK])
        gate = sb("gate", [P, 2, 2, D])
        rows = sb("rows", [P, 4, D])
        arena = sb("arena", [P, 18432])
        psum = ctx.enter_context(nc.psum_tensor("psum", [P, 8, 512], f32))

        def pa(name, at=0, width=None):
            o, w = par_at[name]
            return par[:, o + at:o + at + (width or w - at)]

        def co(name, at=0, width=None):
            o, w = con_at[name]
            return con[:, o + at:o + at + (width or w - at)]

        ident = co("ident")
        cpad = sb("cpad", [P, KB, 32])
        modT = sb("modT", [P, 48, 2])
        scale1 = sb("scale1", [P, 2, KB, 2])
        gain = sb("gain", [P, 2, KB, 2])
        gain8 = sb("gain8", [P, 6, HD])
        nsink = sb("nsink", [P, 8])
        lam = sb("lam", [P, 8])
        sub8 = sb("sub8", [P, P])
        sumsq = sb("sumsq", [P, 8, 8])
        rstd = sb("rstd", [P, 8, 8])
        mhalf = sb("mhalf", [P, 8])
        nbias, psums, esink, rden, mx = (sb(n, [P, 4, 8]) for n in ("nbias", "psums", "esink", "rden", "mx"))

        brow = arena[:, 8192:9216].rearrange("p (b n) -> p b n", b=2)
        mrow = arena[:, 9216:10240].rearrange("p (b n) -> p b n", b=2)
        qT = arena[:, 0:4096].rearrange("p (h n) -> p h n", h=8)
        kP = arena[:, 4096:8192].rearrange("p (g s n) -> p g s n", g=4, s=2)
        vA = arena[:, 8192:9216].rearrange("p (t n) -> p t n", t=4)
        probs = arena[:, 12288:14336].rearrange("p (b n) -> p b n", b=2)
        probsT = arena[:, 14336:16384].rearrange("p (b n) -> p b n", b=2)
        oA = rows
        qP = arena[:, 0:4096].rearrange("p (h s n) -> p h s n", h=8, s=2)
        kT = arena[:, 4096:8192].rearrange("p (h n) -> p h n", h=8)
        vC = arena[:, 8192:12288].rearrange("p (t n) -> p t n", t=4)
        R = [rows[:, 0, 0:512], rows[:, 0, 512:1024]]
        SQ, TX, TA, TB = rows[:, 1, 0:512], rows[:, 1, 512:1024], rows[:, 2, 0:512], rows[:, 2, 512:1024]
        KDUP = [rows[:, 3, 0:256], rows[:, 3, 256:512]]
        TMP = rows[:, 3, 512:1024]
        hrow = arena[:, 0:4096].rearrange("p (t n) -> p t n", t=4)
        facc = arena[:, 4096:8192].rearrange("p (t n) -> p t n", t=4)
        xgT = arena[:, 8192:10240].rearrange("p (b k n) -> p b k n", b=2, k=KB)
        pick = arena[:, 10240:11264].rearrange("p (b t n) -> p b t n", b=2, t=4)
        share = arena[:, 11264:12288].rearrange("p (b t n) -> p b t n", b=2, t=4)
        shareT = arena[:, 12288:12800].rearrange("p (t n) -> p t n", t=4)
        siluG, act_ = arena[:, 12800:13312], arena[:, 13312:13824]
        actT = arena[:, 13824:14336].rearrange("p (f n) -> p f n", f=4)
        ySlot = arena[:, 14336:15360]
        route = arena[:, 15360:18432].rearrange("p (a t e) -> p a t e", a=16, t=4)
        mark = sb("mark", [P, 2])
        late_rounds = sb("late_rounds", [1, 1], i32)
        PR = arena[:, 0:2 * IN2].rearrange("p (t n) -> p t n", t=2)
        qT2 = arena[:, 3584:4608].rearrange("p (h n) -> p h n", h=4)
        kSW = arena[:, 4608:6656].rearrange("p (w g s n) -> p w g s n", w=2, g=2, s=2)
        kvT2 = arena[:, 6656:7168].rearrange("p (b n) -> p b n", b=4)
        XB = arena[:, 7168:8128].rearrange("p (w c g i) -> p w c g i", w=2, c=16, g=2)
        hid = arena[:, 8192:8704].rearrange("p (w n) -> p w n", w=2)
        hidT = arena[:, 8704:8832].rearrange("p (b n) -> p b n", b=4)
        vBD = arena[:, 9152:9664].rearrange("p (h n) -> p h n", h=8)
        cqT = arena[:, 9664:10432].rearrange("p (b n) -> p b n", b=3)
        KD = [arena[:, 10496 + 768 * m:11264 + 768 * m].rearrange("p (b s n) -> p b s n", b=6, s=2) for m in range(2)]
        KWD = [arena[:, 12032 + 256 * m:12288 + 256 * m].rearrange("p (b s n) -> p b s n", b=2, s=2) for m in range(2)]
        CQ = [arena[:, 12544 + 384 * m:12928 + 384 * m] for m in range(2)]
        qM = arena[:, 16384:18432].rearrange("p (h n) -> p h n", h=8)
        spare = gate[:, :, :, :].rearrange("p a b n -> p (a b n)")
        kM = spare[:, 0:2048].rearrange("p (h n) -> p h n", h=8)
        VM = spare[:, 2048:3072].rearrange("p (t n) -> p t n", t=2)
        kC = spare[:, 3072:3136].rearrange("p (g s n) -> p g s n", g=2, s=2)
        hv = spare[:, 3136:3392].rearrange("p (j h n) -> p j h n", j=2, h=8)
        gs = spare[:, 3392:3440].rearrange("p (t n) -> p t n", t=2)
        kpe = spare[:, 3440:3504].rearrange("p (t n) -> p t n", t=2)
        aT = arena[:, 8192:16384].rearrange("p (f n) -> p f n", f=32)
        g2 = sb("g2", [P, 56])
        G_ATTN, G_Q, G_KV, G_MIX, G_MLP = 0, 16, 20, 22, 38

        params_in, consts_in, x_in, out_done = (sem(n) for n in ("params_in", "consts_in", "x_in", "out_done"))
        bias_in = [sem(f"bias_in{i}") for i in range(2)]
        zeroed = sem("zeroed")
        loaded = [sem(f"loaded{i}") for i in range(RING)]
        used = sem("used")
        mm_v, v_free = sem("mm_v"), sem("v_free")
        mm_a, a_free = sem("mm_a"), sem("a_free")
        v_step, a_step, p_step = sem("v_step"), sem("a_step"), sem("p_step")
        c_ready, mod_row, mod_ready, mod_sc = (sem(n) for n in ("c_ready", "mod_row", "mod_ready", "mod_sc"))
        x_ready, ss_ready, rs_done, xn_ready, gain_ready = (sem(n) for n in ("x_ready", "ss_ready", "rs_done", "xn_ready", "gain_ready"))
        hs_ready, hs_done, rows_ready = sem("hs_ready"), sem("hs_done"), sem("rows_ready")
        att_s, att_m, att_e, att_t, att_tv, att_ta, att_pv, att_o = (
            sem(n) for n in ("att_s", "att_m", "att_e", "att_t", "att_tv", "att_ta", "att_pv", "att_o"))
        routed, exp_ready, chosen, pick_ready, sil_ready = (
            sem(n) for n in ("routed", "exp_ready", "chosen", "pick_ready", "sil_ready"))
        final_in = sem("final_in")
        rounds_ready = sem("rounds_ready")
        late = [{n: sem(f"late_{n}{l}") for n in ("loaded", "free", "product", "v", "a", "step", "round", "added")} for l in range(2)]

        def row(src, off, n):
            return src[off:off + n]

        def cols512(w, c):
            return [w[512 * h:512 * h + 512, 512 * c:512 * c + 512].rearrange("(k p) n -> p k n", p=P) for h in range(2)]

        def rows256(w, c):
            return w[256 * c:256 * c + 256, :].rearrange("(k p) n -> p k n", p=P)

        def groups_ab():
            out = []
            for tile in (2, 3):
                for p in range(8):
                    out.append(dict(tile=tile, nk=512, heads=[2 * p, 2 * p + 1]))
            for tile in (0, 1):
                for p in range(4):
                    out.append(dict(tile=tile, nk=256, heads=list(range(4 * p, 4 * p + 4))))
            for g in out:
                tile, nk = g["tile"], g["nk"]
                g["scores"] = [(qT[:, h // 2, P * tile:P * tile + P], kP[:, h // 4, h % 2, 0:nk]) for h in g["heads"]]
                local = tile >= 2 and g["heads"][0] < 8
                g["mask"] = (256, co("window", 256 * (tile - 2), 256)) if local else None
                g["sink"] = g["heads"][0] if g["heads"][0] < 8 else None
                g["pv"] = [[vA[:, b, HD * (h // 4):HD * (h // 4) + HD] for b in range(nk // P)] for h in g["heads"]]
                g["dv"], g["out"] = HD, oA[:, tile, HD * g["heads"][0]:HD * (g["heads"][-1] + 1)]
                g["scale"] = SCALE
            return out

        def groups_c():
            out = []
            for tile in (0, 1):
                for h in range(8):
                    out.append(dict(
                        nk=512, heads=[h, h], mask=None, sink=None, dv=P, scale=SCALE, diff=True,
                        scores=[(qP[:, h, s, P * tile:P * tile + P], kT[:, h, :]) for s in range(2)],
                        pv=[[vC[:, b, P * h:P * h + P] for b in range(4)]] * 2,
                        out=oA[:, tile, P * h:P * h + P]))
            return out

        def groups_2():
            out = []
            for m in (0, 1):
                nk = P * (m + 1)
                q = [qT2[:, h // 2, P * m:P * m + P] for h in range(8)]
                out.append(dict(nk=16, heads=list(range(8)), mask=(0, co("cmp_add", at=16 * m, width=16)), sink=None, dv=HD, scale=SCALE,
                                scores=[(q[h], kC[:, h // 4, h % 2, :]) for h in range(8)], pv_all=vBD,
                                gate=(m, 0), keep=co("cmp_keep", at=16 * m, width=1), out=oA[:, m, 0:512], first=True))
                for kind in ("sel", "win", "mla"):
                    w = 0 if kind == "sel" else 1
                    for h0 in range(0, 8, 1024 // nk):
                        hs = list(range(h0, h0 + 1024 // nk))[:8]
                        g = dict(nk=nk, heads=hs, mask=(P * m, co("causal")), sink=None, dv=HD)
                        if kind == "mla":
                            g.update(scale=MLA_SCALE, out=oA[:, m, 512 + HD * h0:512 + HD * (hs[-1] + 1)],
                                     scores=[(qM[0:MLA_D, h, P * m:P * m + P], kM[0:MLA_D, h, 0:nk]) for h in hs],
                                     pv=[[VM[:, b, HD * h:HD * h + HD] for b in range(m + 1)] for h in hs])
                        else:
                            v0 = VW2 if w else VS2
                            g.update(scale=SCALE, out=oA[:, m, HD * h0:HD * (hs[-1] + 1)], gate=(m, 1 + w), first=False,
                                     scores=[(q[h], kSW[:, w, h // 4, h % 2, 0:nk]) for h in hs],
                                     pv=[[PR[:, b, v0 + HD * (h // 4):v0 + HD * (h // 4) + HD] for b in range(m + 1)] for h in hs])
                        out.append(g)
            return out

        AB = [dict(norm=[(0, 8, 0)], v=None, q=(0, 4, 0), k=None),
              dict(norm=[(0, 2, 1), (4, 4, 2)], v=(128, 128, 0), q=(256, 2, 4), k=(0, 0)),
              dict(norm=[(0, 4, 2), (4, 2, 3)], v=(384, 128, 128), q=(0, 2, 6), k=(256, 2))]

        def width(g):
            return g["nk"] * len(g["heads"])

        def flat(bank):
            return psum[:, bank:bank + 2, :].rearrange("p a n -> p (a n)")

        block = ctx.enter_context(nc.Block())

        @block.gpsimd
        def _(pool):
            pool.dma_start(con[:, :], t["consts"]).then_inc(consts_in, 16)
            pool.memset(cpad[:, :, :], 0.0)
            pool.memset(brow, 0.0).then_inc(zeroed, 1)
            pool.memset(kP, 0.0).then_inc(zeroed, 1)
            pool.memset(mhalf[:, :], -0.5).then_inc(p_step, 1)
            ss, hs, step = Tally(ss_ready), Tally(hs_ready), Tally(p_step)
            step.n = 1

            def rsqrt(out, total, n):
                pool.tensor_scalar(out, total, EPS * n, None, ALU.add).then_inc(p_step, 1)
                pool.wait_ge(p_step, step.next())
                return pool.tensor_tensor(out, out, mhalf[:, 0:out.shape[-1]], ALU.pow)

            def rsqrt_rows(nt):
                pool.wait_ge(ss_ready, ss.next())
                rsqrt(rstd[:, 0, 0:nt], sumsq[:, 0, 0:nt], D).then_inc(rs_done, 1)

            def rsqrt_heads(jobs, n, width=8):
                for j in range(jobs):
                    pool.wait_ge(hs_ready, hs.next())
                    b = 1 + (hs.n - 1) % 2
                    rsqrt(rstd[:, b, 0:width], sumsq[:, b, 0:width], n).then_inc(hs_done, 1)

            def pads2():
                pool.wait_ge(x_ready, 4)
                pool.memset(kSW, 0.0)
                pool.memset(kC, 0.0)
                pool.memset(hv, 0.0).then_inc(zeroed, 1)

            def latents():
                for m in range(2):
                    rsqrt_heads(1, 256, 1)
                    rsqrt_heads(1, P, 1)

            def pads():
                pool.wait_ge(x_ready, 2)
                pool.memset(brow, 0.0).then_inc(zeroed, 1)
                pool.memset(qP, 0.0).then_inc(zeroed, 1)

            rsqrt_rows(4)
            rsqrt_heads(12, HD)
            rsqrt_rows(4)
            pads()
            rsqrt_rows(4)
            rsqrt_heads(2 * 2 + 2 * 4, HD)
            rsqrt_heads(2, P)
            rsqrt_rows(2)
            for l in range(DEPTH):
                if not l:
                    pads2()
                rsqrt_rows(2)
                latents()
                rsqrt_heads(2, 512, 2)
                rsqrt_rows(2)
            rsqrt_rows(2)

        @block.scalar
        def _(act):
            act.dma_start(par[:, :], t["params"]).then_inc(params_in, 16)
            jobs, chunks = Tally(mm_a), Tally(used)
            exps_in, routing = Tally(att_m), Tally(routed)
            turned = Tally(att_t)
            job = [0]
            own = {}

            def so_far(sem):
                return own.setdefault(sem.name, Tally(sem)).next()

            def next_bank():
                job[0] += 1
                return psum[:, 4 + (job[0] - 1) % 4, :]

            def bias_row(l, c):
                n = 12 * l + c
                if c >= 2:
                    act.wait_ge(mod_row, n - 1)
                else:
                    act.wait_ge(zeroed, 1 + 2 * l)
                for r in range(2):
                    act.dma_start(brow[r:r + 1, c % 2, :], t["b_mod"][l:l + 1, 512 * c:512 * c + 512]).then_inc(bias_in[c % 2], 16)

            def mod(l):
                if l:
                    act.wait_ge(x_ready, 2)
                bias_row(l, 0)
                bias_row(l, 1)
                if not l:
                    act.wait_ge(params_in, 16)
                    act.activation(cpad[:, :, 0:2], pa("c").rearrange("p (k r) -> p k r", r=2), ACT.Silu).then_inc(c_ready, 1)
                    act.wait_ge(c_ready, so_far(c_ready))
                for c in range(12):
                    act.wait_ge(mm_a, jobs.next())
                    bank = next_bank()
                    act.activation(modT[:, 4 * c:4 * c + 4, :], bank[:, 0:8].rearrange("p (k r) -> p k r", r=2), ACT.Copy).then_inc(a_free, 1)
                    act.wait_ge(a_free, so_far(a_free))
                    if c in (4, 5, 10, 11):
                        for r in range(2):
                            act.wait_ge(mm_a, jobs.next())
                            bank = next_bank()
                            act.activation(gate[:, c // 6, r, 512 * (c % 2):512 * (c % 2) + 512], bank, ACT.Copy).then_inc(a_free, 1)
                            act.wait_ge(a_free, so_far(a_free))
                    if c + 2 < 12:
                        bias_row(l, c + 2)
                for w in range(2):
                    inst = act.activation(scale1[:, w, :, :], modT[:, 8 + 24 * w:16 + 24 * w, :], ACT.Copy, bias=1.0)
                inst.then_inc(mod_ready, 1)
                act.wait_ge(mod_ready, so_far(mod_ready))

            def norm(n, which, tiles):
                if n:
                    act.wait_ge(x_ready, n)
                else:
                    act.wait_ge(x_in, 32)
                for m, tile in enumerate(tiles):
                    inst = act.activation(rows[:, m, :], X[:, tile, :], ACT.Square, accum_out=sumsq[:, 0, m:m + 1])
                inst.then_inc(ss_ready, 1)
                act.wait_ge(ss_ready, so_far(ss_ready))
                act.wait_ge(gain_ready, n // 2 + 1)
                for k in range(1, KB, 2):
                    act.wait_ge(mm_a, jobs.next())
                    bank = next_bank()
                    for a, b, r in [(0, 256, 1), (256, 512, 0)] if len(tiles) == 4 else [(0, 256, 0)]:
                        inst = act.activation(hT[:, k, a:b], bank[:, a:b], ACT.Identity,
                                              bias=modT[:, 24 * which + k, r:r + 1], scale=gain[:, which, k, r:r + 1])
                    inst.then_inc(a_free, 1)
                    act.wait_ge(a_free, so_far(a_free))

            def squares(n, tiles):
                act.wait_ge(x_ready, n)
                for m, tile in enumerate(tiles):
                    inst = act.activation(rows[:, m, :], X[:, tile, :], ACT.Square, accum_out=sumsq[:, 0, m:m + 1])
                inst.then_inc(ss_ready, 1)
                act.wait_ge(ss_ready, so_far(ss_ready))

            def turned2(g):
                for k in range(1, KB, 2):
                    act.wait_ge(mm_a, jobs.next())
                    bank = next_bank()
                    act.activation(hT[:, k, 0:SEQ], bank[:, 0:SEQ], ACT.Copy, scale=g2[:, g + k:g + k + 1]).then_inc(a_free, 1)
                    act.wait_ge(a_free, so_far(a_free))

            def norm2(n, g):
                squares(n, [2, 3])
                if n == 4:
                    act.wait_ge(gain_ready, 3)
                turned2(g)

            def project2(l):
                act.wait_ge(zeroed, 5)

                def halves(bank, which, cols):
                    k = bank[:, 0:256].rearrange("p (g n) -> p g n", g=2)
                    act.activation(kSW[0:64, which, :, 0, cols], k[0:64], ACT.Copy)
                    act.activation(kSW[64:128, which, :, 1, cols], k[64:128], ACT.Copy).then_inc(a_free, 1)
                    act.wait_ge(a_free, so_far(a_free))

                for c in range(4):
                    for m in range(2):
                        cols = slice(P * m, P * m + P)
                        act.wait_ge(mm_a, jobs.next())
                        bank = next_bank()
                        if c == 0:
                            act.activation(qT2[:, :, cols], bank.rearrange("p (h n) -> p h n", h=4), ACT.Copy).then_inc(a_free, 1)
                            act.wait_ge(a_free, so_far(a_free))
                        elif c == 1:
                            src = bank.rearrange("p (b n o) -> p b n o", b=4, o=2)
                            dst = kvT2[:, :, 64 * m:64 * m + 64]
                            act.activation(dst[0:64], src[0:64, :, :, 0], ACT.Copy)
                            act.activation(dst[64:128], src[64:128, :, :, 1], ACT.Copy).then_inc(a_free, 1)
                            act.wait_ge(a_free, so_far(a_free))
                            act.wait_ge(mm_a, jobs.next())
                            bank = next_bank()
                            halves(bank, 0, cols)
                        elif c == 2:
                            halves(bank, 1, cols)
                        else:
                            for b in range(3):
                                g = G_Q + 2 * l + b if b < 2 else G_KV + l
                                inst = act.activation(cqT[:, b, cols], bank[:, P * b:P * b + P], ACT.Copy, scale=g2[:, g:g + 1])
                            inst.then_inc(a_free, 1)
                            act.wait_ge(a_free, so_far(a_free))
                act.wait_ge(routed, routing.next())
                act.activation(gs, PR[:, :, GA2:GA2 + 24], ACT.Exp, scale=-1.0).then_inc(exp_ready, 1)
                act.wait_ge(exp_ready, so_far(exp_ready))
                for dst in (qM, kM):
                    for m in range(2):
                        for j in range(2):
                            act.wait_ge(mm_a, jobs.next())
                            bank = next_bank()
                            act.activation(dst[0:MLA_D, 4 * j:4 * j + 4, P * m:P * m + P],
                                           bank[0:MLA_D, :].rearrange("p (h n) -> p h n", h=4), ACT.Copy).then_inc(a_free, 1)
                            act.wait_ge(a_free, so_far(a_free))

            def compress():
                for w in range(2):
                    act.wait_ge(used, chunks.next(2))
                    bank = next_bank()
                    act.activation(hid[0:30, w, :], bank[0:30, 0:256], ACT.Silu).then_inc(a_free, 1)
                    act.wait_ge(a_free, so_far(a_free))

            def mlp():
                for c in range(8):
                    act.wait_ge(mm_a, jobs.next())
                    bank = next_bank()
                    f = aT[:, 4 * c:4 * c + 2, :]
                    act.activation(f, bank.rearrange("p (f n) -> p f n", f=2), ACT.Relu).then_inc(a_step, 1)
                    act.wait_ge(a_step, so_far(a_step))
                    act.activation(f, f, ACT.Square).then_inc(a_free, 1)
                    act.wait_ge(a_free, so_far(a_free))

            def heads_ab():
                for j in range(12):
                    cols = slice(P * (j % 4), P * (j % 4) + P)
                    b = AB[j // 4]
                    act.wait_ge(mm_a, jobs.next())
                    bank = next_bank()
                    _, nq, q0 = b["q"]
                    inst = act.activation(qT[:, q0:q0 + nq, cols], bank[:, 0:P * nq].rearrange("p (h n) -> p h n", h=nq), ACT.Copy)
                    if b["k"]:
                        g0 = b["k"][1]
                        ks = bank[:, 256:512].rearrange("p (g n) -> p g n", g=2)
                        act.wait_ge(zeroed, 2)
                        act.activation(kP[0:64, g0:g0 + 2, 0, cols], ks[0:64], ACT.Copy)
                        inst = act.activation(kP[64:128, g0:g0 + 2, 1, cols], ks[64:128], ACT.Copy)
                    inst.then_inc(a_free, 1)
                    act.wait_ge(a_free, so_far(a_free))

            def heads_c():
                for c in range(4):
                    for tile in range(4) if c >= 2 else (2, 3):
                        act.wait_ge(mm_a, jobs.next())
                        bank = next_bank().rearrange("p (h n) -> p h n", h=4)
                        if c < 2:
                            cols = slice(P * (tile - 2), P * (tile - 2) + P)
                            act.wait_ge(zeroed, 4)
                            act.activation(qP[0:64, 4 * c:4 * c + 4, 0, cols], bank[0:64], ACT.Copy)
                            act.activation(qP[64:128, 4 * c:4 * c + 4, 1, cols], bank[64:128], ACT.Copy).then_inc(a_free, 1)
                            act.wait_ge(a_free, so_far(a_free))
                        else:
                            act.activation(kT[:, 4 * c - 8:4 * c - 4, P * tile:P * tile + P], bank, ACT.Copy).then_inc(a_free, 1)
                            act.wait_ge(a_free, so_far(a_free))

            def attention(groups):
                def exps(g):
                    act.wait_ge(att_m, exps_in.next())
                    b, nk, heads = (exps_in.n - 1) % 4, g["nk"], len(g["heads"])
                    s = psum[:, 2 * (b % 2):2 * (b % 2) + 2, :].rearrange("p a n -> p (a n)")
                    if g["sink"] is not None:
                        act.activation(esink[:, b, 0:heads], mx[:, b, 0:heads], ACT.Exp)
                    for u in range(heads):
                        inst = act.activation(probs[:, b % 2, nk * u:nk * u + nk], s[:, nk * u:nk * u + nk], ACT.Exp,
                                              bias=nbias[:, b, u:u + 1], scale=g["scale"], accum_out=psums[:, b, u:u + 1])
                    inst.then_inc(att_e, 1)
                    act.wait_ge(att_e, so_far(att_e))

                exps(groups[0])
                for n in range(len(groups)):
                    act.wait_ge(att_t, turned.next())
                    if width(groups[n]) == 1024:
                        act.activation(probsT[:, (turned.n - 1) % 2, 512:1024], psum[:, 5, :], ACT.Copy).then_inc(att_ta, 1)
                        act.wait_ge(att_ta, so_far(att_ta))
                    else:
                        act.activation(mark[:, 1:2], par[:, 0:1], ACT.Copy).then_inc(att_ta, 1)
                        act.wait_ge(att_ta, so_far(att_ta))
                    if n + 1 < len(groups):
                        exps(groups[n + 1])

            def lam_exp():
                act.wait_ge(routed, routing.next())
                act.activation(lam[:, 2:4], lam[:, 0:2], ACT.Exp).then_inc(exp_ready, 1)
                act.wait_ge(exp_ready, so_far(exp_ready))

            def outputs_T(nt):
                for k in range(1, KB, 2):
                    act.wait_ge(mm_a, jobs.next())
                    bank = next_bank()
                    act.activation(hT[:, k, 0:P * nt], bank[:, 0:P * nt], ACT.Copy).then_inc(a_free, 1)
                    act.wait_ge(a_free, so_far(a_free))

            def moe(l):
                nt = 4 - 2 * l
                norm(2 * l + 1, 1, [0, 1, 2, 3][2 * l:])
                for tile in range(nt):
                    act.wait_ge(mm_a, jobs.next())
                    bank = next_bank()
                    act.activation(hrow[:, tile, 512:1024], bank, ACT.Copy).then_inc(a_free, 1)
                    act.wait_ge(a_free, so_far(a_free))
                act.wait_ge(routed, routing.next())
                for tile in range(nt):
                    inst = act.activation(route[:, 1, tile, 0:4], route[:, 0, tile, 0:4], ACT.Exp,
                                          bias=route[:, 2, tile, 0:1], accum_out=route[:, 2, tile, 1:2])
                inst.then_inc(exp_ready, 1)
                act.wait_ge(exp_ready, so_far(exp_ready))
                act.wait_ge(routed, routing.next())
                act.activation(route[:, 2, 0:nt, 4:5], route[:, 2, 0:nt, 3:4], ACT.Exp).then_inc(exp_ready, 1)
                act.wait_ge(exp_ready, so_far(exp_ready))

                def gathered(b):
                    for h in range(2):
                        act.wait_ge(mm_a, jobs.next())
                        act.activation(xgT[:, b, 4 * h:4 * h + 4, :], psum[:, 5 + h, :].rearrange("p (k n) -> p k n", k=4),
                                  ACT.Copy).then_inc(a_free, 1)
                        act.wait_ge(a_free, so_far(a_free))

                gathered(0)
                own.setdefault(sil_ready.name, Tally(sil_ready))
                with laps(act, PAIRS // 2, {jobs: 6, chunks: 24, own[sil_ready.name]: 2, own[a_free.name]: 6}):
                    for b in range(2):
                        act.wait_ge(used, chunks.next(4))
                        act.activation(siluG, psum[:, 4, :], ACT.Silu).then_inc(sil_ready, 1)
                        act.wait_ge(sil_ready, so_far(sil_ready))
                        gathered(1 - b)
                        act.wait_ge(mm_a, jobs.next())
                        act.activation(ySlot[:, 0:512], psum[:, 7, :], ACT.Copy).then_inc(a_free, 1)
                        act.wait_ge(a_free, so_far(a_free))
                        chunks.n += 8

                s = late[l]
                product, mine = Tally(s["product"]), Tally(s["a"])
                own[s["a"].name] = mine
                act.wait_ge(rounds_ready, l + 1)
                count = act.value_load(late_rounds[0:1, 0:1], min_val=0, max_val=nt)
                with laps(act, nt, {product: 5 * EXPERTS, mine: 3 * EXPERTS}) as r:
                    with act.If(count > r):
                        with laps(act, EXPERTS, {product: 5, mine: 3}):
                            act.wait_ge(s["product"], product.next())
                            act.activation(xgT[:, 0], psum[:, 5:7, :].rearrange("p a (k n) -> p (a k) n", k=4), ACT.Copy).then_inc(s["a"], 1)
                            act.wait_ge(s["a"], so_far(s["a"]))
                            act.wait_ge(s["product"], product.next())
                            act.activation(siluG, psum[:, 4, :], ACT.Silu).then_inc(s["a"], 1)
                            act.wait_ge(s["a"], so_far(s["a"]))
                            act.wait_ge(s["product"], product.next(2))
                            act.activation(ySlot[:, 0:512], psum[:, 7, :], ACT.Copy).then_inc(s["a"], 1)
                            act.wait_ge(s["a"], so_far(s["a"]))
                            product.n += 1
                    act.end_ifs()

            mod(0)
            chunks.n += 24
            norm(0, 0, [0, 1, 2, 3])
            heads_ab()
            chunks.n += 6
            attention(groups_ab())
            outputs_T(4)
            chunks.n += 4
            moe(0)
            mod(1)
            chunks.n += 24
            norm(2, 0, [0, 1, 2, 3])
            heads_c()
            chunks.n += 12
            lam_exp()
            attention(groups_c())
            outputs_T(2)
            chunks.n += 4
            moe(1)
            for l in range(DEPTH):
                norm2(4 + 2 * l, G_ATTN + KB * l)
                project2(l)
                chunks.n += 10
                compress()
                attention(groups_2())
                turned2(G_MIX + KB * l)
                chunks.n += 4
                norm2(5 + 2 * l, G_MLP + KB * l)
                mlp()
                chunks.n += 32
            squares(8, [2, 3])

        @block.vector
        def _(dve):
            jobs, chunks = Tally(mm_v), Tally(used)
            heads_done, norms_done = Tally(hs_done), Tally(rs_done)
            scored, expd, turned, valued = Tally(att_s), Tally(att_e), Tally(att_t), Tally(att_pv)
            exp_in, silus = Tally(exp_ready), Tally(sil_ready)
            job = [0]
            own = {}

            def so_far(sem):
                return own.setdefault(sem.name, Tally(sem)).next()

            def next_bank():
                job[0] += 1
                return psum[:, (job[0] - 1) % 4, :]

            def init():
                dve.wait_ge(params_in, 16)
                dve.wait_ge(consts_in, 16)
                dve.tensor_scalar(gain8[:, :, :], pa("head_gain").rearrange("p (a n) -> p a n", a=6), HD ** 0.5, None, ALU.mult)
                dve.tensor_scalar(nsink[:, :], pa("sink"), -1.0, None, ALU.mult)
                dve.tensor_scalar(sub8[:, :], pa("subln"), (1 - LAM_INIT) * 128 ** 0.5, None, ALU.mult).then_inc(v_step, 1)
                dve.wait_ge(v_step, so_far(v_step))

            def mod(l):
                for c in range(12):
                    dve.wait_ge(used, chunks.next(2))
                    dve.wait_ge(bias_in[c % 2], 32 * (6 * l + c // 2 + 1))
                    dve.tensor_tensor(mrow[:, c % 2, :], psum[:, c % 4, :], brow[:, c % 2, :], ALU.add).then_inc(mod_row, 1)
                    dve.wait_ge(mod_row, so_far(mod_row))
                dve.wait_ge(mod_ready, l + 1)
                for w, name in enumerate(("norm_mix", "norm_ffn")):
                    g = pa(name, at=KB * l, width=KB)[:, :, None].to_broadcast([P, KB, 2])
                    dve.tensor_tensor(gain[:, w, :, :], scale1[:, w, :, :], g, ALU.mult).then_inc(v_step, 1)
                    dve.wait_ge(v_step, so_far(v_step))
                dve.tensor_scalar(gain[:, :, :, :], gain[:, :, :, :], D ** 0.5, None, ALU.mult).then_inc(gain_ready, 1)
                dve.wait_ge(gain_ready, so_far(gain_ready))

            def scaled_rows(tiles, back=True):
                dve.wait_ge(rs_done, norms_done.next())
                for m, tile in enumerate(tiles):
                    dve.tensor_scalar(rows[:, m, :], X[:, tile, :], rstd[:, 0, m:m + 1], None, ALU.mult).then_inc(xn_ready, 1)
                    dve.wait_ge(xn_ready, so_far(xn_ready))

            def norm(n, which, tiles):
                scaled_rows(tiles)
                dve.wait_ge(gain_ready, n // 2 + 1)
                for k in range(0, KB, 2):
                    dve.wait_ge(mm_v, jobs.next())
                    bank = next_bank()
                    for a, b, r in [(0, 256, 1), (256, 512, 0)] if len(tiles) == 4 else [(0, 256, 0)]:
                        inst = dve.tensor_scalar(hT[:, k, a:b], bank[:, a:b], gain[:, which, k, r:r + 1],
                                                 modT[:, 24 * which + k, r:r + 1], ALU.mult, ALU.add)
                    inst.then_inc(v_free, 1)
                    dve.wait_ge(v_free, so_far(v_free))

            def h64(ap, n=HD):
                return ap.rearrange("p (h n) -> p h n", n=n)

            def rope(dst, src, heads, n, cos, sin):
                m = n // 2
                s, a, b = h64(src, n), h64(TA[:, 0:heads * n], n), h64(TB[:, 0:heads * n], n)
                dve.tensor_tensor(a, s, cos[:, None, :].to_broadcast([P, heads, n]), ALU.mult)
                dve.tensor_tensor(b[:, :, 0:m], s[:, :, m:n], sin[:, None, 0:m].to_broadcast([P, heads, m]), ALU.mult)
                dve.tensor_tensor(b[:, :, m:n], s[:, :, 0:m], sin[:, None, m:n].to_broadcast([P, heads, m]), ALU.mult).then_inc(v_step, 1)
                dve.wait_ge(v_step, so_far(v_step))
                return dve.tensor_tensor(h64(dst, n), a, b, ALU.add)

            def head_norm(bank, gains, keep=None, n=HD):
                heads = 512 // n
                dve.tensor_copy(TX, bank).then_inc(v_free, 1)
                dve.wait_ge(v_free, so_far(v_free))
                dve.tensor_tensor(SQ, TX, TX, ALU.mult).then_inc(v_step, 1)
                dve.wait_ge(v_step, so_far(v_step))
                b = 1 + heads_done.n % 2
                dve.tensor_reduce(sumsq[:, b, 0:heads], h64(SQ, n), AX, ALU.add).then_inc(hs_ready, 1)
                dve.wait_ge(hs_ready, so_far(hs_ready))
                heads_done.n += 1
                if keep:
                    dve.tensor_copy(keep[0], TX[:, keep[1]:keep[1] + keep[0].shape[-1]]).then_inc(v_step, 1)
                    dve.wait_ge(v_step, so_far(v_step))
                dve.wait_ge(hs_done, heads_done.value())
                dve.tensor_tensor(h64(TX, n), h64(TX, n), rstd[:, b, 0:heads, None].to_broadcast([P, heads, n]), ALU.mult).then_inc(v_step, 1)
                dve.wait_ge(v_step, so_far(v_step))
                for h0, nh, g in gains:
                    x = h64(TX)[:, h0:h0 + nh, :]
                    inst = dve.tensor_tensor(x, x, gain8[:, g:g + 1, :].to_broadcast([P, nh, HD]), ALU.mult)
                inst.then_inc(v_step, 1)
                dve.wait_ge(v_step, so_far(v_step))

            def heads_ab():
                for j in range(12):
                    c, tile, b = j // 4, j % 4, AB[j // 4]
                    if tile == 3:
                        dve.wait_ge(used, chunks.next(2))
                    else:
                        dve.wait_ge(mm_v, jobs.next())
                    bank = next_bank()
                    keep = None
                    if b["v"]:
                        s0, w, d0 = b["v"]
                        keep = (vA[:, tile, d0:d0 + w], s0)
                    head_norm(bank, b["norm"], keep)
                    r = R[j % 2]
                    if tile >= 2:
                        tab = slice(HD * (tile - 2), HD * (tile - 2) + HD)
                        inst = rope(r, TX, 8, HD, co("cos_ax")[:, tab], co("sin_ax")[:, tab])
                    else:
                        inst = dve.tensor_copy(r, TX)
                    if b["k"]:
                        inst.then_inc(v_step, 1)
                        dve.wait_ge(v_step, so_far(v_step))
                        k0 = b["k"][0]
                        inst = dve.tensor_copy(KDUP[j % 2].rearrange("p (g s n) -> p g s n", g=2, s=2),
                                               h64(r[:, k0:k0 + P])[:, :, None, :].to_broadcast([P, 2, 2, HD]))
                    inst.then_inc(rows_ready, 1)
                    dve.wait_ge(rows_ready, so_far(rows_ready))

            def heads_c():
                j = 0
                for c in range(6):
                    tiles = (2, 3) if c < 2 else (0, 1, 2, 3)
                    for tile in tiles:
                        if tile == 3:
                            dve.wait_ge(used, chunks.next(2))
                        else:
                            dve.wait_ge(mm_v, jobs.next())
                        bank = next_bank()
                        if c >= 4:
                            dve.tensor_copy(vC[:, tile, 512 * (c - 4):512 * (c - 4) + 512], bank).then_inc(v_free, 1)
                            dve.wait_ge(v_free, so_far(v_free))
                            continue
                        head_norm(bank, [(0, 8, 4 if c < 2 else 5)])
                        if tile >= 2:
                            tab = slice(HD * (tile - 2), HD * (tile - 2) + HD)
                            inst = rope(R[j % 2], TX, 8, HD, co("cos_ax")[:, tab], co("sin_ax")[:, tab])
                        else:
                            inst = dve.tensor_copy(R[j % 2], TX)
                        inst.then_inc(rows_ready, 1)
                        dve.wait_ge(rows_ready, so_far(rows_ready))
                        j += 1

            def attention(groups):
                def maxima(g):
                    dve.wait_ge(att_s, scored.next())
                    b, nk, heads = (scored.n - 1) % 4, g["nk"], len(g["heads"])
                    s = psum[:, 2 * (b % 2):2 * (b % 2) + 2, :].rearrange("p a n -> p (a n)")[:, 0:nk * heads].rearrange("p (u n) -> p u n", u=heads)
                    if g["mask"]:
                        at, m = g["mask"]
                        w = m.shape[-1]
                        part = s[:, :, at:at + w]
                        dve.tensor_tensor(part, part, m[:, None, :].to_broadcast([P, heads, w]), ALU.add).then_inc(v_step, 1)
                        dve.wait_ge(v_step, so_far(v_step))
                    dve.tensor_reduce(mx[:, b, 0:heads], s, AX, ALU.max).then_inc(v_step, 1)
                    dve.wait_ge(v_step, so_far(v_step))
                    if g["sink"] is None:
                        dve.tensor_scalar(nbias[:, b, 0:heads], mx[:, b, 0:heads], -g["scale"], None, ALU.mult).then_inc(att_m, 1)
                        dve.wait_ge(att_m, so_far(att_m))
                    else:
                        h = g["sink"]
                        dve.scalar_tensor_tensor(nbias[:, b, 0:heads], mx[:, b, 0:heads], -g["scale"], nsink[:, h:h + heads], ALU.mult, ALU.min).then_inc(v_step, 1)
                        dve.wait_ge(v_step, so_far(v_step))
                        dve.tensor_tensor(mx[:, b, 0:heads], nbias[:, b, 0:heads], nsink[:, h:h + heads], ALU.subtract).then_inc(att_m, 1)
                        dve.wait_ge(att_m, so_far(att_m))

                def evac(g):
                    dve.wait_ge(att_t, turned.next())
                    w = min(512, width(g))
                    dve.tensor_copy(probsT[:, (turned.n - 1) % 2, 0:w], psum[:, 4, 0:w]).then_inc(att_tv, 1)
                    dve.wait_ge(att_tv, so_far(att_tv))

                def output(g):
                    dve.wait_ge(att_pv, valued.next())
                    dve.wait_ge(att_e, expd.next())
                    b, heads, dv = (valued.n - 1) % 4, len(g["heads"]), g["dv"]
                    den = psums[:, b, 0:heads]
                    if g["sink"] is not None:
                        dve.tensor_tensor(den, den, esink[:, b, 0:heads], ALU.add).then_inc(v_step, 1)
                        dve.wait_ge(v_step, so_far(v_step))
                    dve.reciprocal(rden[:, b, 0:heads], den).then_inc(v_step, 1)
                    dve.wait_ge(v_step, so_far(v_step))
                    o = psum[:, 6 + b % 2, 0:heads * dv].rearrange("p (u n) -> p u n", u=heads)
                    r = rden[:, b, 0:heads]
                    if "keep" in g:
                        dve.tensor_scalar(r, r, g["keep"], None, ALU.mult).then_inc(v_step, 1)
                        dve.wait_ge(v_step, so_far(v_step))
                    if "gate" in g:
                        m, branch = g["gate"]
                        h = g["heads"][0]
                        dve.tensor_tensor(r, r, gs[:, m, 3 * h + branch:3 * (h + heads - 1) + branch + 1:3], ALU.mult).then_inc(v_step, 1)
                        dve.wait_ge(v_step, so_far(v_step))
                    if g.get("diff"):
                        dve.tensor_tensor(rden[:, b, 1:2], rden[:, b, 1:2], lam[:, 6:7], ALU.mult).then_inc(v_step, 1)
                        dve.wait_ge(v_step, so_far(v_step))
                        dve.tensor_scalar(TA2, o[:, 1, :], rden[:, b, 1:2], None, ALU.mult).then_inc(v_step, 1)
                        dve.wait_ge(v_step, so_far(v_step))
                        dve.scalar_tensor_tensor(g["out"], o[:, 0, :], rden[:, b, 0:1], TA2, ALU.mult, ALU.subtract).then_inc(att_o, 1)
                        dve.wait_ge(att_o, so_far(att_o))
                    elif "gate" in g and not g["first"]:
                        part = rows[:, 3, 0:heads * dv].rearrange("p (u n) -> p u n", u=heads)
                        dve.tensor_tensor(part, o, r[:, :, None].to_broadcast([P, heads, dv]), ALU.mult).then_inc(v_step, 1)
                        dve.wait_ge(v_step, so_far(v_step))
                        dve.tensor_tensor(g["out"], g["out"], rows[:, 3, 0:heads * dv], ALU.add).then_inc(att_o, 1)
                        dve.wait_ge(att_o, so_far(att_o))
                    else:
                        dve.tensor_tensor(g["out"].rearrange("p (u n) -> p u n", u=heads), o,
                                     rden[:, b, 0:heads, None].to_broadcast([P, heads, dv]), ALU.mult).then_inc(att_o, 1)
                        dve.wait_ge(att_o, so_far(att_o))

                maxima(groups[0])
                for n in range(len(groups)):
                    if n + 1 < len(groups):
                        maxima(groups[n + 1])
                    evac(groups[n])
                    if n:
                        output(groups[n - 1])
                output(groups[-1])

            TA2 = arena[:, 16384:16512]
            LP = arena[:, 16512:17024]

            def differential():
                lp = pa("lam").rearrange("p (a n) -> p a n", a=4)
                dve.tensor_tensor(LP[:, 0:128].rearrange("p (a n) -> p a n", a=2), lp[:, 0:4:2, :], lp[:, 1:4:2, :], ALU.mult).then_inc(v_step, 1)
                dve.wait_ge(v_step, so_far(v_step))
                dve.tensor_reduce(lam[:, 0:2], LP[:, 0:128].rearrange("p (a n) -> p a n", a=2), AX, ALU.add).then_inc(routed, 1)
                dve.wait_ge(routed, so_far(routed))
                dve.wait_ge(exp_ready, exp_in.next())
                dve.tensor_tensor(lam[:, 4:5], lam[:, 2:3], lam[:, 3:4], ALU.subtract).then_inc(v_step, 1)
                dve.wait_ge(v_step, so_far(v_step))
                dve.tensor_scalar(lam[:, 6:7], lam[:, 4:5], LAM_INIT, None, ALU.add).then_inc(v_step, 1)
                dve.wait_ge(v_step, so_far(v_step))

            def sub_norm():
                for tile in range(2):
                    o = oA[:, tile, :].rearrange("p (h n) -> p h n", h=8)
                    sq = arena[:, 16384:17408]
                    dve.tensor_tensor(sq, oA[:, tile, :], oA[:, tile, :], ALU.mult).then_inc(v_step, 1)
                    dve.wait_ge(v_step, so_far(v_step))
                    b = 1 + heads_done.n % 2
                    dve.tensor_reduce(sumsq[:, b, 0:8], sq.rearrange("p (h n) -> p h n", h=8), AX, ALU.add).then_inc(hs_ready, 1)
                    dve.wait_ge(hs_ready, so_far(hs_ready))
                    dve.wait_ge(hs_done, heads_done.next())
                    dve.tensor_tensor(o, o, rstd[:, b, 0:8, None].to_broadcast([P, 8, P]), ALU.mult).then_inc(v_step, 1)
                    dve.wait_ge(v_step, so_far(v_step))
                    dve.tensor_tensor(o, o, sub8[:, None, :].to_broadcast([P, 8, P]), ALU.mult).then_inc(rows_ready, 1)
                    dve.wait_ge(rows_ready, so_far(rows_ready))

            def outputs_T(nt):
                for k in range(0, KB, 2):
                    dve.wait_ge(mm_v, jobs.next())
                    bank = next_bank()
                    dve.tensor_copy(hT[:, k, 0:P * nt], bank[:, 0:P * nt]).then_inc(v_free, 1)
                    dve.wait_ge(v_free, so_far(v_free))

            def add_output(which, tiles):
                for c in range(2):
                    cols = slice(512 * c, 512 * c + 512)
                    for tile in tiles:
                        if tile == 3:
                            dve.wait_ge(used, chunks.next(2))
                        else:
                            dve.wait_ge(mm_v, jobs.next())
                        bank = next_bank()
                        if which is None:
                            dve.tensor_tensor(X[:, tile, cols], X[:, tile, cols], bank, ALU.add).then_inc(v_free, 1)
                            dve.wait_ge(v_free, so_far(v_free))
                            continue
                        dve.tensor_tensor(TMP, bank, gate[:, which, 1 if tile < 2 else 0, cols], ALU.mult).then_inc(v_free, 1)
                        dve.wait_ge(v_free, so_far(v_free))
                        dve.tensor_tensor(X[:, tile, cols], X[:, tile, cols], TMP, ALU.add).then_inc(v_step, 1)
                        dve.wait_ge(v_step, so_far(v_step))
                dve.memset(mark[:, 0:1], 0.0).then_inc(x_ready, 1)
                dve.wait_ge(x_ready, so_far(x_ready))

            def choose(l, nt):
                def tab(a, w=EXPERTS, at=0):
                    return route[:, a, 0:nt, at:at + w]

                def over(ap, w):
                    return ap.to_broadcast([P, nt, w])

                def one_hot(dst, src, best, rank, w, scratch):
                    dve.tensor_tensor(scratch, src, over(best, w), ALU.is_equal).then_inc(v_step, 1)
                    dve.wait_ge(v_step, so_far(v_step))
                    dve.tensor_tensor(scratch, scratch, rank[:, None, :].to_broadcast([P, nt, w]), ALU.mult).then_inc(v_step, 1)
                    dve.wait_ge(v_step, so_far(v_step))
                    dve.tensor_reduce(tab(2, 1, 8), scratch, AX, ALU.max).then_inc(v_step, 1)
                    dve.wait_ge(v_step, so_far(v_step))
                    dve.tensor_tensor(dst, scratch, over(tab(2, 1, 8), w), ALU.is_equal).then_inc(v_step, 1)
                    dve.wait_ge(v_step, so_far(v_step))

                dve.wait_ge(mm_v, jobs.next())
                bank = next_bank()
                br = pa("b_route", at=ROUTES * l, width=ROUTES)[:, None, :].to_broadcast([P, nt, ROUTES])
                dve.tensor_tensor(tab(0, ROUTES), bank[:, 0:ROUTES * nt].rearrange("p (t e) -> p t e", t=nt), br, ALU.add).then_inc(v_free, 1)
                dve.wait_ge(v_free, so_far(v_free))
                lg, le = tab(0, 4), tab(0, EXPERTS, 4)
                dve.tensor_reduce(tab(2, 1, 5), lg, AX, ALU.max).then_inc(v_step, 1)
                dve.wait_ge(v_step, so_far(v_step))
                dve.tensor_scalar(tab(2, 1, 0), tab(2, 1, 5), -1.0, None, ALU.mult).then_inc(routed, 1)
                dve.wait_ge(routed, so_far(routed))
                one_hot(tab(3, 4), lg, tab(2, 1, 5), co("rank_g"), 4, tab(4, 4))
                inside = tab(5).rearrange("p t (g e) -> p t g e", g=GROUPS)
                for tile in range(nt):
                    dve.tensor_copy(inside[:, tile], route[:, 3, tile, 0:4, None].to_broadcast([P, GROUPS, PER_GROUP])).then_inc(v_step, 1)
                    dve.wait_ge(v_step, so_far(v_step))
                dve.tensor_tensor(tab(6), le, tab(5), ALU.mult).then_inc(v_step, 1)
                dve.wait_ge(v_step, so_far(v_step))
                dve.tensor_scalar(tab(7), tab(5), -NEG, NEG, ALU.mult, ALU.add).then_inc(v_step, 1)
                dve.wait_ge(v_step, so_far(v_step))
                dve.tensor_tensor(tab(6), tab(6), tab(7), ALU.add).then_inc(v_step, 1)
                dve.wait_ge(v_step, so_far(v_step))
                dve.tensor_reduce(tab(2, 1, 6), tab(6), AX, ALU.max).then_inc(v_step, 1)
                dve.wait_ge(v_step, so_far(v_step))
                one_hot(tab(8), tab(6), tab(2, 1, 6), co("rank_e"), EXPERTS, tab(7))
                dve.scalar_tensor_tensor(tab(7), tab(8), 2 * NEG, tab(6), ALU.mult, ALU.add).then_inc(v_step, 1)
                dve.wait_ge(v_step, so_far(v_step))
                dve.tensor_reduce(tab(2, 1, 7), tab(7), AX, ALU.max).then_inc(v_step, 1)
                dve.wait_ge(v_step, so_far(v_step))
                dve.tensor_tensor(tab(2, 1, 3), tab(2, 1, 7), tab(2, 1, 6), ALU.subtract).then_inc(routed, 1)
                dve.wait_ge(routed, so_far(routed))
                one_hot(tab(9), tab(7), tab(2, 1, 7), co("rank_e"), EXPERTS, tab(10))
                dve.tensor_tensor(tab(11), tab(8), tab(9), ALU.add).then_inc(v_step, 1)
                dve.wait_ge(v_step, so_far(v_step))
                dve.tensor_copy(tab(10), tab(11)).then_inc(chosen, 1)
                dve.wait_ge(chosen, so_far(chosen))
                dve.wait_ge(exp_ready, exp_in.next(2))
                dve.tensor_scalar(tab(2, 1, 9), tab(2, 1, 4), 1.0, None, ALU.add).then_inc(v_step, 1)
                dve.wait_ge(v_step, so_far(v_step))
                dve.tensor_tensor(tab(2, 1, 9), tab(2, 1, 9), tab(2, 1, 1), ALU.mult).then_inc(v_step, 1)
                dve.wait_ge(v_step, so_far(v_step))
                dve.reciprocal(tab(2, 1, 10), tab(2, 1, 9)).then_inc(v_step, 1)
                dve.wait_ge(v_step, so_far(v_step))
                dve.tensor_tensor(tab(2, 1, 11), tab(2, 1, 10), tab(2, 1, 4), ALU.mult).then_inc(v_step, 1)
                dve.wait_ge(v_step, so_far(v_step))
                dve.memset(route[:, 12:14, :, :], -1.0).then_inc(v_step, 1)
                dve.wait_ge(v_step, so_far(v_step))
                dve.tensor_tensor(tab(8), tab(8), over(tab(2, 1, 10), EXPERTS), ALU.mult).then_inc(v_step, 1)
                dve.wait_ge(v_step, so_far(v_step))
                dve.tensor_tensor(tab(9), tab(9), over(tab(2, 1, 11), EXPERTS), ALU.mult).then_inc(v_step, 1)
                dve.wait_ge(v_step, so_far(v_step))
                dve.tensor_tensor(tab(12), tab(8), tab(9), ALU.add).then_inc(v_step, 1)
                dve.wait_ge(v_step, so_far(v_step))
                dve.wait_ge(mm_v, jobs.next())
                bank = next_bank()
                pos = bank[:, 0:EXPERTS * nt].rearrange("p (t e) -> p t e", t=nt)
                dve.scalar_tensor_tensor(tab(7), pos, 1.0, tab(11), ALU.add, ALU.mult).then_inc(v_step, 1)
                dve.wait_ge(v_step, so_far(v_step))
                dve.tensor_scalar(tab(13), tab(7), -1.0, None, ALU.add).then_inc(v_step, 1)
                dve.wait_ge(v_step, so_far(v_step))
                fullest = route[:, 14, 0, 0:1]
                dve.tensor_reduce(fullest, bank[:, EXPERTS * nt:EXPERTS * nt + EXPERTS], AX, ALU.max).then_inc(v_free, 1)
                dve.wait_ge(v_free, so_far(v_free))
                for r in range(nt):
                    inst = dve.tensor_scalar(route[:, 14, 0, 1 + r:2 + r], fullest, float(SLOTS + P * r), None, ALU.is_gt)
                inst.then_inc(v_step, 1)
                dve.wait_ge(v_step, so_far(v_step))
                dve.tensor_reduce(fullest, route[:, 14, 0, 1:1 + nt], AX, ALU.add).then_inc(v_step, 1)
                dve.wait_ge(v_step, so_far(v_step))
                dve.tensor_copy(late_rounds[:, :], route[0:1, 14, 0, 0:1]).then_inc(rounds_ready, 1)
                dve.wait_ge(rounds_ready, so_far(rounds_ready))

            def late_rows(l, nt):
                s = late[l]
                product, silu, steps = Tally(s["product"]), Tally(s["a"]), {s[n].name: Tally(s[n]) for n in ("v", "step", "round", "added")}
                own.update(steps)

                at = route[:, 15, 0:nt, 0:EXPERTS]
                dve.memset(mark[:, 0:1], 0.0).then_inc(s["free"], 1)
                dve.wait_ge(s["free"], so_far(s["free"]))
                count = dve.value_load(late_rounds[0:1, 0:1], min_val=0, max_val=nt)
                dve.tensor_scalar(at, route[:, 13, 0:nt, 0:EXPERTS], P - SLOTS, None, ALU.add).then_inc(v_step, 1)
                dve.wait_ge(v_step, so_far(v_step))
                per = {product: 5, silu: 3, steps[s["v"].name]: 5, steps[s["step"].name]: 1, steps[s["added"].name]: 2 * nt}
                with laps(dve, nt, {**{t: EXPERTS * n for t, n in per.items()}, steps[s["round"].name]: 1}) as r:
                    with dve.If(count > r):
                        dve.tensor_scalar(at, at, -P, None, ALU.add).then_inc(s["round"], 1)
                        rounds = steps[s["round"].name]
                        rounds.n += 1
                        with laps(dve, EXPERTS, per) as e:
                            dve.wait_ge(s["round"], rounds.value())
                            col = route[:, 15, 0:nt, bass.ds(e, 1)].to_broadcast([P, nt, P])
                            dve.tensor_tensor(pick[:, 0, 0:nt, :], co("slot")[:, None, :].to_broadcast([P, nt, P]), col, ALU.is_equal).then_inc(s["step"], 1)
                            dve.wait_ge(s["step"], so_far(s["step"]))
                            col = route[:, 12, 0:nt, bass.ds(e, 1)].to_broadcast([P, nt, P])
                            dve.tensor_tensor(share[:, 0, 0:nt, :], pick[:, 0, 0:nt, :], col, ALU.mult).then_inc(s["v"], 1)
                            dve.wait_ge(s["v"], so_far(s["v"]))
                            dve.wait_ge(s["product"], product.next())
                            dve.tensor_copy(shareT[:, 0:nt, :], psum[:, 0, 0:P * nt].rearrange("p (t n) -> p t n", t=nt)).then_inc(s["v"], 1)
                            dve.wait_ge(s["v"], so_far(s["v"]))
                            dve.wait_ge(s["product"], product.next())
                            dve.wait_ge(s["a"], silu.next(2))
                            dve.tensor_tensor(act_, psum[:, 1, :], siluG, ALU.mult).then_inc(s["v"], 1)
                            dve.wait_ge(s["v"], so_far(s["v"]))
                            dve.wait_ge(s["product"], product.next())
                            dve.tensor_copy(actT, psum[:, 2, :].rearrange("p (f n) -> p f n", f=4)).then_inc(s["v"], 1)
                            dve.wait_ge(s["v"], so_far(s["v"]))
                            dve.wait_ge(s["product"], product.next())
                            dve.tensor_copy(ySlot[:, 512:1024], psum[:, 3, :]).then_inc(s["v"], 1)
                            dve.wait_ge(s["v"], so_far(s["v"]))
                            silu.n += 1
                            dve.wait_ge(s["product"], product.next())
                            for tile in range(nt):
                                for h in range(2):
                                    f = facc[:, tile, 512 * h:512 * h + 512]
                                    dve.tensor_tensor(f, f, psum[:, 2 * tile + h, :], ALU.add).then_inc(s["added"], 1)
                                    dve.wait_ge(s["added"], so_far(s["added"]))
                    dve.end_ifs()

            def moe(l):
                nt = 4 - 2 * l
                tiles = [0, 1, 2, 3][2 * l:]
                norm(2 * l + 1, 1, tiles)
                for tile in range(nt):
                    dve.wait_ge(mm_v, jobs.next())
                    bank = next_bank()
                    dve.tensor_copy(hrow[:, tile, 0:512], bank).then_inc(v_free, 1)
                    dve.wait_ge(v_free, so_far(v_free))
                choose(l, nt)
                dve.memset(facc[:, 0:nt, :], 0.0).then_inc(v_step, 1)
                dve.wait_ge(v_step, so_far(v_step))

                def selector(dst, e0, weigh, signal):
                    d = dst[:, 0:nt, :].rearrange("p t (e s) -> p t e s", e=2)
                    for e in range(2):
                        slots = co("slot", width=SLOTS)[:, None, :].to_broadcast([P, nt, SLOTS])
                        col = route[:, 13, 0:nt, bass.ds(e0 + e, 1)].to_broadcast([P, nt, SLOTS])
                        inst = dve.tensor_tensor(d[:, :, e, :], slots, col, ALU.is_equal)
                    if weigh:
                        inst.then_inc(v_step, 1)
                        dve.wait_ge(v_step, so_far(v_step))
                        for e in range(2):
                            col = route[:, 12, 0:nt, bass.ds(e0 + e, 1)].to_broadcast([P, nt, SLOTS])
                            inst = dve.tensor_tensor(d[:, :, e, :], d[:, :, e, :], col, ALU.mult)
                    if signal:
                        inst.then_inc(pick_ready, 1)
                        dve.wait_ge(pick_ready, so_far(pick_ready))

                def add_pair():
                    for tile in range(nt):
                        for h in range(2):
                            dve.wait_ge(mm_v, jobs.next())
                            bank = next_bank()
                            f = facc[:, tile, 512 * h:512 * h + 512]
                            dve.tensor_tensor(f, f, bank, ALU.add).then_inc(v_free, 1)
                            dve.wait_ge(v_free, so_far(v_free))

                dve.memset(shareT[:, 0:nt, :], 0.0)
                dve.memset(ySlot, 0.0)
                selector(pick[:, 0], 0, False, False)
                selector(share[:, 0], 0, True, True)
                selector(pick[:, 1], 2, False, True)
                base = job[0]
                per_pair = 4 + 2 * nt
                assert per_pair % 4 == 0
                job[0] = 0
                mine = {own[v_step.name]: 2, own[v_free.name]: 2 * per_pair, own[pick_ready.name]: 2}
                with laps(dve, PAIRS // 2, {jobs: 2 * (per_pair - 2), chunks: 24, silus: 2, **mine}) as i:
                    for b in range(2):
                        add_pair()
                        dve.wait_ge(used, chunks.next(8))
                        bank = next_bank()
                        dve.wait_ge(sil_ready, silus.next())
                        dve.tensor_tensor(act_, bank, siluG, ALU.mult).then_inc(v_free, 1)
                        dve.wait_ge(v_free, so_far(v_free))
                        dve.wait_ge(mm_v, jobs.next())
                        bank = next_bank()
                        dve.tensor_copy(actT, bank.rearrange("p (f n) -> p f n", f=4)).then_inc(v_free, 1)
                        dve.wait_ge(v_free, so_far(v_free))
                        dve.wait_ge(mm_v, jobs.next())
                        bank = next_bank()
                        dve.tensor_copy(shareT[:, 0:nt, :], bank[:, 0:P * nt].rearrange("p (t n) -> p t n", t=nt)).then_inc(v_free, 1)
                        dve.wait_ge(v_free, so_far(v_free))
                        selector(share[:, 1 - b], 4 * i + 2 * b + 2, True, False)
                        selector(pick[:, b], 4 * i + 2 * b + 4, False, True)
                        dve.wait_ge(used, chunks.next(4))
                        bank = next_bank()
                        dve.tensor_copy(ySlot[:, 512:1024], bank).then_inc(v_free, 1)
                        dve.wait_ge(v_free, so_far(v_free))
                add_pair()
                job[0] = base + PAIRS * per_pair + 2 * nt
                late_rows(l, nt)
                for tile in range(nt):
                    dve.tensor_tensor(facc[:, tile, :], facc[:, tile, :], gate[:, 1, 1 if tile + 2 * l < 2 else 0, :], ALU.mult).then_inc(v_step, 1)
                    dve.wait_ge(v_step, so_far(v_step))
                    x = X[:, tile + 2 * l, :]
                    last = dve.tensor_tensor(x, x, facc[:, tile, :], ALU.add)
                    if tile == nt - 1:
                        last.then_inc(x_ready, 1)
                        dve.wait_ge(x_ready, so_far(x_ready))
                    else:
                        last.then_inc(v_step, 1)
                        dve.wait_ge(v_step, so_far(v_step))

            def gains2():
                for name, at, n in (("attn_norm", G_ATTN, D), ("q_norm", G_Q, 256), ("kv_norm", G_KV, P),
                                    ("mix_norm", G_MIX, 512), ("mlp_norm", G_MLP, D)):
                    w = par_at[name][1]
                    inst = dve.tensor_scalar(g2[:, at:at + w], pa(name), n ** 0.5, None, ALU.mult)
                inst.then_inc(gain_ready, 1)
                dve.wait_ge(gain_ready, so_far(gain_ready))

            def turned2(g):
                for k in range(0, KB, 2):
                    dve.wait_ge(mm_v, jobs.next())
                    bank = next_bank()
                    dve.tensor_scalar(hT[:, k, 0:SEQ], bank[:, 0:SEQ], g2[:, g + k:g + k + 1], None, ALU.mult).then_inc(v_free, 1)
                    dve.wait_ge(v_free, so_far(v_free))

            def rotated(dst, src, heads, cos, sin):
                n = cos.shape[-1]
                m = n // 2
                a, b = h64(TA[:, 0:heads * n], n), h64(TB[:, 0:heads * n], n)
                dve.tensor_tensor(a, src, cos[:, None, :].to_broadcast([P, heads, n]), ALU.mult)
                dve.tensor_tensor(b[:, :, 0:m], src[:, :, m:n], sin[:, None, 0:m].to_broadcast([P, heads, m]), ALU.mult)
                dve.tensor_tensor(b[:, :, m:n], src[:, :, 0:m], sin[:, None, m:n].to_broadcast([P, heads, m]), ALU.mult).then_inc(v_step, 1)
                dve.wait_ge(v_step, so_far(v_step))
                return dve.tensor_tensor(dst, a, b, ALU.add)

            def project2():
                for c in range(4):
                    for m in range(2):
                        cos, sin = (co(n, at=HD * m, width=HD) for n in ("cos_a", "sin_a"))
                        if m:
                            dve.wait_ge(used, chunks.next(2))
                        else:
                            dve.wait_ge(mm_v, jobs.next())
                        bank = next_bank()
                        if c == 0:
                            dve.tensor_copy(TX, bank).then_inc(v_free, 1)
                            dve.wait_ge(v_free, so_far(v_free))
                            rotated(h64(R[m]), h64(TX), 8, cos, sin).then_inc(rows_ready, 1)
                            dve.wait_ge(rows_ready, so_far(rows_ready))
                            continue
                        w = min(512, IN2 - 512 * c)
                        dve.tensor_copy(PR[:, m, 512 * c:512 * c + w], bank[:, 0:w]).then_inc(v_free, 1)
                        dve.wait_ge(v_free, so_far(v_free))
                        if c == 1:
                            for b, col in ((0, KC2), (4, KS2)):
                                rotated(h64(TX[:, 0:P]), h64(PR[:, m, col:col + P]), 2, cos, sin).then_inc(v_step, 1)
                                dve.wait_ge(v_step, so_far(v_step))
                                dve.tensor_copy(KD[m][:, b:b + 2], h64(TX[:, 0:P])[:, :, None, :].to_broadcast([P, 2, 2, HD])).then_inc(v_step, 1)
                                dve.wait_ge(v_step, so_far(v_step))
                            dve.tensor_copy(KD[m][:, 2:4], h64(PR[:, m, VC2:VC2 + P])[:, :, None, :].to_broadcast([P, 2, 2, HD])).then_inc(rows_ready, 1)
                            dve.wait_ge(rows_ready, so_far(rows_ready))
                        elif c == 2:
                            rotated(h64(TX[:, 0:P]), h64(PR[:, m, KW2:KW2 + P]), 2, cos, sin).then_inc(v_step, 1)
                            dve.wait_ge(v_step, so_far(v_step))
                            dve.tensor_copy(KWD[m], h64(TX[:, 0:P])[:, :, None, :].to_broadcast([P, 2, 2, HD])).then_inc(rows_ready, 1)
                            dve.wait_ge(rows_ready, so_far(rows_ready))
                        else:
                            for col, n, at in ((CQ2, 256, 0), (CKV2, P, 256)):
                                x = PR[:, m, col:col + n]
                                dve.tensor_tensor(SQ[:, 0:n], x, x, ALU.mult).then_inc(v_step, 1)
                                dve.wait_ge(v_step, so_far(v_step))
                                b = 1 + heads_done.n % 2
                                dve.tensor_reduce(sumsq[:, b, 0:1], SQ[:, 0:n], AX, ALU.add).then_inc(hs_ready, 1)
                                dve.wait_ge(hs_ready, so_far(hs_ready))
                                dve.wait_ge(hs_done, heads_done.next())
                                dve.tensor_scalar(CQ[m][:, at:at + n], x, rstd[:, b, 0:1], None, ALU.mult).then_inc(v_step, 1)
                                dve.wait_ge(v_step, so_far(v_step))
                            kr = PR[:, m, KR2:KR2 + 32]
                            rotated(kpe[:, m:m + 1, :], kr[:, None, :], 1,
                                    co("cos_b", at=32 * m, width=32), co("sin_b", at=32 * m, width=32)).then_inc(rows_ready, 1)
                            dve.wait_ge(rows_ready, so_far(rows_ready))
                dve.memset(mark[:, 0:1], 0.0).then_inc(routed, 1)
                dve.wait_ge(routed, so_far(routed))
                dve.wait_ge(exp_ready, exp_in.next())
                dve.tensor_scalar(gs, gs, 1.0, None, ALU.add).then_inc(v_step, 1)
                dve.wait_ge(v_step, so_far(v_step))
                dve.reciprocal(gs, gs).then_inc(v_step, 1)
                dve.wait_ge(v_step, so_far(v_step))
                for m in range(2):
                    q = rows[:, m, 0:768]
                    dve.wait_ge(mm_v, jobs.next())
                    bank = next_bank()
                    dve.tensor_copy(q[:, 0:512], bank).then_inc(v_free, 1)
                    dve.wait_ge(v_free, so_far(v_free))
                    if m:
                        dve.wait_ge(used, chunks.next(1))
                    else:
                        dve.wait_ge(mm_v, jobs.next())
                    bank = next_bank()
                    dve.tensor_copy(q[:, 512:768], bank[:, 0:256]).then_inc(v_free, 1)
                    dve.wait_ge(v_free, so_far(v_free))
                    part = q.rearrange("p (h n) -> p h n", h=8)[:, :, HD:MLA_D]
                    rotated(part, part, 8, co("cos_b", at=32 * m, width=32), co("sin_b", at=32 * m, width=32)).then_inc(rows_ready, 1)
                    dve.wait_ge(rows_ready, so_far(rows_ready))
                for m in range(2):
                    k = rows[:, 2 + m, 0:768].rearrange("p (h n) -> p h n", h=8)
                    for j in range(2):
                        if m and j:
                            dve.wait_ge(used, chunks.next(1))
                        else:
                            dve.wait_ge(mm_v, jobs.next())
                        kv = next_bank().rearrange("p (h n) -> p h n", h=4)
                        dve.tensor_copy(k[:, 4 * j:4 * j + 4, 0:HD], kv[:, :, 0:HD])
                        dve.tensor_copy(h64(VM[:, m, 256 * j:256 * j + 256]), kv[:, :, HD:P]).then_inc(v_free, 1)
                        dve.wait_ge(v_free, so_far(v_free))
                    dve.tensor_copy(k[:, :, HD:MLA_D], kpe[:, m:m + 1, :].to_broadcast([P, 8, 32])).then_inc(rows_ready, 1)
                    dve.wait_ge(rows_ready, so_far(rows_ready))

            def compress(l):
                for w, name in enumerate(("pos_k", "pos_v")):
                    pos = pa(name, at=16 * l, width=16)
                    for g in range(2):
                        x = kvT2[:, 2 * w + g, :]
                        win = bass.AP(tensor=x.tensor, offset=x.offset, ap=[list(x.ap[0]), [1, 16], [8, 15]])
                        inst = dve.tensor_tensor(XB[:, w, :, g, :], win, pos[:, :, None].to_broadcast([P, 16, 15]), ALU.add)
                    inst.then_inc(rows_ready, 1)
                    dve.wait_ge(rows_ready, so_far(rows_ready))
                chunks.n += 4
                dve.wait_ge(mm_v, jobs.next())
                bank = next_bank()
                t4 = bank[:, 0:P].rearrange("p (b n) -> p b n", b=4)
                dve.tensor_copy(hidT[:, 0:2, 0:30], t4[:, 0:2, 0:30])
                for j in range(2):
                    src = t4[:, 2 + j, 0:30].rearrange("p (g i) -> p g i", g=2)[:, :, None, :].to_broadcast([P, 2, 4, 15])
                    inst = dve.tensor_copy(hv[:, j, :, 0:15].rearrange("p (g h) i -> p g h i", g=2), src)
                inst.then_inc(v_free, 1)
                dve.wait_ge(v_free, so_far(v_free))
                dve.wait_ge(mm_v, jobs.next())
                bank = next_bank()
                kc = bank[:, 0:30].rearrange("p (g i) -> p g i", g=2)
                dve.tensor_copy(kC[0:64, :, 0, 0:15], kc[0:64])
                dve.tensor_copy(kC[64:128, :, 1, 0:15], kc[64:128])
                dve.tensor_tensor(vBD, bank[:, None, 64:128].to_broadcast([P, 8, HD]),
                                  co("block_diag")[:, :, None].to_broadcast([P, 8, HD]), ALU.mult).then_inc(v_free, 1)
                dve.wait_ge(v_free, so_far(v_free))

            def mix_norm():
                for m in range(2):
                    o = oA[:, m, :]
                    sq = rows[:, 2, :]
                    dve.tensor_tensor(sq, o, o, ALU.mult).then_inc(v_step, 1)
                    dve.wait_ge(v_step, so_far(v_step))
                    b = 1 + heads_done.n % 2
                    dve.tensor_reduce(sumsq[:, b, 0:2], sq.rearrange("p (h n) -> p h n", h=2), AX, ALU.add).then_inc(hs_ready, 1)
                    dve.wait_ge(hs_ready, so_far(hs_ready))
                    dve.wait_ge(hs_done, heads_done.next())
                    o2 = o.rearrange("p (h n) -> p h n", h=2)
                    dve.tensor_tensor(o2, o2, rstd[:, b, 0:2, None].to_broadcast([P, 2, 512]), ALU.mult).then_inc(rows_ready, 1)
                    dve.wait_ge(rows_ready, so_far(rows_ready))

            def mlp():
                for c in range(8):
                    dve.wait_ge(used, chunks.next(2))
                    bank = next_bank()
                    f = aT[:, 4 * c + 2:4 * c + 4, :]
                    dve.tensor_scalar(f, bank.rearrange("p (f n) -> p f n", f=2), 0.0, None, ALU.max).then_inc(v_step, 1)
                    dve.wait_ge(v_step, so_far(v_step))
                    dve.tensor_tensor(f, f, f, ALU.mult).then_inc(v_free, 1)
                    dve.wait_ge(v_free, so_far(v_free))
                for m in range(2):
                    for h in range(2):
                        if m and h:
                            dve.wait_ge(used, chunks.next(16))
                        else:
                            dve.wait_ge(mm_v, jobs.next())
                        bank = next_bank()
                        x = X[:, 2 + m, 512 * h:512 * h + 512]
                        dve.tensor_tensor(x, x, bank, ALU.add).then_inc(v_free, 1)
                        dve.wait_ge(v_free, so_far(v_free))
                dve.memset(mark[:, 0:1], 0.0).then_inc(x_ready, 1)
                dve.wait_ge(x_ready, so_far(x_ready))

            def final_norm():
                dve.wait_ge(rs_done, norms_done.next())
                dve.wait_ge(final_in, 16)
                for m in range(2):
                    dve.tensor_scalar(rows[:, m, :], X[:, 2 + m, :], rstd[:, 0, m:m + 1], D ** 0.5, ALU.mult, ALU.mult).then_inc(v_step, 1)
                    dve.wait_ge(v_step, so_far(v_step))
                    dve.tensor_tensor(rows[:, m, :], rows[:, m, :], arena[:, 0:D], ALU.mult).then_inc(x_ready, 1)
                    dve.wait_ge(x_ready, so_far(x_ready))

            init()
            mod(0)
            norm(0, 0, [0, 1, 2, 3])
            heads_ab()
            attention(groups_ab())
            outputs_T(4)
            add_output(0, [0, 1, 2, 3])
            moe(0)
            mod(1)
            norm(2, 0, [0, 1, 2, 3])
            heads_c()
            differential()
            attention(groups_c())
            sub_norm()
            outputs_T(2)
            add_output(0, [2, 3])
            moe(1)
            gains2()
            for l in range(DEPTH):
                scaled_rows([2, 3])
                turned2(G_ATTN + KB * l)
                project2()
                compress(l)
                attention(groups_2())
                mix_norm()
                turned2(G_MIX + KB * l)
                add_output(None, [2, 3])
                scaled_rows([2, 3])
                turned2(G_MLP + KB * l)
                mlp()
            final_norm()

        @block.tensor
        def _(pe):
            v_done, a_done = Tally(v_free), Tally(a_free)
            vi, ai, chunk = [0], [0], [0]
            chunk_in = [Tally(s, 16) for s in loaded]
            xn, rws, outs, picks = Tally(xn_ready), Tally(rows_ready), Tally(att_o), Tally(pick_ready)
            expd, tv, ta = Tally(att_e), Tally(att_tv), Tally(att_ta)
            mixed, choice = Tally(mod_row), Tally(chosen)

            def v_bank():
                v_done.n += 1
                vi[0] += 1
                return psum[:, (vi[0] - 1) % 4, :]

            def a_bank():
                a_done.n += 1
                ai[0] += 1
                return psum[:, 4 + (ai[0] - 1) % 4, :]

            def weights(n):
                out = []
                for _ in range(n):
                    slot = chunk[0] % RING
                    chunk[0] += 1
                    pe.wait_ge(loaded[slot], chunk_in[slot].next())
                    out.append(ring[:, slot, :])
                return out

            def k512(pair):
                return [pair[k // 4].rearrange("p (k n) -> p k n", k=4)[:, k % 4, :] for k in range(KB)]

            def transpose(out, in_):
                return pe.transpose(out, in_, ident)

            def mod(l):
                if not l:
                    pe.wait_ge(c_ready, 1)
                    pe.wait_ge(consts_in, 16)
                pe.wait_ge(v_free, v_done.value())
                pe.wait_ge(a_free, a_done.value())

                def columns(c):
                    pe.wait_ge(mod_row, mixed.next())
                    pe.wait_ge(a_free, a_done.value(back=3))
                    bank = a_bank()
                    m = mrow[:, c % 2, :]
                    for j in range(4):
                        inst = pe.matmul(bank[:, 2 * j:2 * j + 2], m[:, P * j:P * j + P], co("fold"), start=True, stop=True)
                    inst.then_inc(mm_a, 1)
                    if c in (4, 5, 10, 11):
                        for r in range(2):
                            pe.wait_ge(a_free, a_done.value(back=3))
                            bank = a_bank()
                            pe.matmul(bank, co("spread", at=P * r, width=P), m, start=True, stop=True).then_inc(mm_a, 1)

                for c in range(12):
                    w = k512(weights(2))
                    for k in range(KB):
                        j = k % 4
                        inst = pe.matmul(psum[32 * j:32 * j + 32, c % 4, :], cpad[:, k, :], w[k], start=k < 4, stop=k >= 4)
                        if k in (3, 7):
                            inst.then_inc(used, 1)
                    if c:
                        columns(c - 1)
                columns(11)

            def norm(nt):
                for m in range(nt):
                    pe.wait_ge(xn_ready, xn.next())
                for k in range(KB):
                    if k % 2:
                        pe.wait_ge(a_free, a_done.value(back=3))
                        bank = a_bank()
                    else:
                        pe.wait_ge(v_free, v_done.value(back=3))
                        bank = v_bank()
                    for m in range(nt):
                        inst = transpose(bank[:, P * m:P * m + P], rows[:, m, P * k:P * k + P])
                    inst.then_inc(mm_a if k % 2 else mm_v, 1)

            def columns512(w, m, last):
                pe.wait_ge(v_free, v_done.value(back=3))
                bank = v_bank()
                for k in range(KB):
                    inst = pe.matmul(bank, hT[:, k, P * m:P * m + P], w[k], start=k == 0, stop=k == KB - 1)
                    if last and k == 3:
                        inst.then_inc(used, 1)
                inst.then_inc(used if last else mm_v, 1)

            def heads(blocks, tiles_of, turn):
                pe.wait_ge(v_free, v_done.value())
                pe.wait_ge(a_free, a_done.value())
                waiting = []
                for c in range(blocks):
                    w = k512(weights(2))
                    tiles = tiles_of(c)
                    for tile in tiles:
                        columns512(w, tile, tile == tiles[-1])
                        if waiting:
                            turn(*waiting.pop())
                        waiting.append((c, tile))
                turn(*waiting.pop())

            turn_n = [0]

            def turn_ab(c, tile):
                pe.wait_ge(rows_ready, rws.next())
                b = turn_n[0] % 2
                turn_n[0] += 1
                pe.wait_ge(a_free, a_done.value(back=3))
                bank = a_bank()
                s0, nq, _ = AB[c]["q"]
                for j in range(nq):
                    inst = transpose(bank[:, P * j:P * j + P], R[b][:, s0 + P * j:s0 + P * j + P])
                if AB[c]["k"]:
                    for j in range(2):
                        inst = transpose(bank[:, 256 + P * j:256 + P * j + P], KDUP[b][:, P * j:P * j + P])
                inst.then_inc(mm_a, 1)

            def turn_c(c, tile):
                if c >= 4:
                    return
                pe.wait_ge(rows_ready, rws.next())
                b = turn_n[0] % 2
                turn_n[0] += 1
                pe.wait_ge(a_free, a_done.value(back=3))
                bank = a_bank()
                for j in range(4):
                    inst = transpose(bank[:, P * j:P * j + P], R[b][:, P * j:P * j + P])
                inst.then_inc(mm_a, 1)

            att_n = [0]

            def attention(groups):
                pe.wait_ge(v_free, v_done.value())
                pe.wait_ge(a_free, a_done.value())
                base = att_n[0]
                att_n[0] += len(groups)

                def scores(n):
                    g = groups[n]
                    if base + n >= 2:
                        pe.wait_ge(att_e, base + n - 1)
                    s = psum[:, 2 * ((base + n) % 2):2 * ((base + n) % 2) + 2, :].rearrange("p a n -> p (a n)")
                    for u, (q, k) in enumerate(g["scores"]):
                        inst = pe.matmul(s[:, g["nk"] * u:g["nk"] * u + g["nk"]], q, k, start=True, stop=True)
                    inst.then_inc(att_s, 1)

                def turn(n):
                    pe.wait_ge(att_e, base + n + 1)
                    if base + n:
                        pe.wait_ge(att_tv, base + n)
                        pe.wait_ge(att_ta, base + n)
                    p = probs[:, (base + n) % 2, :]
                    for b in range(width(groups[n]) // P):
                        inst = transpose(psum[:, 4 + b // 4, P * (b % 4):P * (b % 4) + P], p[:, P * b:P * b + P])
                    inst.then_inc(att_t, 1)

                def values(n):
                    g = groups[n]
                    pe.wait_ge(att_tv, base + n + 1)
                    pe.wait_ge(att_ta, base + n + 1)
                    if base + n >= 2:
                        pe.wait_ge(att_o, base + n - 1)
                    pT, dv, b = probsT[:, (base + n) % 2, :], g["dv"], 0
                    o = psum[:, 6 + (base + n) % 2, :]
                    if "pv_all" in g:
                        inst = pe.matmul(o, pT[:, 0:P], g["pv_all"].rearrange("p h n -> p (h n)"), start=True, stop=True)
                    for u, vs in enumerate(g.get("pv", [])):
                        for m, vb in enumerate(vs):
                            inst = pe.matmul(o[:, dv * u:dv * u + dv], pT[:, P * b:P * b + P], vb, start=m == 0, stop=m == len(vs) - 1)
                            b += 1
                    inst.then_inc(att_pv, 1)

                scores(0)
                for n in range(len(groups)):
                    if n + 1 < len(groups):
                        scores(n + 1)
                    if n:
                        values(n - 1)
                    turn(n)
                values(len(groups) - 1)
                pe.wait_ge(att_o, att_n[0])

            def output(tiles, rows_in):
                nt = len(tiles)
                pe.wait_ge(rows_ready, rws.next(rows_in))
                for k in range(KB):
                    if k % 2:
                        pe.wait_ge(a_free, a_done.value(back=3))
                        bank = a_bank()
                    else:
                        pe.wait_ge(v_free, v_done.value(back=3))
                        bank = v_bank()
                    for m in range(nt):
                        inst = transpose(bank[:, P * m:P * m + P], oA[:, m, P * k:P * k + P])
                    inst.then_inc(mm_a if k % 2 else mm_v, 1)
                pe.wait_ge(v_free, v_done.value())
                pe.wait_ge(a_free, a_done.value())
                for c in range(2):
                    w = k512(weights(2))
                    for m in range(nt):
                        columns512(w, m, m == nt - 1)

            def late_products(l, nt):
                s = late[l]
                loads, rows_v, rows_a, added = Tally(s["loaded"], 16), Tally(s["v"]), Tally(s["a"]), Tally(s["added"])
                chunk = [ring[:, j, :] for j in range(6)]
                up = [[chunk[2 * a + k // 4].rearrange("p (k n) -> p k n", k=4)[:, k % 4, :] for k in range(KB)] for a in range(2)]
                down = [chunk[4 + f // 2].rearrange("p (f n) -> p f n", f=2)[:, f % 2, :] for f in range(4)]
                pe.wait_ge(rounds_ready, l + 1)
                count = pe.value_load(late_rounds[0:1, 0:1], min_val=0, max_val=nt)
                per = {loads: 6, rows_v: 5, rows_a: 3, added: 2 * nt}
                with laps(pe, nt, {t: EXPERTS * n for t, n in per.items()}) as r:
                    with pe.If(count > r):
                        with laps(pe, EXPERTS, per):
                            pe.wait_ge(s["v"], rows_v.next())
                            for k in range(KB):
                                for m in range(nt):
                                    pe.matmul(psum[:, 5 + k // 4, P * (k % 4):P * (k % 4) + P], hrow[:, m, P * k:P * k + P], pick[:, 0, m, :],
                                              start=m == 0, stop=m == nt - 1)
                            for m in range(nt):
                                inst = transpose(psum[:, 0, P * m:P * m + P], share[:, 0, m, :])
                            inst.then_inc(s["product"], 1)
                            pe.wait_ge(s["loaded"], loads.next(6))
                            pe.wait_ge(s["a"], rows_a.next())
                            for bank, w in ((4, up[0]), (1, up[1])):
                                for k in range(KB):
                                    inst = pe.matmul(psum[:, bank, :], xgT[:, 0, k, :], w[k], start=k == 0, stop=k == KB - 1)
                            inst.then_inc(s["product"], 1)
                            pe.wait_ge(s["v"], rows_v.next(2))
                            for f in range(4):
                                inst = transpose(psum[:, 2, P * f:P * f + P], act_[:, P * f:P * f + P])
                            inst.then_inc(s["product"], 1)
                            pe.wait_ge(s["v"], rows_v.next())
                            for bank, h in ((7, 0), (3, 1)):
                                for f in range(4):
                                    inst = pe.matmul(psum[:, bank, :], actT[:, f, :], down[f][:, 512 * h:512 * h + 512], start=f == 0, stop=f == 3)
                            inst.then_inc(s["product"], 1)
                            pe.wait_ge(s["a"], rows_a.next(2))
                            pe.wait_ge(s["v"], rows_v.next())
                            for m in range(nt):
                                for h in range(2):
                                    inst = pe.matmul(psum[:, 2 * m + h, :], shareT[:, m, :], ySlot[:, 512 * h:512 * h + 512], start=True, stop=True)
                                    if not m and not h:
                                        inst.then_inc(s["free"], 1)
                            inst.then_inc(s["product"], 1)
                            pe.wait_ge(s["added"], added.next(2 * nt))
                    pe.end_ifs()

            def moe(l):
                nt = 4 - 2 * l
                norm(nt)
                pe.wait_ge(v_free, v_done.value())
                pe.wait_ge(a_free, a_done.value())
                for m in range(nt):
                    for h in range(2):
                        if h:
                            pe.wait_ge(a_free, a_done.value(back=3))
                            bank = a_bank()
                        else:
                            pe.wait_ge(v_free, v_done.value(back=3))
                            bank = v_bank()
                        for k in range(4):
                            inst = transpose(bank[:, P * k:P * k + P], hT[:, 4 * h + k, P * m:P * m + P])
                        inst.then_inc(mm_a if h else mm_v, 1)
                pe.wait_ge(v_free, v_done.value(back=3))
                bank = v_bank()
                wr = pa("w_route", at=KB * ROUTES * l, width=KB * ROUTES).rearrange("p (k e) -> p k e", k=KB)
                for m in range(nt):
                    for k in range(KB):
                        inst = pe.matmul(bank[:, ROUTES * m:ROUTES * m + ROUTES], hT[:, k, P * m:P * m + P], wr[:, k, :],
                                         start=k == 0, stop=k == KB - 1)
                inst.then_inc(mm_v, 1)
                pe.wait_ge(chosen, choice.next())
                pe.wait_ge(v_free, v_done.value(back=3))
                bank = v_bank()
                for m in range(nt):
                    out = bank[:, EXPERTS * m:EXPERTS * m + EXPERTS]
                    for j in range(m):
                        pe.matmul(out, co("ones"), route[:, 11, j, 0:EXPERTS], start=j == 0, stop=False)
                    pe.matmul(out, co("before"), route[:, 11, m, 0:EXPERTS], start=m == 0, stop=True)
                for m in range(nt):
                    inst = pe.matmul(bank[:, EXPERTS * nt:EXPERTS * nt + EXPERTS], co("ones"), route[:, 11, m, 0:EXPERTS],
                                     start=m == 0, stop=m == nt - 1)
                inst.then_inc(mm_v, 1)
                pe.wait_ge(v_free, v_done.value())
                pe.wait_ge(a_free, a_done.value())

                def gather(b, h):
                    for k in range(4):
                        for m in range(nt):
                            kk = 4 * h + k
                            inst = pe.matmul(psum[:, 5 + h, P * k:P * k + P], hrow[:, m, P * kk:P * kk + P], pick[:, b, m, :],
                                             start=m == 0, stop=m == nt - 1)
                    inst.then_inc(mm_a, 1)
                    a_done.n += 1

                def up(out, b):
                    for k in range(KB):
                        if k in (0, 4):
                            w = weights(2)
                        for e in range(2):
                            m = w[e].rearrange("p (k n) -> p k n", k=4)[:, k % 4, :]
                            inst = pe.matmul(out[64 * e:64 * e + 64, :], xgT[:, b, k, 64 * e:64 * e + 64], m,
                                             start=k == 0, stop=k == KB - 1)
                            if k in (3, 7):
                                inst.then_inc(used, 1)

                def add_pair():
                    pe.wait_ge(v_free, v_done.value())
                    pe.wait_ge(a_free, a_done.value())
                    for m in range(nt):
                        for h in range(2):
                            pe.wait_ge(v_free, v_done.value(back=3))
                            bank = v_bank()
                            pe.matmul(bank, shareT[:, m, :], ySlot[:, 512 * h:512 * h + 512], start=True, stop=True).then_inc(mm_v, 1)

                pe.wait_ge(pick_ready, picks.next())
                for h in range(2):
                    gather(0, h)
                base = vi[0]
                vi[0] = 0
                per_pair = 4 + 2 * nt
                tallies = {v_done: 2 * per_pair, a_done: 6, picks: 2}
                tallies.update({c: 24 // RING for c in chunk_in})
                with laps(pe, PAIRS // 2, tallies):
                    for b in range(2):
                        pe.wait_ge(a_free, a_done.value())
                        up(psum[:, 4, :], b)
                        add_pair()
                        pe.wait_ge(v_free, v_done.value(back=3))
                        bank = v_bank()
                        up(bank, b)
                        pe.wait_ge(pick_ready, picks.next())
                        gather(1 - b, 0)
                        pe.wait_ge(v_free, v_done.value())
                        bank = v_bank()
                        for f in range(4):
                            inst = transpose(bank[:, P * f:P * f + P], act_[:, P * f:P * f + P])
                        inst.then_inc(mm_v, 1)
                        gather(1 - b, 1)
                        bank = v_bank()
                        for m in range(nt):
                            inst = transpose(bank[:, P * m:P * m + P], share[:, b, m, :])
                        inst.then_inc(mm_v, 1)
                        pe.wait_ge(v_free, v_done.value(back=1))
                        outs = [psum[:, 7, :], v_bank()]
                        for f in range(4):
                            if f in (0, 2):
                                w = weights(2)
                            for h in range(2):
                                for e in range(2):
                                    m = w[e].rearrange("p (k n) -> p k n", k=2)[:, f % 2, 512 * h:512 * h + 512]
                                    inst = pe.matmul(outs[h][64 * e:64 * e + 64, :], actT[:, f, 64 * e:64 * e + 64], m,
                                                     start=f == 0, stop=f == 3)
                                    if h and f % 2:
                                        inst.then_inc(used, 1)
                                if not h and f == 3:
                                    inst.then_inc(mm_a, 1)
                                    a_done.n += 1
                add_pair()
                vi[0] = base + PAIRS * per_pair + 2 * nt
                pe.wait_ge(pick_ready, picks.next())
                pe.wait_ge(v_free, v_done.value())
                pe.wait_ge(a_free, a_done.value())
                late_products(l, nt)

            def turn(parts):
                pe.wait_ge(rows_ready, rws.next())
                for part in parts:
                    pe.wait_ge(a_free, a_done.value(back=3))
                    bank = a_bank()
                    for j, x in enumerate(part):
                        inst = transpose(bank[0:x.shape[-1], P * j:P * j + P], x)
                    inst.then_inc(mm_a, 1)

            def project2():
                def blocks(x, w=P):
                    return [x[:, w * j:w * j + w] for j in range(x.shape[-1] // w)]

                def turned(c, m):
                    if c == 0:
                        turn([blocks(R[m])])
                    elif c == 1:
                        b = blocks(KD[m].rearrange("p b s n -> p (b s n)"))
                        turn([b[0:4], b[4:6]])
                    elif c == 2:
                        turn([blocks(KWD[m].rearrange("p b s n -> p (b s n)"))])
                    else:
                        turn([blocks(CQ[m])])

                pe.wait_ge(v_free, v_done.value())
                pe.wait_ge(a_free, a_done.value())
                waiting = []
                for c in range(4):
                    n = min(512, IN2 - 512 * c)
                    w = [x[:, 0:4 * n].rearrange("p (k n) -> p k n", k=4) for x in weights(2)]
                    for m in range(2):
                        pe.wait_ge(v_free, v_done.value(back=3))
                        bank = v_bank()
                        for k in range(KB):
                            inst = pe.matmul(bank[:, 0:n], hT[:, k, P * m:P * m + P], w[k // 4][:, k % 4, :], start=k == 0, stop=k == KB - 1)
                            if m and k == 3:
                                inst.then_inc(used, 1)
                        inst.then_inc(used if m else mm_v, 1)
                        if waiting:
                            turned(*waiting.pop())
                        waiting.append((c, m))
                turned(*waiting.pop())
                pe.wait_ge(v_free, v_done.value())
                pe.wait_ge(a_free, a_done.value())
                w = weights(1)[0][:, 0:1536].rearrange("p (k n) -> p k n", k=2)
                for m in range(2):
                    for a, b in ((0, 512), (512, 768)):
                        pe.wait_ge(v_free, v_done.value(back=3))
                        bank = v_bank()
                        for k in range(2):
                            inst = pe.matmul(bank[:, 0:b - a], cqT[:, k, P * m:P * m + P], w[:, k, a:b], start=k == 0, stop=k == 1)
                        inst.then_inc(used if m and a else mm_v, 1)
                for m in range(2):
                    b = blocks(rows[:, m, 0:768], MLA_D)
                    turn([b[0:4], b[4:8]])
                w = weights(1)[0][:, 0:1024]
                for m in range(2):
                    for j in range(2):
                        pe.wait_ge(v_free, v_done.value(back=3))
                        bank = v_bank()
                        inst = pe.matmul(bank, cqT[:, 2, P * m:P * m + P], w[:, 512 * j:512 * j + 512], start=True, stop=True)
                        inst.then_inc(used if m and j else mm_v, 1)
                for m in range(2):
                    b = blocks(rows[:, 2 + m, 0:768], MLA_D)
                    turn([b[0:4], b[4:8]])

            def compress():
                for s in range(2):
                    pe.wait_ge(rows_ready, rws.next())
                    w = weights(2)
                    pe.wait_ge(a_free, a_done.value(back=3))
                    bank = a_bank()
                    for c in range(16):
                        inst = pe.matmul(bank[0:30, 0:256], XB[:, s, c].rearrange("p g i -> p (g i)"),
                                         w[c // 8].rearrange("p (c n) -> p c n", c=8)[:, c % 8, :], start=c == 0, stop=c == 15)
                        if c % 8 == 7:
                            inst.then_inc(used, 1)
                pe.wait_ge(a_free, a_done.value())
                pe.wait_ge(v_free, v_done.value(back=3))
                bank = v_bank()
                for s in range(2):
                    for j in range(2):
                        at = 32 * (2 * s + j)
                        inst = pe.transpose(bank[:, at:at + 30], hid[0:30, s, P * j:P * j + P], ident[0:30, 0:30])
                inst.then_inc(mm_v, 1)
                pe.wait_ge(v_free, v_done.value())
                pe.wait_ge(v_free, v_done.value(back=3))
                bank = v_bank()
                k2 = pa("cmp_w2k", at=256 * layer[0], width=256).rearrange("p (j n) -> p j n", j=2)
                v2 = pa("cmp_w2v", at=P * layer[0], width=P).rearrange("p (j n) -> p j n", j=2)
                for j in range(2):
                    pe.matmul(bank[:, 0:30], k2[:, j, :], hidT[:, j, 0:30], start=j == 0, stop=j == 1)
                for j in range(2):
                    inst = pe.matmul(bank[:, 64:128], hv[:, j].rearrange("p h n -> p (h n)"), v2[:, j, :], start=j == 0, stop=j == 1)
                inst.then_inc(mm_v, 1)
                layer[0] += 1

            layer = [0]

            def mlp():
                pe.wait_ge(v_free, v_done.value())
                pe.wait_ge(a_free, a_done.value())
                for c in range(8):
                    w = k512(weights(2))
                    for b in range(2):
                        if b:
                            pe.wait_ge(v_free, v_done.value(back=3))
                            bank = v_bank()
                        else:
                            pe.wait_ge(a_free, a_done.value(back=3))
                            bank = a_bank()
                        for f in range(2):
                            at = P * (2 * b + f)
                            for k in range(KB):
                                inst = pe.matmul(bank[:, SEQ * f:SEQ * f + SEQ], w[k][:, at:at + P], hT[:, k, 0:SEQ],
                                                 start=k == 0, stop=k == KB - 1)
                                if b and f and k == 3:
                                    inst.then_inc(used, 1)
                        inst.then_inc(used if b else mm_a, 1)
                pe.wait_ge(v_free, v_done.value())
                pe.wait_ge(a_free, a_done.value())
                banks = [v_bank() for _ in range(4)]
                for c in range(16):
                    w = weights(1)[0].rearrange("p (k n) -> p k n", k=2)
                    for f in range(2):
                        for m in range(2):
                            for h in range(2):
                                inst = pe.matmul(banks[2 * m + h], aT[:, 2 * c + f, P * m:P * m + P], w[:, f, 512 * h:512 * h + 512],
                                                 start=c == 0 and f == 0, stop=c == 15 and f == 1)
                                if f and m and h:
                                    inst.then_inc(used, 1)
                                elif f and c == 15:
                                    inst.then_inc(mm_v, 1)

            all4 = [0, 1, 2, 3]
            mod(0)
            norm(4)
            heads(3, lambda c: all4, turn_ab)
            attention(groups_ab())
            output(all4, 0)
            moe(0)
            mod(1)
            norm(4)
            heads(6, lambda c: [2, 3] if c < 2 else all4, turn_c)
            attention(groups_c())
            output([2, 3], 2)
            moe(1)
            for l in range(DEPTH):
                norm(2)
                project2()
                compress()
                attention(groups_2())
                output([2, 3], 2)
                norm(2)
                mlp()

        @block.sync
        def _(sp):
            sp.dma_start(X[:, 2:4, :], t["x"][0].rearrange("(t p) n -> p t n", p=P)).then_inc(x_in, 16)
            sp.dma_start(X[:, 0:2, :], t["ctx"][0].rearrange("(t p) n -> p t n", p=P)).then_inc(x_in, 16)
            freed = Tally(used)
            count = [0]

            def load(src):
                slot = count[0] % RING
                if count[0] >= RING:
                    freed.n = count[0] - RING + 1
                    sp.wait_ge(used, freed.value())
                dst = ring[:, slot, 0:src.shape[1] * src.shape[2]].rearrange("p (k n) -> p k n", k=src.shape[1])
                sp.dma_start(dst, src).then_inc(loaded[slot], 16)
                count[0] += 1

            def matrix(w, cols):
                for c in range(cols):
                    for src in cols512(w, c):
                        load(src)

            def experts(l):
                before = count[0]
                with sp.Fori(0, PAIRS) as i:
                    freed.laps = [(i, 12)]
                    for j in range(12):
                        e = j % 2
                        if j < 8:
                            src = t["w1" if j < 4 else "w3"][l, bass.ds(2 * i + e, 1), 512 * (j // 2 % 2):512 * (j // 2 % 2) + 512, :]
                            src = src.rearrange("o (k p) n -> p (o k) n", p=P)
                        else:
                            m = (j - 8) // 2
                            src = t["w2"][l, bass.ds(2 * i + e, 1), 256 * m:256 * m + 256, :]
                            src = src.rearrange("o (k p) n -> p (o k) n", p=P)
                        load(src)
                    freed.laps = []
                count[0] = before + 12 * PAIRS
                nt = 4 - 2 * l
                free = Tally(late[l]["free"])
                sp.wait_ge(rounds_ready, l + 1)
                rounds = sp.value_load(late_rounds[0:1, 0:1], min_val=0, max_val=nt)
                free.n = 1
                with laps(sp, nt, {free: EXPERTS}) as r:
                    with sp.If(rounds > r):
                        freed.n = count[0]
                        sp.wait_ge(used, freed.value())
                        with laps(sp, EXPERTS, {free: 1}) as e:
                            sp.wait_ge(late[l]["free"], free.value())
                            for j in range(6):
                                if j < 4:
                                    src = t["w1" if j < 2 else "w3"][l, bass.ds(e, 1), 512 * (j % 2):512 * (j % 2) + 512, :]
                                else:
                                    src = t["w2"][l, bass.ds(e, 1), 256 * (j - 4):256 * (j - 4) + 256, :]
                                dst = ring[:, j, :].rearrange("p (k n) -> p k n", k=4 if j < 4 else 2)
                                sp.dma_start(dst, src.rearrange("o (k p) n -> p (o k) n", p=P)).then_inc(late[l]["loaded"], 16)
                            free.n += 1
                    sp.end_ifs()
                sp.wait_ge(late[l]["free"], rounds * EXPERTS + 1)

            def project2(l):
                for c in range(4):
                    n = min(512, IN2 - 512 * c)
                    for h in range(2):
                        load(t["w_in_2"][l, 512 * h:512 * h + 512, 512 * c:512 * c + n].rearrange("(k p) n -> p k n", p=P))
                load(t["w_q_up_2"][l].rearrange("(k p) n -> p k n", p=P))
                load(t["w_kv_up_2"][l].rearrange("(k p) n -> p k n", p=P))

            def compress(l):
                for w in ("cmp_w1_k_2", "cmp_w1_v_2"):
                    for h in range(2):
                        load(t[w][l, 1024 * h:1024 * h + 1024, :].rearrange("(k p) n -> p k n", p=P))

            def mlp(l):
                matrix(t["w_ff1_2"][l], 8)
                for c in range(16):
                    load(rows256(t["w_ff2_2"][l], c))

            matrix(t["w_mod"][0], 12)
            matrix(t["w_in_ab"][0], 3)
            matrix(t["w_out_ab"][0], 2)
            experts(0)
            matrix(t["w_mod"][1], 12)
            matrix(t["w_in_c"][0], 6)
            matrix(t["w_out_c"][0], 2)
            experts(1)
            for l in range(DEPTH):
                project2(l)
                compress(l)
                matrix(t["w_out_2"][l], 2)
                mlp(l)
            sp.wait_ge(x_ready, 8)
            sp.dma_start(arena[:, 0:D], t["final_norm_2"].rearrange("(a n) -> a n", a=1).to_broadcast([P, D])).then_inc(final_in, 16)
            for m in range(2):
                sp.wait_ge(x_ready, 9 + m)
                sp.dma_start(t["out"][0, P * m:P * m + P, :], rows[:, m, :]).then_inc(out_done, 16)
            sp.wait_ge(out_done, 32)



def lay_out(inputs):
    g = {k: np.asarray(v) for k, v in inputs.items()}

    def by_feature(v):
        v = v.reshape(-1, P)
        return v.T

    def everywhere(v):
        return np.broadcast_to(v.reshape(1, -1), (P, v.size))

    def blocks(w):
        w = w.reshape(-1, P, w.shape[-1])
        return w.transpose(1, 0, 2).reshape(P, -1)

    cc = np.stack([g["c"][0], g["c_ctx"]], -1)
    heads = np.concatenate([g[n][0] for n in ("qn_a", "kn_a", "qn_b", "kn_b", "qn_c", "kn_c")])
    v = {
        "c": blocks(cc), "norm_mix": by_feature(g["norm_mix"]), "norm_ffn": by_feature(g["norm_ffn"]),
        "head_gain": everywhere(heads), "sink": everywhere(g["sink_a"]), "lam": everywhere(g["lam_c"]),
        "subln": everywhere(g["subln_c"]),
        "w_route": blocks(np.concatenate([g["w_group"], g["w_expert"]], -1)),
        "b_route": everywhere(np.concatenate([g["b_group"], g["b_expert"]], -1)),
        "attn_norm": by_feature(g["attn_norm_2"]), "q_norm": by_feature(g["mla_q_norm_2"]),
        "kv_norm": by_feature(g["mla_kv_norm_2"]),
        "mix_norm": by_feature(np.concatenate([g["nsa_out_norm_2"], g["mla_out_norm_2"]], -1)),
        "mlp_norm": by_feature(g["mlp_norm_2"]),
        "pos_k": by_feature(g["cmp_pos_k_2"]), "pos_v": by_feature(g["cmp_pos_v_2"]),
        "cmp_w2k": blocks(np.concatenate([g["cmp_w2_k_2"]] * 2, -1)), "cmp_w2v": blocks(g["cmp_w2_v_2"]),
    }
    for n, w in PARAMS:
        assert v[n].shape == (P, w), (n, v[n].shape, w)
    return np.ascontiguousarray(np.concatenate([v[n] for n, _ in PARAMS], 1))


WEIGHTS = ["x", "ctx", "w_mod", "b_mod", "w_in_ab", "w_out_ab", "w_in_c", "w_out_c", "w1", "w3", "w2",
           "w_in_2", "w_q_up_2", "w_kv_up_2", "cmp_w1_k_2", "cmp_w1_v_2", "w_out_2", "w_ff1_2", "w_ff2_2", "final_norm_2"]


def arrays_of(inputs):
    arrays = {n: np.ascontiguousarray(inputs[n]) for n in WEIGHTS}
    arrays["params"] = lay_out(inputs)
    arrays["consts"] = np.ascontiguousarray(constants())
    return arrays


def kernel(**inputs):
    import concourse.bacc as bacc
    from concourse.bass_utils import run_bass_kernel_spmd

    nc = bacc.Bacc("TRN2", target_bir_lowering=False, num_devices=1)
    arrays = arrays_of(inputs)
    t = {n: nc.dram_tensor("in_" + n, a.shape, mybir.dt.from_np(a.dtype), kind="ExternalInput").ap() for n, a in arrays.items()}
    t["out"] = nc.dram_tensor("out", (1, SEQ, D), mybir.dt.float32, kind="ExternalOutput").ap()
    build(nc, t)
    r = run_bass_kernel_spmd(nc, [{"in_" + n: a for n, a in arrays.items()}], core_ids=[0])
    return r.results[0]["out"]
```

```python
from contextlib import ExitStack, contextmanager

import numpy as np

import concourse.bass as bass
from concourse import mybir

P = 128
D = 1024
KB = D // P
DEPTH = 2
SEQ = 256
CTX = 256
TOK = SEQ + CTX
HD = 64
NEG = -1e30
EPS = 1e-6
GROUPS, PER_GROUP, EXPERTS = 4, 8, 32
ROUTES = GROUPS + EXPERTS
SLOTS = 64
PAIRS = EXPERTS // 2
DFF = 4096
MOD_BLOCKS = 6 * D // 512
SCALE = HD ** -0.5
MLA_D = 96
MLA_SCALE = MLA_D ** -0.5
LAM_INIT = 0.8 - 0.6 * float(np.exp(-0.3))
IN2 = 1720
IN2_PAD = 2048
Q2, KC2, VC2, KS2, VS2, KW2, VW2, GA2, CQ2, CKV2, KR2 = 0, 512, 640, 768, 896, 1024, 1152, 1280, 1304, 1560, 1688
RING = 6
CHUNK = 4 * 512

PARAMS = [
    ("c", 2 * KB), ("norm_mix", 2 * KB), ("norm_ffn", 2 * KB), ("head_gain", 6 * HD), ("sink", 8), ("lam", 4 * HD),
    ("subln", 1), ("w_route", 2 * KB * ROUTES), ("b_route", 2 * ROUTES), ("attn_norm", 2 * KB), ("q_norm", 4),
    ("kv_norm", 2), ("b_mod", 2 * 6 * KB), ("mix_norm", 2 * KB), ("mlp_norm", 2 * KB), ("pos_k", 32), ("pos_v", 32),
    ("cmp_w2k", 2 * 2 * 128), ("cmp_w2v", 2 * 2 * 64),
]
CONSTS = [
    ("ident", 128), ("cos_ax", 128), ("sin_ax", 128), ("cos_a", 128), ("sin_a", 128), ("cos_b", 64), ("sin_b", 64),
    ("window", 512), ("causal", 128), ("cmp_add", 32), ("cmp_keep", 32), ("before", 128), ("ones", 128),
    ("slot", P), ("rank_e", EXPERTS), ("rank_g", GROUPS), ("fold", 2), ("block_diag", 8),
]


def offsets(spec):
    at, out = 0, {}
    for name, width in spec:
        out[name] = (at, width)
        at += width
    return out, at


def constants():
    c = {}
    part = np.arange(P)
    c["ident"] = np.eye(P)

    def rope(cos, sin):
        cc, ss = np.concatenate([cos, cos], -1), np.concatenate([-sin, sin], -1)
        return [t.reshape(2, P, -1).transpose(1, 0, 2).reshape(P, -1) for t in (cc, ss)]

    half = HD // 2
    inv = (np.float32(10000.0) ** (-np.arange(0, half, 2, dtype=np.float32) / half)).astype(np.float32)
    rows, cols = np.repeat(np.arange(4, dtype=np.float32), 64), np.tile(np.arange(64, dtype=np.float32), 4)
    ang = np.concatenate([rows[:, None] * inv, cols[:, None] * inv], -1)
    c["cos_ax"], c["sin_ax"] = rope(np.cos(ang), np.sin(ang))
    for name, dim in (("a", HD), ("b", 32)):
        inv = (np.float32(1.0) / (np.float32(10000.0) ** (np.arange(0, dim, 2, dtype=np.float32) / dim))).astype(np.float32)
        ang = np.arange(SEQ, dtype=np.float32)[:, None] * inv[None, :]
        c["cos_" + name], c["sin_" + name] = rope(np.cos(ang), np.sin(ang))
    q = np.arange(SEQ).reshape(2, P)
    k = np.arange(SEQ)
    c["window"] = np.concatenate([np.where(np.abs(k[None] - q[t][:, None]) <= 128, 0.0, NEG) for t in range(2)], 1)
    c["causal"] = np.where(part[None] <= part[:, None], 0.0, NEG)
    end = np.where(np.arange(16) < 15, np.arange(16) * 16 + 31, 1 << 20)
    keep = np.concatenate([(end[None] <= q[t][:, None]) for t in range(2)], 1)
    c["cmp_add"], c["cmp_keep"] = np.where(keep, 0.0, NEG), keep * 1.0
    c["before"] = (part[:, None] < part[None]) * 1.0
    c["ones"] = np.ones((P, P))
    c["slot"] = np.broadcast_to(np.arange(P), (P, P))
    c["rank_e"] = np.broadcast_to(EXPERTS - np.arange(EXPERTS), (P, EXPERTS))
    c["rank_g"] = np.broadcast_to(GROUPS - np.arange(GROUPS), (P, GROUPS))
    c["fold"] = np.stack([part % 32 == r for r in range(2)], 1) * 1.0
    c["block_diag"] = (part[:, None] // 16 == np.arange(8)[None]) * 1.0
    return np.concatenate([c[n].astype(np.float32).reshape(P, w) for n, w in CONSTS], 1)


class Tally:

    def __init__(self, sem, unit=1):
        self.sem, self.unit, self.n, self.laps = sem, unit, 0, []

    def value(self, back=0):
        value = (self.n - back) * self.unit
        if not self.laps:
            return max(value, 0)
        for i, per in self.laps:
            if per:
                value = value + i * (per * self.unit)
        return value

    def next(self, more=1):
        self.n += more
        return self.value()


@contextmanager
def laps(eng, trips, per):
    with eng.Fori(0, trips) as i:
        start = {t: t.n for t in per}
        for t, m in per.items():
            t.laps.append((i, m))
        yield i
        for t, m in per.items():
            assert t.n - start[t] == m, (t.sem, t.n - start[t], m)
            t.laps.pop()
    for t, m in per.items():
        t.n = start[t] + m * trips


def build(nc, t):
    f32, i32 = mybir.dt.float32, mybir.dt.int32
    ALU, ACT, AX = mybir.AluOpType, mybir.ActivationFunctionType, mybir.AxisListType.X
    par_at, par_w = offsets(PARAMS)
    con_at, con_w = offsets(CONSTS)

    ctx = ExitStack()
    with ctx:
        def sb(name, shape, dt=f32):
            return ctx.enter_context(nc.sbuf_tensor(name, shape, dt))

        def sem(name):
            return ctx.enter_context(nc.semaphore(name))

        par, con = sb("par", [P, par_w]), sb("con", [P, con_w])
        ring = sb("ring", [P, RING, CHUNK])
        X = sb("X", [P, 4, D])
        hT = sb("hT", [P, KB, TOK])
        gate = sb("gate", [P, 2, 2, D])
        rows = sb("rows", [P, 4, D])
        arena = sb("arena", [P, 18432])
        psum = ctx.enter_context(nc.psum_tensor("psum", [P, 8, 512], f32))

        def pa(name, at=0, width=None):
            o, w = par_at[name]
            return par[:, o + at:o + at + (width or w - at)]

        def co(name, at=0, width=None):
            o, w = con_at[name]
            return con[:, o + at:o + at + (width or w - at)]

        ident = co("ident")
        cpad = sb("cpad", [P, KB, 32])
        modT = sb("modT", [P, 48, 2])
        scale1 = sb("scale1", [P, 2, KB, 2])
        gain = sb("gain", [P, 2, KB, 2])
        gain8 = sb("gain8", [P, 6, HD])
        nsink = sb("nsink", [P, 8])
        lam = sb("lam", [P, 8])
        sub8 = sb("sub8", [P, 1])
        sumsq = sb("sumsq", [P, 3, 8])
        rstd = sb("rstd", [P, 3, 8])
        scaler = sb("scaler", [P, 4, P])
        mhalf = sb("mhalf", [P, 8])
        nbias, psums, esink, rden, mx = (sb(n, [P, 4, 8]) for n in ("nbias", "psums", "esink", "rden", "mx"))

        mrow = arena[:, 9216:10240].rearrange("p (b n) -> p b n", b=2)
        qT = arena[:, 0:4096].rearrange("p (h n) -> p h n", h=8)
        kP = arena[:, 4096:8192].rearrange("p (g s n) -> p g s n", g=4, s=2)
        vA = arena[:, 8192:9216].rearrange("p (t n) -> p t n", t=4)
        probs = arena[:, 12288:14336].rearrange("p (b n) -> p b n", b=2)
        probsT = arena[:, 14336:16384].rearrange("p (b n) -> p b n", b=2)
        oA = rows
        qP = arena[:, 0:4096].rearrange("p (h s n) -> p h s n", h=8, s=2)
        kT = arena[:, 4096:8192].rearrange("p (h n) -> p h n", h=8)
        vC = arena[:, 8192:12288].rearrange("p (t n) -> p t n", t=4)
        R = [rows[:, 0, 0:512], rows[:, 0, 512:1024]]
        SQ, TX, TA, TB = rows[:, 1, 0:512], rows[:, 1, 512:1024], rows[:, 2, 0:512], rows[:, 2, 512:1024]
        KDUP = [rows[:, 3, 0:256], rows[:, 3, 256:512]]
        TMP = rows[:, 3, 512:1024]
        hrow = arena[:, 0:4096].rearrange("p (t n) -> p t n", t=4)
        facc = arena[:, 4096:8192].rearrange("p (t n) -> p t n", t=4)
        xgT = arena[:, 8192:10240].rearrange("p (b k n) -> p b k n", b=2, k=KB)
        pick = arena[:, 10240:11264].rearrange("p (b t n) -> p b t n", b=2, t=4)
        share = arena[:, 11264:12288].rearrange("p (b t n) -> p b t n", b=2, t=4)
        shareT = arena[:, 12288:12800].rearrange("p (t n) -> p t n", t=4)
        siluG, act_ = arena[:, 12800:13312], arena[:, 13312:13824]
        actT = arena[:, 13824:14336].rearrange("p (f n) -> p f n", f=4)
        ySlot = arena[:, 14336:15360]
        route = arena[:, 15360:18432].rearrange("p (a t e) -> p a t e", a=16, t=4)
        mark = sb("mark", [P, 2])
        late_rounds = sb("late_rounds", [1, 1], i32)
        PR = arena[:, 0:2 * IN2].rearrange("p (t n) -> p t n", t=2)
        qT2 = arena[:, 3584:4608].rearrange("p (h n) -> p h n", h=4)
        kSW = arena[:, 4608:6656].rearrange("p (w g s n) -> p w g s n", w=2, g=2, s=2)
        kvT2 = arena[:, 6656:7168].rearrange("p (b n) -> p b n", b=4)
        XB = arena[:, 7168:8128].rearrange("p (w c g i) -> p w c g i", w=2, c=16, g=2)
        hid = arena[:, 8192:8704].rearrange("p (w n) -> p w n", w=2)
        hidT = arena[:, 8704:8832].rearrange("p (b n) -> p b n", b=4)
        vBD = arena[:, 9152:9664].rearrange("p (h n) -> p h n", h=8)
        cqT = arena[:, 9664:10432].rearrange("p (b n) -> p b n", b=3)
        KD = [arena[:, 10496 + 768 * m:11264 + 768 * m].rearrange("p (b s n) -> p b s n", b=6, s=2) for m in range(2)]
        KWD = [arena[:, 12032 + 256 * m:12288 + 256 * m].rearrange("p (b s n) -> p b s n", b=2, s=2) for m in range(2)]
        CQ = [arena[:, 12544 + 384 * m:12928 + 384 * m] for m in range(2)]
        qM = arena[:, 16384:18432].rearrange("p (h n) -> p h n", h=8)
        spare = gate[:, :, :, :].rearrange("p a b n -> p (a b n)")
        kM = spare[:, 0:2048].rearrange("p (h n) -> p h n", h=8)
        VM = spare[:, 2048:3072].rearrange("p (t n) -> p t n", t=2)
        kC = spare[:, 3072:3136].rearrange("p (g s n) -> p g s n", g=2, s=2)
        hv = spare[:, 3136:3392].rearrange("p (j h n) -> p j h n", j=2, h=8)
        gs = spare[:, 3392:3440].rearrange("p (t n) -> p t n", t=2)
        kpe = spare[:, 3440:3504].rearrange("p (t n) -> p t n", t=2)
        aT = arena[:, 8192:16384].rearrange("p (f n) -> p f n", f=32)
        g2 = sb("g2", [P, 56])
        G_ATTN, G_Q, G_KV, G_MIX, G_MLP = 0, 16, 20, 22, 38

        mod_w = [hT[:, 4 * h:4 * h + 4, :] for h in range(2)]
        mod_sums = rows[:, 1, 0:512]
        gate_diag = [arena[:, o:o + 2048].rearrange("p (w k n) -> p w k n", w=2, k=KB) for o in (10240, 16384)]

        params_in, consts_in, x_in, out_done = (sem(n) for n in ("params_in", "consts_in", "x_in", "out_done"))
        zeroed = sem("zeroed")
        loaded = [sem(f"loaded{i}") for i in range(RING)]
        used = sem("used")
        mm_v, v_free = sem("mm_v"), sem("v_free")
        mm_a, a_free = sem("mm_a"), sem("a_free")
        v_step, a_step, p_step = sem("v_step"), sem("a_step"), sem("p_step")
        c_ready, mod_row = sem("c_ready"), sem("mod_row")
        x_tile = sem("x_tile")
        x_ready, ss_ready, rs_done, xn_ready, gain_ready = (sem(n) for n in ("x_ready", "ss_ready", "rs_done", "xn_ready", "gain_ready"))
        hs_ready, hs_done, rows_ready = sem("hs_ready"), sem("hs_done"), sem("rows_ready")
        att_s, att_m, att_e, att_t, att_tv, att_ta, att_pv, att_o = (
            sem(n) for n in ("att_s", "att_m", "att_e", "att_t", "att_tv", "att_ta", "att_pv", "att_o"))
        routed, exp_ready, chosen, pick_ready, sil_ready = (
            sem(n) for n in ("routed", "exp_ready", "chosen", "pick_ready", "sil_ready"))
        final_in, c_in = sem("final_in"), sem("c_in")
        mod_loaded, mod_free, mod_product, mod_taken = (sem(n) for n in ("mod_loaded", "mod_free", "mod_product", "mod_taken"))
        diag_ready = sem("diag_ready")
        rounds_ready = sem("rounds_ready")
        late = [{n: sem(f"late_{n}{l}") for n in ("loaded", "free", "product", "v", "a", "step", "round", "added")} for l in range(2)]

        def row(src, off, n):
            return src[off:off + n]

        def cols512(w, c):
            return [w[512 * h:512 * h + 512, 512 * c:512 * c + 512].rearrange("(k p) n -> p k n", p=P) for h in range(2)]

        def rows256(w, c):
            return w[256 * c:256 * c + 256, :].rearrange("(k p) n -> p k n", p=P)

        def groups_ab():
            out = []
            for tile in (2, 3):
                for p in range(8):
                    out.append(dict(tile=tile, nk=512, heads=[2 * p, 2 * p + 1]))
            for tile in (0, 1):
                for p in range(4):
                    out.append(dict(tile=tile, nk=256, heads=list(range(4 * p, 4 * p + 4))))
            for g in out:
                tile, nk = g["tile"], g["nk"]
                g["scores"] = [(qT[:, h // 2, P * tile:P * tile + P], kP[:, h // 4, h % 2, 0:nk]) for h in g["heads"]]
                local = tile >= 2 and g["heads"][0] < 8
                g["mask"] = (256, co("window", 256 * (tile - 2), 256)) if local else None
                g["sink"] = g["heads"][0] if g["heads"][0] < 8 else None
                g["pv"] = [[vA[:, b, HD * (h // 4):HD * (h // 4) + HD] for b in range(nk // P)] for h in g["heads"]]
                g["dv"], g["out"] = HD, oA[:, tile, HD * g["heads"][0]:HD * (g["heads"][-1] + 1)]
                g["scale"] = SCALE
            return out

        def groups_c():
            out = []
            for tile in (0, 1):
                for h in range(8):
                    out.append(dict(
                        nk=512, heads=[h, h], mask=None, sink=None, dv=P, scale=SCALE, diff=True,
                        scores=[(qP[:, h, s, P * tile:P * tile + P], kT[:, h, :]) for s in range(2)],
                        pv=[[vC[:, b, P * h:P * h + P] for b in range(4)]] * 2,
                        out=oA[:, tile, P * h:P * h + P]))
            return out

        def groups_2():
            out = []
            for m in (0, 1):
                nk = P * (m + 1)
                q = [qT2[:, h // 2, P * m:P * m + P] for h in range(8)]
                out.append(dict(nk=16, heads=list(range(8)), mask=(0, co("cmp_add", at=16 * m, width=16)), sink=None, dv=HD, scale=SCALE,
                                scores=[(q[h], kC[:, h // 4, h % 2, :]) for h in range(8)], pv_all=vBD,
                                gate=(m, 0), keep=co("cmp_keep", at=16 * m, width=1), out=oA[:, m, 0:512], first=True))
                for kind in ("sel", "win", "mla"):
                    w = 0 if kind == "sel" else 1
                    for h0 in range(0, 8, 1024 // nk):
                        hs = list(range(h0, h0 + 1024 // nk))[:8]
                        g = dict(nk=nk, heads=hs, mask=(P * m, co("causal")), sink=None, dv=HD)
                        if kind == "mla":
                            g.update(scale=MLA_SCALE, out=oA[:, m, 512 + HD * h0:512 + HD * (hs[-1] + 1)],
                                     scores=[(qM[0:MLA_D, h, P * m:P * m + P], kM[0:MLA_D, h, 0:nk]) for h in hs],
                                     pv=[[VM[:, b, HD * h:HD * h + HD] for b in range(m + 1)] for h in hs])
                        else:
                            v0 = VW2 if w else VS2
                            g.update(scale=SCALE, out=oA[:, m, HD * h0:HD * (hs[-1] + 1)], gate=(m, 1 + w), first=False,
                                     scores=[(q[h], kSW[:, w, h // 4, h % 2, 0:nk]) for h in hs],
                                     pv=[[PR[:, b, v0 + HD * (h // 4):v0 + HD * (h // 4) + HD] for b in range(m + 1)] for h in hs])
                        out.append(g)
            return out

        AB = [dict(norm=[(0, 8, 0)], v=None, q=(0, 4, 0), k=None),
              dict(norm=[(0, 2, 1), (4, 4, 2)], v=(128, 128, 0), q=(256, 2, 4), k=(0, 0)),
              dict(norm=[(0, 4, 2), (4, 2, 3)], v=(384, 128, 128), q=(0, 2, 6), k=(256, 2))]

        def width(g):
            return g["nk"] * len(g["heads"])

        def flat(bank):
            return psum[:, bank:bank + 2, :].rearrange("p a n -> p (a n)")

        block = ctx.enter_context(nc.Block())

        @block.gpsimd
        def _(pool):
            pool.dma_start(con[:, :], t["consts"]).then_inc(consts_in, 16)
            pool.memset(cpad[:, :, :], 0.0).then_inc(zeroed, 1)
            pool.memset(kP, 0.0).then_inc(zeroed, 1)
            pool.memset(mhalf[:, :], -0.5).then_inc(p_step, 1)
            ss, hs, step = Tally(ss_ready), Tally(hs_ready), Tally(p_step)
            step.n = 1

            def rsqrt(out, total, n):
                pool.tensor_scalar(out, total, EPS * n, None, ALU.add).then_inc(p_step, 1)
                pool.wait_ge(p_step, step.next())
                return pool.tensor_tensor(out, out, mhalf[:, 0:out.shape[-1]], ALU.pow)

            def rsqrt_rows(nt):
                pool.wait_ge(ss_ready, ss.next())
                rsqrt(rstd[:, 0, 0:nt], sumsq[:, 0, 0:nt], D).then_inc(rs_done, 1)

            def rsqrt_heads(jobs, n, width=8):
                for j in range(jobs):
                    pool.wait_ge(hs_ready, hs.next())
                    b = 1 + (hs.n - 1) % 2
                    rsqrt(rstd[:, b, 0:width], sumsq[:, b, 0:width], n).then_inc(hs_done, 1)

            def pads2():
                pool.wait_ge(x_ready, 4)
                pool.memset(kSW, 0.0)
                pool.memset(kC, 0.0)
                pool.memset(hv, 0.0).then_inc(zeroed, 1)

            def latents():
                for m in range(2):
                    rsqrt_heads(1, 256, 1)
                    rsqrt_heads(1, P, 1)

            def pads():
                pool.wait_ge(x_ready, 2)
                rsqrt_rows(4)
                pool.memset(qP, 0.0).then_inc(zeroed, 1)

            rsqrt_rows(4)
            rsqrt_heads(12, HD)
            rsqrt_rows(4)
            pads()
            rsqrt_heads(2 * 2 + 2 * 4, HD)
            rsqrt_heads(2, P)
            rsqrt_rows(2)
            for l in range(DEPTH):
                rsqrt_rows(2)
                if not l:
                    pads2()
                latents()
                rsqrt_heads(2, 512, 2)
                rsqrt_rows(2)
            rsqrt_rows(2)

        @block.scalar
        def _(act):
            c_w = par_at["c"][1]
            act.dma_start(par[:, 0:c_w], t["params"][:, 0:c_w]).then_inc(c_in, 16)
            act.dma_start(par[:, c_w:], t["params"][:, c_w:]).then_inc(params_in, 16)
            jobs, chunks = Tally(mm_a), Tally(used)
            exps_in, routing = Tally(att_m), Tally(routed)
            turned = Tally(att_t)
            job = [0]
            own = {}

            def so_far(sem):
                return own.setdefault(sem.name, Tally(sem)).next()

            def next_bank():
                job[0] += 1
                return psum[:, 4 + (job[0] - 1) % 4, :]

            tile_in = Tally(x_tile)

            def squares(tiles):
                for m, tile in enumerate(tiles):
                    act.wait_ge(x_tile, tile_in.next())
                    inst = act.activation(rows[:, m, :], X[:, tile, :], ACT.Square, accum_out=sumsq[:, 0, m:m + 1])
                inst.then_inc(ss_ready, 1)
                act.wait_ge(ss_ready, so_far(ss_ready))

            def start():
                act.wait_ge(c_in, 16)
                act.wait_ge(zeroed, 1)
                act.activation(cpad[:, :, 0:2], pa("c").rearrange("p (k r) -> p k r", r=2), ACT.Silu).then_inc(c_ready, 1)
                act.wait_ge(c_ready, so_far(c_ready))
                act.wait_ge(x_in, 32)
                for m in range(4):
                    inst = act.activation(rows[:, m, :], X[:, m, :], ACT.Square, accum_out=sumsq[:, 0, m:m + 1])
                inst.then_inc(ss_ready, 1)
                act.wait_ge(ss_ready, so_far(ss_ready))

            def gates(l):
                for w in range(2):
                    for r in range(2 - l):
                        for h in range(2):
                            act.wait_ge(mm_a, jobs.next())
                            bank = next_bank()
                            act.activation(gate[:, w, r, 512 * h:512 * h + 512], bank, ACT.Copy).then_inc(a_free, 1)
                            act.wait_ge(a_free, so_far(a_free))

            def norm(n, which, tiles):
                act.wait_ge(gain_ready, n + 1)
                for k in range(1, KB, 2):
                    act.wait_ge(mm_a, jobs.next())
                    bank = next_bank()
                    for a, b, r in [(0, 256, 1), (256, 512, 0)] if len(tiles) == 4 else [(0, 256, 0)]:
                        inst = act.activation(hT[:, k, a:b], bank[:, a:b], ACT.Identity,
                                              bias=modT[:, 24 * which + k, r:r + 1], scale=gain[:, which, k, r:r + 1])
                    inst.then_inc(a_free, 1)
                    act.wait_ge(a_free, so_far(a_free))

            def turned2(g):
                for k in range(1, KB, 2):
                    act.wait_ge(mm_a, jobs.next())
                    bank = next_bank()
                    act.activation(hT[:, k, 0:SEQ], bank[:, 0:SEQ], ACT.Copy, scale=g2[:, g + k:g + k + 1]).then_inc(a_free, 1)
                    act.wait_ge(a_free, so_far(a_free))

            def norm2(n, g):
                squares([2, 3])
                turned2(g)

            def project2(l):
                act.wait_ge(zeroed, 4)

                def halves(bank, which, cols):
                    k = bank[:, 0:256].rearrange("p (g n) -> p g n", g=2)
                    act.activation(kSW[0:64, which, :, 0, cols], k[0:64], ACT.Copy)
                    act.activation(kSW[64:128, which, :, 1, cols], k[64:128], ACT.Copy).then_inc(a_free, 1)
                    act.wait_ge(a_free, so_far(a_free))

                for c in range(4):
                    for m in range(2):
                        cols = slice(P * m, P * m + P)
                        act.wait_ge(mm_a, jobs.next())
                        bank = next_bank()
                        if c == 0:
                            act.activation(qT2[:, :, cols], bank.rearrange("p (h n) -> p h n", h=4), ACT.Copy).then_inc(a_free, 1)
                            act.wait_ge(a_free, so_far(a_free))
                        elif c == 1:
                            src = bank.rearrange("p (b n o) -> p b n o", b=4, o=2)
                            dst = kvT2[:, :, 64 * m:64 * m + 64]
                            act.activation(dst[0:64], src[0:64, :, :, 0], ACT.Copy)
                            act.activation(dst[64:128], src[64:128, :, :, 1], ACT.Copy).then_inc(a_free, 1)
                            act.wait_ge(a_free, so_far(a_free))
                            act.wait_ge(mm_a, jobs.next())
                            bank = next_bank()
                            halves(bank, 0, cols)
                        elif c == 2:
                            halves(bank, 1, cols)
                        else:
                            for b in range(3):
                                g = G_Q + 2 * l + b if b < 2 else G_KV + l
                                inst = act.activation(cqT[:, b, cols], bank[:, P * b:P * b + P], ACT.Copy, scale=g2[:, g:g + 1])
                            inst.then_inc(a_free, 1)
                            act.wait_ge(a_free, so_far(a_free))
                act.wait_ge(routed, routing.next())
                act.activation(gs, PR[:, :, GA2:GA2 + 24], ACT.Exp, scale=-1.0).then_inc(exp_ready, 1)
                act.wait_ge(exp_ready, so_far(exp_ready))
                for dst in (qM, kM):
                    for m in range(2):
                        for j in range(2):
                            act.wait_ge(mm_a, jobs.next())
                            bank = next_bank()
                            act.activation(dst[0:MLA_D, 4 * j:4 * j + 4, P * m:P * m + P],
                                           bank[0:MLA_D, :].rearrange("p (h n) -> p h n", h=4), ACT.Copy).then_inc(a_free, 1)
                            act.wait_ge(a_free, so_far(a_free))

            def compress():
                for w in range(2):
                    act.wait_ge(used, chunks.next(2))
                    bank = next_bank()
                    act.activation(hid[0:30, w, :], bank[0:30, 0:256], ACT.Silu).then_inc(a_free, 1)
                    act.wait_ge(a_free, so_far(a_free))

            def mlp():
                for c in range(8):
                    act.wait_ge(mm_a, jobs.next())
                    bank = next_bank()
                    f = aT[:, 4 * c:4 * c + 2, :]
                    act.activation(f, bank.rearrange("p (f n) -> p f n", f=2), ACT.Relu).then_inc(a_step, 1)
                    act.wait_ge(a_step, so_far(a_step))
                    act.activation(f, f, ACT.Square).then_inc(a_free, 1)
                    act.wait_ge(a_free, so_far(a_free))

            def heads_ab():
                for j in range(12):
                    cols = slice(P * (j % 4), P * (j % 4) + P)
                    b = AB[j // 4]
                    act.wait_ge(mm_a, jobs.next())
                    bank = next_bank()
                    _, nq, q0 = b["q"]
                    inst = act.activation(qT[:, q0:q0 + nq, cols], bank[:, 0:P * nq].rearrange("p (h n) -> p h n", h=nq), ACT.Copy)
                    if b["k"]:
                        g0 = b["k"][1]
                        ks = bank[:, 256:512].rearrange("p (g n) -> p g n", g=2)
                        act.wait_ge(zeroed, 2)
                        act.activation(kP[0:64, g0:g0 + 2, 0, cols], ks[0:64], ACT.Copy)
                        inst = act.activation(kP[64:128, g0:g0 + 2, 1, cols], ks[64:128], ACT.Copy)
                    inst.then_inc(a_free, 1)
                    act.wait_ge(a_free, so_far(a_free))

            def heads_c():
                for c in range(4):
                    for tile in range(4) if c >= 2 else (2, 3):
                        act.wait_ge(mm_a, jobs.next())
                        bank = next_bank().rearrange("p (h n) -> p h n", h=4)
                        if c < 2:
                            cols = slice(P * (tile - 2), P * (tile - 2) + P)
                            act.wait_ge(zeroed, 3)
                            act.activation(qP[0:64, 4 * c:4 * c + 4, 0, cols], bank[0:64], ACT.Copy)
                            act.activation(qP[64:128, 4 * c:4 * c + 4, 1, cols], bank[64:128], ACT.Copy).then_inc(a_free, 1)
                            act.wait_ge(a_free, so_far(a_free))
                        else:
                            act.activation(kT[:, 4 * c - 8:4 * c - 4, P * tile:P * tile + P], bank, ACT.Copy).then_inc(a_free, 1)
                            act.wait_ge(a_free, so_far(a_free))

            def attention(groups):
                def exps(g):
                    act.wait_ge(att_m, exps_in.next())
                    b, nk, heads = (exps_in.n - 1) % 4, g["nk"], len(g["heads"])
                    s = psum[:, 2 * (b % 2):2 * (b % 2) + 2, :].rearrange("p a n -> p (a n)")
                    if g["sink"] is not None:
                        act.activation(esink[:, b, 0:heads], mx[:, b, 0:heads], ACT.Exp)
                    for u in range(heads):
                        inst = act.activation(probs[:, b % 2, nk * u:nk * u + nk], s[:, nk * u:nk * u + nk], ACT.Exp,
                                              bias=nbias[:, b, u:u + 1], scale=g["scale"], accum_out=psums[:, b, u:u + 1])
                    inst.then_inc(att_e, 1)
                    act.wait_ge(att_e, so_far(att_e))

                exps(groups[0])
                for n in range(len(groups)):
                    act.wait_ge(att_t, turned.next())
                    if width(groups[n]) == 1024:
                        act.activation(probsT[:, (turned.n - 1) % 2, 512:1024], psum[:, 5, :], ACT.Copy).then_inc(att_ta, 1)
                        act.wait_ge(att_ta, so_far(att_ta))
                    else:
                        act.activation(mark[:, 1:2], par[:, 0:1], ACT.Copy).then_inc(att_ta, 1)
                        act.wait_ge(att_ta, so_far(att_ta))
                    if n + 1 < len(groups):
                        exps(groups[n + 1])

            def lam_exp():
                act.wait_ge(routed, routing.next())
                act.activation(lam[:, 2:4], lam[:, 0:2], ACT.Exp).then_inc(exp_ready, 1)
                act.wait_ge(exp_ready, so_far(exp_ready))

            def outputs_T(nt, gains=None):
                for k in range(1, KB, 2):
                    act.wait_ge(mm_a, jobs.next())
                    bank = next_bank()
                    scale = 1.0 if gains is None else gains[:, 0:1]
                    act.activation(hT[:, k, 0:P * nt], bank[:, 0:P * nt], ACT.Copy, scale=scale).then_inc(a_free, 1)
                    act.wait_ge(a_free, so_far(a_free))

            def moe(l):
                nt = 4 - 2 * l
                squares([0, 1, 2, 3][2 * l:])
                norm(2 * l + 1, 1, [0, 1, 2, 3][2 * l:])
                act.wait_ge(routed, routing.next())
                for tile in range(nt):
                    inst = act.activation(route[:, 1, tile, 0:4], route[:, 0, tile, 0:4], ACT.Exp,
                                          bias=route[:, 2, tile, 0:1], accum_out=route[:, 2, tile, 1:2])
                inst.then_inc(exp_ready, 1)
                act.wait_ge(exp_ready, so_far(exp_ready))
                for tile in range(nt):
                    for h in range(2):
                        act.wait_ge(mm_a, jobs.next())
                        bank = next_bank()
                        act.activation(hrow[:, tile, 512 * h:512 * h + 512], bank, ACT.Copy).then_inc(a_free, 1)
                        act.wait_ge(a_free, so_far(a_free))
                act.wait_ge(routed, routing.next())
                act.activation(route[:, 2, 0:nt, 4:5], route[:, 2, 0:nt, 3:4], ACT.Exp).then_inc(exp_ready, 1)
                act.wait_ge(exp_ready, so_far(exp_ready))

                def gathered(b):
                    for h in range(2):
                        act.wait_ge(mm_a, jobs.next())
                        act.activation(xgT[:, b, 4 * h:4 * h + 4, :], psum[:, 5 + h, :].rearrange("p (k n) -> p k n", k=4),
                                  ACT.Copy).then_inc(a_free, 1)
                        act.wait_ge(a_free, so_far(a_free))

                gathered(0)
                own.setdefault(sil_ready.name, Tally(sil_ready))
                with laps(act, PAIRS // 2, {jobs: 6, chunks: 24, own[sil_ready.name]: 2, own[a_free.name]: 6}):
                    for b in range(2):
                        act.wait_ge(used, chunks.next(4))
                        act.activation(siluG, psum[:, 4, :], ACT.Silu).then_inc(sil_ready, 1)
                        act.wait_ge(sil_ready, so_far(sil_ready))
                        gathered(1 - b)
                        act.wait_ge(mm_a, jobs.next())
                        act.activation(ySlot[:, 0:512], psum[:, 7, :], ACT.Copy).then_inc(a_free, 1)
                        act.wait_ge(a_free, so_far(a_free))
                        chunks.n += 8

                s = late[l]
                product, mine = Tally(s["product"]), Tally(s["a"])
                own[s["a"].name] = mine
                act.wait_ge(rounds_ready, l + 1)
                count = act.value_load(late_rounds[0:1, 0:1], min_val=0, max_val=nt)
                with laps(act, nt, {product: 5 * EXPERTS, mine: 3 * EXPERTS}) as r:
                    with act.If(count > r):
                        with laps(act, EXPERTS, {product: 5, mine: 3}):
                            act.wait_ge(s["product"], product.next())
                            act.activation(xgT[:, 0], psum[:, 5:7, :].rearrange("p a (k n) -> p (a k) n", k=4), ACT.Copy).then_inc(s["a"], 1)
                            act.wait_ge(s["a"], so_far(s["a"]))
                            act.wait_ge(s["product"], product.next())
                            act.activation(siluG, psum[:, 4, :], ACT.Silu).then_inc(s["a"], 1)
                            act.wait_ge(s["a"], so_far(s["a"]))
                            act.wait_ge(s["product"], product.next(2))
                            act.activation(ySlot[:, 0:512], psum[:, 7, :], ACT.Copy).then_inc(s["a"], 1)
                            act.wait_ge(s["a"], so_far(s["a"]))
                            product.n += 1
                    act.end_ifs()

            start()
            lam_exp()
            norm(0, 0, [0, 1, 2, 3])
            heads_ab()
            attention(groups_ab())
            chunks.n += 24 + 6
            outputs_T(4)
            gates(0)
            chunks.n += 4
            moe(0)
            squares([0, 1, 2, 3])
            chunks.n += 8
            norm(2, 0, [0, 1, 2, 3])
            act.wait_ge(x_ready, 2)
            gates(1)
            heads_c()
            chunks.n += 12
            attention(groups_c())
            outputs_T(2, sub8)
            chunks.n += 4
            moe(1)
            for l in range(DEPTH):
                norm2(4 + 2 * l, G_ATTN + KB * l)
                project2(l)
                chunks.n += 10
                compress()
                attention(groups_2())
                turned2(G_MIX + KB * l)
                chunks.n += 4
                norm2(5 + 2 * l, G_MLP + KB * l)
                mlp()
                chunks.n += 32
            squares([2, 3])

        @block.vector
        def _(dve):
            jobs, chunks = Tally(mm_v), Tally(used)
            heads_done, norms_done = Tally(hs_done), Tally(rs_done)
            scored, expd, turned, valued = Tally(att_s), Tally(att_e), Tally(att_t), Tally(att_pv)
            exp_in, silus = Tally(exp_ready), Tally(sil_ready)
            job = [0]
            own = {}

            def so_far(sem):
                return own.setdefault(sem.name, Tally(sem)).next()

            def next_bank():
                job[0] += 1
                return psum[:, (job[0] - 1) % 4, :]

            def gains2():
                for name, at, n in (("attn_norm", G_ATTN, D), ("q_norm", G_Q, 256), ("kv_norm", G_KV, P),
                                    ("mix_norm", G_MIX, 512), ("mlp_norm", G_MLP, D)):
                    w = par_at[name][1]
                    inst = dve.tensor_scalar(g2[:, at:at + w], pa(name), n ** 0.5, None, ALU.mult)
                inst.then_inc(v_step, 1)
                dve.wait_ge(v_step, so_far(v_step))

            def init():
                dve.wait_ge(params_in, 16)
                dve.wait_ge(consts_in, 16)
                dve.tensor_scalar(gain8[:, :, :], pa("head_gain").rearrange("p (a n) -> p a n", a=6), HD ** 0.5, None, ALU.mult)
                dve.tensor_scalar(nsink[:, :], pa("sink"), -1.0, None, ALU.mult)
                dve.tensor_scalar(sub8[:, :], pa("subln"), (1 - LAM_INIT) * 128 ** 0.5, None, ALU.mult).then_inc(v_step, 1)
                dve.wait_ge(v_step, so_far(v_step))

            def mod_gains(l, w):
                g = pa(("norm_mix", "norm_ffn")[w], at=KB * l, width=KB)[:, :, None].to_broadcast([P, KB, 2])
                dve.tensor_scalar(scale1[:, w, :, :], modT[:, 8 + 24 * w:16 + 24 * w, :], 1.0, D ** 0.5, ALU.add, ALU.mult).then_inc(v_step, 1)
                dve.wait_ge(v_step, so_far(v_step))
                dve.tensor_tensor(gain[:, w, :, :], scale1[:, w, :, :], g, ALU.mult).then_inc(gain_ready, 1)
                dve.wait_ge(gain_ready, so_far(gain_ready))

            def mod_rows(c):
                for x in (c, c + 1):
                    dve.wait_ge(used, chunks.next(2))
                    bank = next_bank()
                    dve.tensor_copy(mrow[:, x % 2, :], bank).then_inc(v_free, 1)
                    dve.wait_ge(v_free, so_far(v_free))
                    dve.memset(mark[:, 0:1], 0.0).then_inc(mod_row, 1)
                    dve.wait_ge(mod_row, so_far(mod_row))

            def with_bias(l, c, bank):
                bias = pa("b_mod", at=6 * KB * l, width=6 * KB)[:, bass.ds(4 * c, 4), None].to_broadcast([P, 4, 2])
                return dve.tensor_tensor(modT[:, bass.ds(4 * c, 4), :], bank[:, 0:8].rearrange("p (k r) -> p k r", r=2), bias, ALU.add)

            def mod_columns(l, c):
                for x in (c, c + 1):
                    dve.wait_ge(mm_v, jobs.next())
                    bank = next_bank()
                    with_bias(l, x, bank).then_inc(v_free, 1)
                    dve.wait_ge(v_free, so_far(v_free))

            def gate_diagonals(l):
                for w in range(2):
                    for r in range(2 - l):
                        column = modT[:, 16 + 24 * w:24 + 24 * w, r:r + 1].to_broadcast([P, KB, P])
                        dve.tensor_tensor(gate_diag[r][:, w], ident[:, None, :].to_broadcast([P, KB, P]), column, ALU.mult)\
                            .then_inc(diag_ready, 1)
                        dve.wait_ge(diag_ready, so_far(diag_ready))

            mod_in = Tally(mod_product)

            def mod_rest():
                scalers(4)
                for c in range(PAIRS // 2, MOD_BLOCKS, 2):
                    mod_rows(c)
                    mod_columns(1, c)
                mod_gains(1, 0)
                mod_gains(1, 1)
                gate_diagonals(1)

            def scalers(nt):
                dve.wait_ge(rs_done, norms_done.next())
                for m in range(nt):
                    dve.tensor_scalar(scaler[:, m, :], ident, rstd[:, 0, m:m + 1], None, ALU.mult).then_inc(xn_ready, 1)
                    dve.wait_ge(xn_ready, so_far(xn_ready))

            def norm(n, which, tiles):
                dve.wait_ge(gain_ready, n + 1)
                for k in range(0, KB, 2):
                    dve.wait_ge(mm_v, jobs.next())
                    bank = next_bank()
                    for a, b, r in [(0, 256, 1), (256, 512, 0)] if len(tiles) == 4 else [(0, 256, 0)]:
                        inst = dve.tensor_scalar(hT[:, k, a:b], bank[:, a:b], gain[:, which, k, r:r + 1],
                                                 modT[:, 24 * which + k, r:r + 1], ALU.mult, ALU.add)
                    inst.then_inc(v_free, 1)
                    dve.wait_ge(v_free, so_far(v_free))

            def h64(ap, n=HD):
                return ap.rearrange("p (h n) -> p h n", n=n)

            def rope(dst, src, heads, n, cos, sin):
                m = n // 2
                s, a, b = h64(src, n), h64(TA[:, 0:heads * n], n), h64(TB[:, 0:heads * n], n)
                dve.tensor_tensor(a, s, cos[:, None, :].to_broadcast([P, heads, n]), ALU.mult)
                dve.tensor_tensor(b[:, :, 0:m], s[:, :, m:n], sin[:, None, 0:m].to_broadcast([P, heads, m]), ALU.mult)
                dve.tensor_tensor(b[:, :, m:n], s[:, :, 0:m], sin[:, None, m:n].to_broadcast([P, heads, m]), ALU.mult).then_inc(v_step, 1)
                dve.wait_ge(v_step, so_far(v_step))
                return dve.tensor_tensor(h64(dst, n), a, b, ALU.add)

            def head_norm(bank, gains, keep=None, n=HD):
                heads = 512 // n
                dve.tensor_copy(TX, bank).then_inc(v_free, 1)
                dve.wait_ge(v_free, so_far(v_free))
                dve.tensor_tensor(SQ, TX, TX, ALU.mult).then_inc(v_step, 1)
                dve.wait_ge(v_step, so_far(v_step))
                b = 1 + heads_done.n % 2
                dve.tensor_reduce(sumsq[:, b, 0:heads], h64(SQ, n), AX, ALU.add).then_inc(hs_ready, 1)
                dve.wait_ge(hs_ready, so_far(hs_ready))
                heads_done.n += 1
                if keep:
                    dve.tensor_copy(keep[0], TX[:, keep[1]:keep[1] + keep[0].shape[-1]]).then_inc(v_step, 1)
                    dve.wait_ge(v_step, so_far(v_step))
                dve.wait_ge(hs_done, heads_done.value())
                dve.tensor_tensor(h64(TX, n), h64(TX, n), rstd[:, b, 0:heads, None].to_broadcast([P, heads, n]), ALU.mult).then_inc(v_step, 1)
                dve.wait_ge(v_step, so_far(v_step))
                for h0, nh, g in gains:
                    x = h64(TX)[:, h0:h0 + nh, :]
                    inst = dve.tensor_tensor(x, x, gain8[:, g:g + 1, :].to_broadcast([P, nh, HD]), ALU.mult)
                inst.then_inc(v_step, 1)
                dve.wait_ge(v_step, so_far(v_step))

            def heads_ab():
                for j in range(12):
                    c, tile, b = j // 4, j % 4, AB[j // 4]
                    if tile == 3:
                        dve.wait_ge(used, chunks.next(2))
                    else:
                        dve.wait_ge(mm_v, jobs.next())
                    bank = next_bank()
                    keep = None
                    if b["v"]:
                        s0, w, d0 = b["v"]
                        keep = (vA[:, tile, d0:d0 + w], s0)
                    head_norm(bank, b["norm"], keep)
                    r = R[j % 2]
                    if tile >= 2:
                        tab = slice(HD * (tile - 2), HD * (tile - 2) + HD)
                        inst = rope(r, TX, 8, HD, co("cos_ax")[:, tab], co("sin_ax")[:, tab])
                    else:
                        inst = dve.tensor_copy(r, TX)
                    if b["k"]:
                        inst.then_inc(v_step, 1)
                        dve.wait_ge(v_step, so_far(v_step))
                        k0 = b["k"][0]
                        inst = dve.tensor_copy(KDUP[j % 2].rearrange("p (g s n) -> p g s n", g=2, s=2),
                                               h64(r[:, k0:k0 + P])[:, :, None, :].to_broadcast([P, 2, 2, HD]))
                    inst.then_inc(rows_ready, 1)
                    dve.wait_ge(rows_ready, so_far(rows_ready))
                    if tile == 0 and c:
                        mod_columns(0, 2 + 2 * c)
                    if tile == 3:
                        mod_rows(4 + 2 * c)
                mod_columns(0, 8)
                mod_gains(0, 1)

            def heads_c():
                j = 0
                for c in range(6):
                    tiles = (2, 3) if c < 2 else (0, 1, 2, 3)
                    for tile in tiles:
                        if tile == 3:
                            dve.wait_ge(used, chunks.next(2))
                        else:
                            dve.wait_ge(mm_v, jobs.next())
                        bank = next_bank()
                        if c >= 4:
                            dve.tensor_copy(vC[:, tile, 512 * (c - 4):512 * (c - 4) + 512], bank).then_inc(v_free, 1)
                            dve.wait_ge(v_free, so_far(v_free))
                            continue
                        head_norm(bank, [(0, 8, 4 if c < 2 else 5)])
                        if tile >= 2:
                            tab = slice(HD * (tile - 2), HD * (tile - 2) + HD)
                            inst = rope(R[j % 2], TX, 8, HD, co("cos_ax")[:, tab], co("sin_ax")[:, tab])
                        else:
                            inst = dve.tensor_copy(R[j % 2], TX)
                        inst.then_inc(rows_ready, 1)
                        dve.wait_ge(rows_ready, so_far(rows_ready))
                        j += 1

            def attention(groups):
                def maxima(g):
                    dve.wait_ge(att_s, scored.next())
                    b, nk, heads = (scored.n - 1) % 4, g["nk"], len(g["heads"])
                    s = psum[:, 2 * (b % 2):2 * (b % 2) + 2, :].rearrange("p a n -> p (a n)")[:, 0:nk * heads].rearrange("p (u n) -> p u n", u=heads)
                    if g["mask"]:
                        at, m = g["mask"]
                        w = m.shape[-1]
                        part = s[:, :, at:at + w]
                        dve.tensor_tensor(part, part, m[:, None, :].to_broadcast([P, heads, w]), ALU.add).then_inc(v_step, 1)
                        dve.wait_ge(v_step, so_far(v_step))
                    dve.tensor_reduce(mx[:, b, 0:heads], s, AX, ALU.max).then_inc(v_step, 1)
                    dve.wait_ge(v_step, so_far(v_step))
                    if g["sink"] is None:
                        dve.tensor_scalar(nbias[:, b, 0:heads], mx[:, b, 0:heads], -g["scale"], None, ALU.mult).then_inc(att_m, 1)
                        dve.wait_ge(att_m, so_far(att_m))
                    else:
                        h = g["sink"]
                        dve.scalar_tensor_tensor(nbias[:, b, 0:heads], mx[:, b, 0:heads], -g["scale"], nsink[:, h:h + heads], ALU.mult, ALU.min).then_inc(v_step, 1)
                        dve.wait_ge(v_step, so_far(v_step))
                        dve.tensor_tensor(mx[:, b, 0:heads], nbias[:, b, 0:heads], nsink[:, h:h + heads], ALU.subtract).then_inc(att_m, 1)
                        dve.wait_ge(att_m, so_far(att_m))

                def evac(g):
                    dve.wait_ge(att_t, turned.next())
                    w = min(512, width(g))
                    dve.tensor_copy(probsT[:, (turned.n - 1) % 2, 0:w], psum[:, 4, 0:w]).then_inc(att_tv, 1)
                    dve.wait_ge(att_tv, so_far(att_tv))

                def output(g):
                    dve.wait_ge(att_pv, valued.next())
                    dve.wait_ge(att_e, expd.next())
                    b, heads, dv = (valued.n - 1) % 4, len(g["heads"]), g["dv"]
                    den = psums[:, b, 0:heads]
                    if g["sink"] is not None:
                        dve.tensor_tensor(den, den, esink[:, b, 0:heads], ALU.add).then_inc(v_step, 1)
                        dve.wait_ge(v_step, so_far(v_step))
                    dve.reciprocal(rden[:, b, 0:heads], den).then_inc(v_step, 1)
                    dve.wait_ge(v_step, so_far(v_step))
                    o = psum[:, 6 + b % 2, 0:heads * dv].rearrange("p (u n) -> p u n", u=heads)
                    r = rden[:, b, 0:heads]
                    if "keep" in g:
                        dve.tensor_scalar(r, r, g["keep"], None, ALU.mult).then_inc(v_step, 1)
                        dve.wait_ge(v_step, so_far(v_step))
                    if "gate" in g:
                        m, branch = g["gate"]
                        h = g["heads"][0]
                        dve.tensor_tensor(r, r, gs[:, m, 3 * h + branch:3 * (h + heads - 1) + branch + 1:3], ALU.mult).then_inc(v_step, 1)
                        dve.wait_ge(v_step, so_far(v_step))
                    if g.get("diff"):
                        dve.tensor_tensor(rden[:, b, 1:2], rden[:, b, 1:2], lam[:, 6:7], ALU.mult).then_inc(v_step, 1)
                        dve.wait_ge(v_step, so_far(v_step))
                        dve.tensor_scalar(TA2, o[:, 1, :], rden[:, b, 1:2], None, ALU.mult).then_inc(v_step, 1)
                        dve.wait_ge(v_step, so_far(v_step))
                        dve.scalar_tensor_tensor(g["out"], o[:, 0, :], rden[:, b, 0:1], TA2, ALU.mult, ALU.subtract).then_inc(att_o, 1)
                        dve.wait_ge(att_o, so_far(att_o))
                    elif "gate" in g and not g["first"]:
                        part = rows[:, 3, 0:heads * dv].rearrange("p (u n) -> p u n", u=heads)
                        dve.tensor_tensor(part, o, r[:, :, None].to_broadcast([P, heads, dv]), ALU.mult).then_inc(v_step, 1)
                        dve.wait_ge(v_step, so_far(v_step))
                        dve.tensor_tensor(g["out"], g["out"], rows[:, 3, 0:heads * dv], ALU.add).then_inc(att_o, 1)
                        dve.wait_ge(att_o, so_far(att_o))
                    else:
                        dve.tensor_tensor(g["out"].rearrange("p (u n) -> p u n", u=heads), o,
                                     rden[:, b, 0:heads, None].to_broadcast([P, heads, dv]), ALU.mult).then_inc(att_o, 1)
                        dve.wait_ge(att_o, so_far(att_o))

                maxima(groups[0])
                for n in range(len(groups)):
                    if n + 1 < len(groups):
                        maxima(groups[n + 1])
                    evac(groups[n])
                    if n:
                        output(groups[n - 1])
                output(groups[-1])

            TA2 = arena[:, 16384:16512]
            LP = arena[:, 16512:17024]

            def differential():
                lp = pa("lam").rearrange("p (a n) -> p a n", a=4)
                dve.tensor_tensor(LP[:, 0:128].rearrange("p (a n) -> p a n", a=2), lp[:, 0:4:2, :], lp[:, 1:4:2, :], ALU.mult).then_inc(v_step, 1)
                dve.wait_ge(v_step, so_far(v_step))
                dve.tensor_reduce(lam[:, 0:2], LP[:, 0:128].rearrange("p (a n) -> p a n", a=2), AX, ALU.add).then_inc(routed, 1)
                dve.wait_ge(routed, so_far(routed))
                dve.wait_ge(exp_ready, exp_in.next())
                dve.tensor_tensor(lam[:, 4:5], lam[:, 2:3], lam[:, 3:4], ALU.subtract).then_inc(v_step, 1)
                dve.wait_ge(v_step, so_far(v_step))
                dve.tensor_scalar(lam[:, 6:7], lam[:, 4:5], LAM_INIT, None, ALU.add).then_inc(v_step, 1)
                dve.wait_ge(v_step, so_far(v_step))

            def rms_rows(heads, scratch):
                o = [oA[:, tile, :].rearrange("p (h n) -> p h n", h=heads) for tile in range(2)]
                at = [1 + (heads_done.n + tile) % 2 for tile in range(2)]
                for tile in range(2):
                    sq = scratch[tile].rearrange("p (h n) -> p h n", h=heads)
                    dve.tensor_tensor(sq, o[tile], o[tile], ALU.mult).then_inc(v_step, 1)
                    dve.wait_ge(v_step, so_far(v_step))
                    dve.tensor_reduce(sumsq[:, at[tile], 0:heads], sq, AX, ALU.add).then_inc(hs_ready, 1)
                    dve.wait_ge(hs_ready, so_far(hs_ready))
                for tile in range(2):
                    dve.wait_ge(hs_done, heads_done.next())
                    scale = rstd[:, at[tile], 0:heads, None].to_broadcast([P, heads, D // heads])
                    dve.tensor_tensor(o[tile], o[tile], scale, ALU.mult).then_inc(rows_ready, 1)
                    dve.wait_ge(rows_ready, so_far(rows_ready))

            def outputs_T(nt, gains=None):
                for k in range(0, KB, 2):
                    dve.wait_ge(mm_v, jobs.next())
                    bank = next_bank()
                    if gains is None:
                        inst = dve.tensor_copy(hT[:, k, 0:P * nt], bank[:, 0:P * nt])
                    else:
                        inst = dve.tensor_scalar(hT[:, k, 0:P * nt], bank[:, 0:P * nt], gains[:, 0:1], None, ALU.mult)
                    inst.then_inc(v_free, 1)
                    dve.wait_ge(v_free, so_far(v_free))

            def add_output(which, tiles):
                for c in range(2):
                    cols = slice(512 * c, 512 * c + 512)
                    for tile in tiles:
                        if tile == 3:
                            dve.wait_ge(used, chunks.next(2))
                        else:
                            dve.wait_ge(mm_v, jobs.next())
                        bank = next_bank()
                        if which is None:
                            dve.tensor_tensor(X[:, tile, cols], X[:, tile, cols], bank, ALU.add).then_inc(v_free, 1)
                            dve.wait_ge(v_free, so_far(v_free))
                            if c:
                                dve.memset(mark[:, 0:1], 0.0).then_inc(x_tile, 1)
                                dve.wait_ge(x_tile, so_far(x_tile))
                            continue
                        dve.tensor_tensor(TMP, bank, gate[:, which, 1 if tile < 2 else 0, cols], ALU.mult).then_inc(v_free, 1)
                        dve.wait_ge(v_free, so_far(v_free))
                        done = x_tile if c else v_step
                        dve.tensor_tensor(X[:, tile, cols], X[:, tile, cols], TMP, ALU.add).then_inc(done, 1)
                        dve.wait_ge(done, so_far(done))
                dve.memset(mark[:, 0:1], 0.0).then_inc(x_ready, 1)
                dve.wait_ge(x_ready, so_far(x_ready))

            def choose(l, nt):
                def tab(a, w=EXPERTS, at=0):
                    return route[:, a, 0:nt, at:at + w]

                def over(ap, w):
                    return ap.to_broadcast([P, nt, w])

                def one_hot(dst, src, best, rank, w, scratch):
                    dve.tensor_tensor(scratch, src, over(best, w), ALU.is_equal).then_inc(v_step, 1)
                    dve.wait_ge(v_step, so_far(v_step))
                    dve.tensor_tensor(scratch, scratch, rank[:, None, :].to_broadcast([P, nt, w]), ALU.mult).then_inc(v_step, 1)
                    dve.wait_ge(v_step, so_far(v_step))
                    dve.tensor_reduce(tab(2, 1, 8), scratch, AX, ALU.max).then_inc(v_step, 1)
                    dve.wait_ge(v_step, so_far(v_step))
                    dve.tensor_tensor(dst, scratch, over(tab(2, 1, 8), w), ALU.is_equal).then_inc(v_step, 1)
                    dve.wait_ge(v_step, so_far(v_step))

                dve.wait_ge(mm_v, jobs.next())
                bank = next_bank()
                br = pa("b_route", at=ROUTES * l, width=ROUTES)[:, None, :].to_broadcast([P, nt, ROUTES])
                dve.tensor_tensor(tab(0, ROUTES), bank[:, 0:ROUTES * nt].rearrange("p (t e) -> p t e", t=nt), br, ALU.add).then_inc(v_free, 1)
                dve.wait_ge(v_free, so_far(v_free))
                lg, le = tab(0, 4), tab(0, EXPERTS, 4)
                dve.tensor_reduce(tab(2, 1, 5), lg, AX, ALU.max).then_inc(v_step, 1)
                dve.wait_ge(v_step, so_far(v_step))
                dve.tensor_scalar(tab(2, 1, 0), tab(2, 1, 5), -1.0, None, ALU.mult).then_inc(routed, 1)
                dve.wait_ge(routed, so_far(routed))
                one_hot(tab(3, 4), lg, tab(2, 1, 5), co("rank_g"), 4, tab(4, 4))
                inside = tab(5).rearrange("p t (g e) -> p t g e", g=GROUPS)
                for tile in range(nt):
                    dve.tensor_copy(inside[:, tile], route[:, 3, tile, 0:4, None].to_broadcast([P, GROUPS, PER_GROUP])).then_inc(v_step, 1)
                    dve.wait_ge(v_step, so_far(v_step))
                dve.tensor_tensor(tab(6), le, tab(5), ALU.mult).then_inc(v_step, 1)
                dve.wait_ge(v_step, so_far(v_step))
                dve.tensor_scalar(tab(7), tab(5), -NEG, NEG, ALU.mult, ALU.add).then_inc(v_step, 1)
                dve.wait_ge(v_step, so_far(v_step))
                dve.tensor_tensor(tab(6), tab(6), tab(7), ALU.add).then_inc(v_step, 1)
                dve.wait_ge(v_step, so_far(v_step))
                dve.tensor_reduce(tab(2, 1, 6), tab(6), AX, ALU.max).then_inc(v_step, 1)
                dve.wait_ge(v_step, so_far(v_step))
                one_hot(tab(8), tab(6), tab(2, 1, 6), co("rank_e"), EXPERTS, tab(7))
                dve.scalar_tensor_tensor(tab(7), tab(8), 2 * NEG, tab(6), ALU.mult, ALU.add).then_inc(v_step, 1)
                dve.wait_ge(v_step, so_far(v_step))
                dve.tensor_reduce(tab(2, 1, 7), tab(7), AX, ALU.max).then_inc(v_step, 1)
                dve.wait_ge(v_step, so_far(v_step))
                dve.tensor_tensor(tab(2, 1, 3), tab(2, 1, 7), tab(2, 1, 6), ALU.subtract).then_inc(routed, 1)
                dve.wait_ge(routed, so_far(routed))
                one_hot(tab(9), tab(7), tab(2, 1, 7), co("rank_e"), EXPERTS, tab(10))
                dve.tensor_tensor(tab(11), tab(8), tab(9), ALU.add).then_inc(v_step, 1)
                dve.wait_ge(v_step, so_far(v_step))
                dve.tensor_copy(tab(10), tab(11)).then_inc(chosen, 1)
                dve.wait_ge(chosen, so_far(chosen))
                dve.wait_ge(exp_ready, exp_in.next(2))
                dve.tensor_scalar(tab(2, 1, 9), tab(2, 1, 4), 1.0, None, ALU.add).then_inc(v_step, 1)
                dve.wait_ge(v_step, so_far(v_step))
                dve.tensor_tensor(tab(2, 1, 9), tab(2, 1, 9), tab(2, 1, 1), ALU.mult).then_inc(v_step, 1)
                dve.wait_ge(v_step, so_far(v_step))
                dve.reciprocal(tab(2, 1, 10), tab(2, 1, 9)).then_inc(v_step, 1)
                dve.wait_ge(v_step, so_far(v_step))
                dve.tensor_tensor(tab(2, 1, 11), tab(2, 1, 10), tab(2, 1, 4), ALU.mult).then_inc(v_step, 1)
                dve.wait_ge(v_step, so_far(v_step))
                dve.memset(route[:, 12:14, :, :], -1.0).then_inc(v_step, 1)
                dve.wait_ge(v_step, so_far(v_step))
                dve.tensor_tensor(tab(8), tab(8), over(tab(2, 1, 10), EXPERTS), ALU.mult).then_inc(v_step, 1)
                dve.wait_ge(v_step, so_far(v_step))
                dve.tensor_tensor(tab(9), tab(9), over(tab(2, 1, 11), EXPERTS), ALU.mult).then_inc(v_step, 1)
                dve.wait_ge(v_step, so_far(v_step))
                dve.tensor_tensor(tab(12), tab(8), tab(9), ALU.add).then_inc(v_step, 1)
                dve.wait_ge(v_step, so_far(v_step))
                dve.wait_ge(mm_v, jobs.next())
                bank = next_bank()
                pos = bank[:, 0:EXPERTS * nt].rearrange("p (t e) -> p t e", t=nt)
                dve.scalar_tensor_tensor(tab(7), pos, 1.0, tab(11), ALU.add, ALU.mult).then_inc(v_step, 1)
                dve.wait_ge(v_step, so_far(v_step))
                dve.tensor_scalar(tab(13), tab(7), -1.0, None, ALU.add).then_inc(v_step, 1)
                dve.wait_ge(v_step, so_far(v_step))
                fullest = route[:, 14, 0, 0:1]
                dve.tensor_reduce(fullest, bank[:, EXPERTS * nt:EXPERTS * nt + EXPERTS], AX, ALU.max).then_inc(v_free, 1)
                dve.wait_ge(v_free, so_far(v_free))
                for r in range(nt):
                    inst = dve.tensor_scalar(route[:, 14, 0, 1 + r:2 + r], fullest, float(SLOTS + P * r), None, ALU.is_gt)
                inst.then_inc(v_step, 1)
                dve.wait_ge(v_step, so_far(v_step))
                dve.tensor_reduce(fullest, route[:, 14, 0, 1:1 + nt], AX, ALU.add).then_inc(v_step, 1)
                dve.wait_ge(v_step, so_far(v_step))
                dve.tensor_copy(late_rounds[:, :], route[0:1, 14, 0, 0:1]).then_inc(rounds_ready, 1)
                dve.wait_ge(rounds_ready, so_far(rounds_ready))

            def late_rows(l, nt, count):
                s = late[l]
                product, silu, steps = Tally(s["product"]), Tally(s["a"]), {s[n].name: Tally(s[n]) for n in ("v", "step", "round", "added")}
                own.update(steps)

                at = route[:, 15, 0:nt, 0:EXPERTS]
                per = {product: 5, silu: 3, steps[s["v"].name]: 5, steps[s["step"].name]: 1, steps[s["added"].name]: 2 * nt}
                with laps(dve, nt, {**{t: EXPERTS * n for t, n in per.items()}, steps[s["round"].name]: 1}) as r:
                    with dve.If(count > r):
                        dve.tensor_scalar(at, at, -P, None, ALU.add).then_inc(s["round"], 1)
                        rounds = steps[s["round"].name]
                        rounds.n += 1
                        with laps(dve, EXPERTS, per) as e:
                            dve.wait_ge(s["round"], rounds.value())
                            col = route[:, 15, 0:nt, bass.ds(e, 1)].to_broadcast([P, nt, P])
                            dve.tensor_tensor(pick[:, 0, 0:nt, :], co("slot")[:, None, :].to_broadcast([P, nt, P]), col, ALU.is_equal).then_inc(s["step"], 1)
                            dve.wait_ge(s["step"], so_far(s["step"]))
                            col = route[:, 12, 0:nt, bass.ds(e, 1)].to_broadcast([P, nt, P])
                            dve.tensor_tensor(share[:, 0, 0:nt, :], pick[:, 0, 0:nt, :], col, ALU.mult).then_inc(s["v"], 1)
                            dve.wait_ge(s["v"], so_far(s["v"]))
                            dve.wait_ge(s["product"], product.next())
                            dve.tensor_copy(shareT[:, 0:nt, :], psum[:, 0, 0:P * nt].rearrange("p (t n) -> p t n", t=nt)).then_inc(s["v"], 1)
                            dve.wait_ge(s["v"], so_far(s["v"]))
                            dve.wait_ge(s["product"], product.next())
                            dve.wait_ge(s["a"], silu.next(2))
                            dve.tensor_tensor(act_, psum[:, 1, :], siluG, ALU.mult).then_inc(s["v"], 1)
                            dve.wait_ge(s["v"], so_far(s["v"]))
                            dve.wait_ge(s["product"], product.next())
                            dve.tensor_copy(actT, psum[:, 2, :].rearrange("p (f n) -> p f n", f=4)).then_inc(s["v"], 1)
                            dve.wait_ge(s["v"], so_far(s["v"]))
                            dve.wait_ge(s["product"], product.next())
                            dve.tensor_copy(ySlot[:, 512:1024], psum[:, 3, :]).then_inc(s["v"], 1)
                            dve.wait_ge(s["v"], so_far(s["v"]))
                            silu.n += 1
                            dve.wait_ge(s["product"], product.next())
                            for tile in range(nt):
                                for h in range(2):
                                    f = facc[:, tile, 512 * h:512 * h + 512]
                                    dve.tensor_tensor(f, f, psum[:, 2 * tile + h, :], ALU.add).then_inc(s["added"], 1)
                                    dve.wait_ge(s["added"], so_far(s["added"]))
                    dve.end_ifs()

            def moe(l):
                nt = 4 - 2 * l
                tiles = [0, 1, 2, 3][2 * l:]
                dve.memset(shareT[:, 0:nt, :], 0.0)
                dve.memset(ySlot, 0.0)
                dve.memset(facc[:, 0:nt, :], 0.0).then_inc(v_step, 1)
                dve.wait_ge(v_step, so_far(v_step))
                scalers(nt)
                norm(2 * l + 1, 1, tiles)
                choose(l, nt)

                def selector(dst, e0, weigh, signal):
                    d = dst[:, 0:nt, :].rearrange("p t (e s) -> p t e s", e=2)
                    for e in range(2):
                        slots = co("slot", width=SLOTS)[:, None, :].to_broadcast([P, nt, SLOTS])
                        col = route[:, 13, 0:nt, bass.ds(e0 + e, 1)].to_broadcast([P, nt, SLOTS])
                        inst = dve.tensor_tensor(d[:, :, e, :], slots, col, ALU.is_equal)
                    if weigh:
                        inst.then_inc(v_step, 1)
                        dve.wait_ge(v_step, so_far(v_step))
                        for e in range(2):
                            col = route[:, 12, 0:nt, bass.ds(e0 + e, 1)].to_broadcast([P, nt, SLOTS])
                            inst = dve.tensor_tensor(d[:, :, e, :], d[:, :, e, :], col, ALU.mult)
                    if signal:
                        inst.then_inc(pick_ready, 1)
                        dve.wait_ge(pick_ready, so_far(pick_ready))

                def add_pair():
                    for tile in range(nt):
                        for h in range(2):
                            dve.wait_ge(mm_v, jobs.next())
                            bank = next_bank()
                            f = facc[:, tile, 512 * h:512 * h + 512]
                            dve.tensor_tensor(f, f, bank, ALU.add).then_inc(v_free, 1)
                            dve.wait_ge(v_free, so_far(v_free))

                selector(pick[:, 0], 0, False, False)
                selector(share[:, 0], 0, True, True)
                selector(pick[:, 1], 2, False, True)
                dve.tensor_scalar(route[:, 15, 0:nt, 0:EXPERTS], route[:, 13, 0:nt, 0:EXPERTS], P - SLOTS, None, ALU.add).then_inc(v_step, 1)
                dve.wait_ge(v_step, so_far(v_step))
                dve.memset(mark[:, 0:1], 0.0).then_inc(late[l]["free"], 1)
                dve.wait_ge(late[l]["free"], so_far(late[l]["free"]))
                count = dve.value_load(late_rounds[0:1, 0:1], min_val=0, max_val=nt)
                base = job[0]
                per_pair = 4 + 2 * nt
                assert per_pair % 4 == 0
                job[0] = 0
                mine = {own[v_step.name]: 2, own[v_free.name]: 2 * per_pair, own[pick_ready.name]: 2}
                if l == 0:
                    mine.update({own.setdefault(mod_taken.name, Tally(mod_taken)): 2, mod_in: 2})
                with laps(dve, PAIRS // 2, {jobs: 2 * (per_pair - 2), chunks: 24, silus: 2, **mine}) as i:
                    for b in range(2):
                        add_pair()
                        if l == 0 and b == 1:
                            dve.wait_ge(mod_product, mod_in.next())
                            dve.tensor_copy(mod_sums, psum[:, 7, :]).then_inc(mod_taken, 1)
                            dve.wait_ge(mod_taken, so_far(mod_taken))
                        dve.wait_ge(used, chunks.next(8))
                        bank = next_bank()
                        dve.wait_ge(sil_ready, silus.next())
                        dve.tensor_tensor(act_, bank, siluG, ALU.mult).then_inc(v_free, 1)
                        dve.wait_ge(v_free, so_far(v_free))
                        if l == 0 and b == 1:
                            dve.wait_ge(mod_product, mod_in.next())
                            with_bias(1, i, psum[:, 7, :]).then_inc(mod_taken, 1)
                            dve.wait_ge(mod_taken, so_far(mod_taken))
                        dve.wait_ge(mm_v, jobs.next())
                        bank = next_bank()
                        dve.tensor_copy(actT, bank.rearrange("p (f n) -> p f n", f=4)).then_inc(v_free, 1)
                        dve.wait_ge(v_free, so_far(v_free))
                        dve.wait_ge(mm_v, jobs.next())
                        bank = next_bank()
                        dve.tensor_copy(shareT[:, 0:nt, :], bank[:, 0:P * nt].rearrange("p (t n) -> p t n", t=nt)).then_inc(v_free, 1)
                        dve.wait_ge(v_free, so_far(v_free))
                        selector(share[:, 1 - b], 4 * i + 2 * b + 2, True, False)
                        selector(pick[:, b], 4 * i + 2 * b + 4, False, True)
                        dve.wait_ge(used, chunks.next(4))
                        bank = next_bank()
                        dve.tensor_copy(ySlot[:, 512:1024], bank).then_inc(v_free, 1)
                        dve.wait_ge(v_free, so_far(v_free))
                add_pair()
                job[0] = base + PAIRS * per_pair + 2 * nt
                late_rows(l, nt, count)
                for tile in range(nt):
                    dve.tensor_tensor(facc[:, tile, :], facc[:, tile, :], gate[:, 1, 1 if tile + 2 * l < 2 else 0, :], ALU.mult).then_inc(v_step, 1)
                    dve.wait_ge(v_step, so_far(v_step))
                    x = X[:, tile + 2 * l, :]
                    dve.tensor_tensor(x, x, facc[:, tile, :], ALU.add).then_inc(x_tile, 1)
                    dve.wait_ge(x_tile, so_far(x_tile))
                dve.memset(mark[:, 0:1], 0.0).then_inc(x_ready, 1)
                dve.wait_ge(x_ready, so_far(x_ready))

            def turned2(g):
                for k in range(0, KB, 2):
                    dve.wait_ge(mm_v, jobs.next())
                    bank = next_bank()
                    dve.tensor_scalar(hT[:, k, 0:SEQ], bank[:, 0:SEQ], g2[:, g + k:g + k + 1], None, ALU.mult).then_inc(v_free, 1)
                    dve.wait_ge(v_free, so_far(v_free))

            def rotated(dst, src, heads, cos, sin):
                n = cos.shape[-1]
                m = n // 2
                a, b = h64(TA[:, 0:heads * n], n), h64(TB[:, 0:heads * n], n)
                dve.tensor_tensor(a, src, cos[:, None, :].to_broadcast([P, heads, n]), ALU.mult)
                dve.tensor_tensor(b[:, :, 0:m], src[:, :, m:n], sin[:, None, 0:m].to_broadcast([P, heads, m]), ALU.mult)
                dve.tensor_tensor(b[:, :, m:n], src[:, :, 0:m], sin[:, None, m:n].to_broadcast([P, heads, m]), ALU.mult).then_inc(v_step, 1)
                dve.wait_ge(v_step, so_far(v_step))
                return dve.tensor_tensor(dst, a, b, ALU.add)

            def project2():
                for c in range(4):
                    for m in range(2):
                        cos, sin = (co(n, at=HD * m, width=HD) for n in ("cos_a", "sin_a"))
                        if m:
                            dve.wait_ge(used, chunks.next(2))
                        else:
                            dve.wait_ge(mm_v, jobs.next())
                        bank = next_bank()
                        if c == 0:
                            dve.tensor_copy(TX, bank).then_inc(v_free, 1)
                            dve.wait_ge(v_free, so_far(v_free))
                            rotated(h64(R[m]), h64(TX), 8, cos, sin).then_inc(rows_ready, 1)
                            dve.wait_ge(rows_ready, so_far(rows_ready))
                            continue
                        w = min(512, IN2 - 512 * c)
                        dve.tensor_copy(PR[:, m, 512 * c:512 * c + w], bank[:, 0:w]).then_inc(v_free, 1)
                        dve.wait_ge(v_free, so_far(v_free))
                        if c == 1:
                            for b, col in ((0, KC2), (4, KS2)):
                                rotated(h64(TX[:, 0:P]), h64(PR[:, m, col:col + P]), 2, cos, sin).then_inc(v_step, 1)
                                dve.wait_ge(v_step, so_far(v_step))
                                dve.tensor_copy(KD[m][:, b:b + 2], h64(TX[:, 0:P])[:, :, None, :].to_broadcast([P, 2, 2, HD])).then_inc(v_step, 1)
                                dve.wait_ge(v_step, so_far(v_step))
                            dve.tensor_copy(KD[m][:, 2:4], h64(PR[:, m, VC2:VC2 + P])[:, :, None, :].to_broadcast([P, 2, 2, HD])).then_inc(rows_ready, 1)
                            dve.wait_ge(rows_ready, so_far(rows_ready))
                        elif c == 2:
                            rotated(h64(TX[:, 0:P]), h64(PR[:, m, KW2:KW2 + P]), 2, cos, sin).then_inc(v_step, 1)
                            dve.wait_ge(v_step, so_far(v_step))
                            dve.tensor_copy(KWD[m], h64(TX[:, 0:P])[:, :, None, :].to_broadcast([P, 2, 2, HD])).then_inc(rows_ready, 1)
                            dve.wait_ge(rows_ready, so_far(rows_ready))
                        else:
                            for col, n, at in ((CQ2, 256, 0), (CKV2, P, 256)):
                                x = PR[:, m, col:col + n]
                                dve.tensor_tensor(SQ[:, 0:n], x, x, ALU.mult).then_inc(v_step, 1)
                                dve.wait_ge(v_step, so_far(v_step))
                                b = 1 + heads_done.n % 2
                                dve.tensor_reduce(sumsq[:, b, 0:1], SQ[:, 0:n], AX, ALU.add).then_inc(hs_ready, 1)
                                dve.wait_ge(hs_ready, so_far(hs_ready))
                                dve.wait_ge(hs_done, heads_done.next())
                                dve.tensor_scalar(CQ[m][:, at:at + n], x, rstd[:, b, 0:1], None, ALU.mult).then_inc(v_step, 1)
                                dve.wait_ge(v_step, so_far(v_step))
                            kr = PR[:, m, KR2:KR2 + 32]
                            rotated(kpe[:, m:m + 1, :], kr[:, None, :], 1,
                                    co("cos_b", at=32 * m, width=32), co("sin_b", at=32 * m, width=32)).then_inc(rows_ready, 1)
                            dve.wait_ge(rows_ready, so_far(rows_ready))
                dve.memset(mark[:, 0:1], 0.0).then_inc(routed, 1)
                dve.wait_ge(routed, so_far(routed))
                dve.wait_ge(exp_ready, exp_in.next())
                dve.tensor_scalar(gs, gs, 1.0, None, ALU.add).then_inc(v_step, 1)
                dve.wait_ge(v_step, so_far(v_step))
                dve.reciprocal(gs, gs).then_inc(v_step, 1)
                dve.wait_ge(v_step, so_far(v_step))
                for m in range(2):
                    q = rows[:, m, 0:768]
                    dve.wait_ge(mm_v, jobs.next())
                    bank = next_bank()
                    dve.tensor_copy(q[:, 0:512], bank).then_inc(v_free, 1)
                    dve.wait_ge(v_free, so_far(v_free))
                    if m:
                        dve.wait_ge(used, chunks.next(1))
                    else:
                        dve.wait_ge(mm_v, jobs.next())
                    bank = next_bank()
                    dve.tensor_copy(q[:, 512:768], bank[:, 0:256]).then_inc(v_free, 1)
                    dve.wait_ge(v_free, so_far(v_free))
                    part = q.rearrange("p (h n) -> p h n", h=8)[:, :, HD:MLA_D]
                    rotated(part, part, 8, co("cos_b", at=32 * m, width=32), co("sin_b", at=32 * m, width=32)).then_inc(rows_ready, 1)
                    dve.wait_ge(rows_ready, so_far(rows_ready))
                for m in range(2):
                    k = rows[:, 2 + m, 0:768].rearrange("p (h n) -> p h n", h=8)
                    for j in range(2):
                        if m and j:
                            dve.wait_ge(used, chunks.next(1))
                        else:
                            dve.wait_ge(mm_v, jobs.next())
                        kv = next_bank().rearrange("p (h n) -> p h n", h=4)
                        dve.tensor_copy(k[:, 4 * j:4 * j + 4, 0:HD], kv[:, :, 0:HD])
                        dve.tensor_copy(h64(VM[:, m, 256 * j:256 * j + 256]), kv[:, :, HD:P]).then_inc(v_free, 1)
                        dve.wait_ge(v_free, so_far(v_free))
                    dve.tensor_copy(k[:, :, HD:MLA_D], kpe[:, m:m + 1, :].to_broadcast([P, 8, 32])).then_inc(rows_ready, 1)
                    dve.wait_ge(rows_ready, so_far(rows_ready))

            def compress(l):
                for w, name in enumerate(("pos_k", "pos_v")):
                    pos = pa(name, at=16 * l, width=16)
                    for g in range(2):
                        x = kvT2[:, 2 * w + g, :]
                        win = bass.AP(tensor=x.tensor, offset=x.offset, ap=[list(x.ap[0]), [1, 16], [8, 15]])
                        inst = dve.tensor_tensor(XB[:, w, :, g, :], win, pos[:, :, None].to_broadcast([P, 16, 15]), ALU.add)
                    inst.then_inc(rows_ready, 1)
                    dve.wait_ge(rows_ready, so_far(rows_ready))
                chunks.n += 4
                dve.wait_ge(mm_v, jobs.next())
                bank = next_bank()
                t4 = bank[:, 0:P].rearrange("p (b n) -> p b n", b=4)
                dve.tensor_copy(hidT[:, 0:2, 0:30], t4[:, 0:2, 0:30])
                for j in range(2):
                    src = t4[:, 2 + j, 0:30].rearrange("p (g i) -> p g i", g=2)[:, :, None, :].to_broadcast([P, 2, 4, 15])
                    inst = dve.tensor_copy(hv[:, j, :, 0:15].rearrange("p (g h) i -> p g h i", g=2), src)
                inst.then_inc(v_free, 1)
                dve.wait_ge(v_free, so_far(v_free))
                dve.wait_ge(mm_v, jobs.next())
                bank = next_bank()
                kc = bank[:, 0:30].rearrange("p (g i) -> p g i", g=2)
                dve.tensor_copy(kC[0:64, :, 0, 0:15], kc[0:64])
                dve.tensor_copy(kC[64:128, :, 1, 0:15], kc[64:128])
                dve.tensor_tensor(vBD, bank[:, None, 64:128].to_broadcast([P, 8, HD]),
                                  co("block_diag")[:, :, None].to_broadcast([P, 8, HD]), ALU.mult).then_inc(v_free, 1)
                dve.wait_ge(v_free, so_far(v_free))

            def mlp():
                for c in range(8):
                    dve.wait_ge(used, chunks.next(2))
                    bank = next_bank()
                    f = aT[:, 4 * c + 2:4 * c + 4, :]
                    dve.tensor_scalar(f, bank.rearrange("p (f n) -> p f n", f=2), 0.0, None, ALU.max).then_inc(v_step, 1)
                    dve.wait_ge(v_step, so_far(v_step))
                    dve.tensor_tensor(f, f, f, ALU.mult).then_inc(v_free, 1)
                    dve.wait_ge(v_free, so_far(v_free))
                for m in range(2):
                    for h in range(2):
                        if m and h:
                            dve.wait_ge(used, chunks.next(16))
                        else:
                            dve.wait_ge(mm_v, jobs.next())
                        bank = next_bank()
                        x = X[:, 2 + m, 512 * h:512 * h + 512]
                        dve.tensor_tensor(x, x, bank, ALU.add).then_inc(v_free, 1)
                        dve.wait_ge(v_free, so_far(v_free))
                    dve.memset(mark[:, 0:1], 0.0).then_inc(x_tile, 1)
                    dve.wait_ge(x_tile, so_far(x_tile))
                dve.memset(mark[:, 0:1], 0.0).then_inc(x_ready, 1)
                dve.wait_ge(x_ready, so_far(x_ready))

            def final_norm():
                dve.wait_ge(rs_done, norms_done.next())
                dve.wait_ge(final_in, 16)
                for m in range(2):
                    dve.tensor_scalar(rows[:, m, :], X[:, 2 + m, :], rstd[:, 0, m:m + 1], D ** 0.5, ALU.mult, ALU.mult).then_inc(v_step, 1)
                    dve.wait_ge(v_step, so_far(v_step))
                    dve.tensor_tensor(rows[:, m, :], rows[:, m, :], arena[:, 0:D], ALU.mult).then_inc(x_ready, 1)
                    dve.wait_ge(x_ready, so_far(x_ready))

            init()
            gains2()
            differential()
            scalers(4)
            for c in (0, 2):
                mod_rows(c)
                mod_columns(0, c)
            mod_gains(0, 0)
            norm(0, 0, [0, 1, 2, 3])
            heads_ab()
            attention(groups_ab())
            mod_rows(10)
            mod_columns(0, 10)
            outputs_T(4)
            gate_diagonals(0)
            add_output(0, [0, 1, 2, 3])
            moe(0)
            mod_rest()
            norm(2, 0, [0, 1, 2, 3])
            heads_c()
            attention(groups_c())
            rms_rows(8, [arena[:, 16384:17408], arena[:, 17408:18432]])
            outputs_T(2, sub8)
            add_output(0, [2, 3])
            moe(1)
            for l in range(DEPTH):
                scalers(2)
                turned2(G_ATTN + KB * l)
                project2()
                compress(l)
                attention(groups_2())
                rms_rows(2, [rows[:, 2, :], rows[:, 3, :]])
                turned2(G_MIX + KB * l)
                add_output(None, [2, 3])
                scalers(2)
                turned2(G_MLP + KB * l)
                mlp()
            final_norm()

        @block.tensor
        def _(pe):
            v_done, a_done = Tally(v_free), Tally(a_free)
            vi, ai, chunk = [0], [0], [0]
            chunk_in = [Tally(s, 16) for s in loaded]
            xn, rws, outs, picks = Tally(xn_ready), Tally(rows_ready), Tally(att_o), Tally(pick_ready)
            expd, tv, ta = Tally(att_e), Tally(att_tv), Tally(att_ta)
            mixed, choice = Tally(mod_row), Tally(chosen)

            def v_bank():
                v_done.n += 1
                vi[0] += 1
                return psum[:, (vi[0] - 1) % 4, :]

            def a_bank():
                a_done.n += 1
                ai[0] += 1
                return psum[:, 4 + (ai[0] - 1) % 4, :]

            def weights(n):
                out = []
                for _ in range(n):
                    slot = chunk[0] % RING
                    chunk[0] += 1
                    pe.wait_ge(loaded[slot], chunk_in[slot].next())
                    out.append(ring[:, slot, :])
                return out

            def k512(pair):
                return [pair[k // 4].rearrange("p (k n) -> p k n", k=4)[:, k % 4, :] for k in range(KB)]

            def transpose(out, in_):
                return pe.transpose(out, in_, ident)

            def mod_block(out, w, signal=None):
                for k in range(KB):
                    j = k % 4
                    inst = pe.matmul(out[32 * j:32 * j + 32, :], cpad[:, k, :], w[k], start=k < 4, stop=k >= 4)
                    if signal is used and k == 3:
                        inst.then_inc(used, 1)
                inst.then_inc(signal, 1)

            def folded(out, sums):
                for j in range(4):
                    inst = pe.matmul(out[:, 2 * j:2 * j + 2], sums[:, P * j:P * j + P], co("fold"), start=True, stop=True)
                return inst

            def mod_products(c):
                for x in (c, c + 1):
                    w = k512(weights(2))
                    pe.wait_ge(v_free, v_done.value(back=3))
                    bank = v_bank()
                    mod_block(bank, w, used)

            def mod_folds(c):
                for x in (c, c + 1):
                    pe.wait_ge(mod_row, mixed.next())
                    pe.wait_ge(v_free, v_done.value(back=3))
                    bank = v_bank()
                    folded(bank, mrow[:, x % 2, :]).then_inc(mm_v, 1)

            diags = Tally(diag_ready)

            def gates(l):
                for w in range(2):
                    for r in range(2 - l):
                        pe.wait_ge(diag_ready, diags.next())
                        for h in range(2):
                            pe.wait_ge(a_free, a_done.value(back=3))
                            bank = a_bank()
                            d = gate_diag[r][:, w, 4 * h:4 * h + 4, :].rearrange("p k n -> p (k n)")
                            pe.matmul(bank, co("ones"), d, start=True, stop=True).then_inc(mm_a, 1)

            mod_in, mod_out = Tally(mod_loaded, 16), Tally(mod_taken)

            def norm(nt):
                for m in range(nt):
                    pe.wait_ge(xn_ready, xn.next())
                for k in range(KB):
                    if k % 2:
                        pe.wait_ge(a_free, a_done.value(back=3))
                        bank = a_bank()
                    else:
                        pe.wait_ge(v_free, v_done.value(back=3))
                        bank = v_bank()
                    for m in range(nt):
                        inst = pe.matmul(bank[:, P * m:P * m + P], X[:, 4 - nt + m, P * k:P * k + P], scaler[:, m, :], start=True, stop=True)
                    inst.then_inc(mm_a if k % 2 else mm_v, 1)

            def columns512(w, m, last):
                pe.wait_ge(v_free, v_done.value(back=3))
                bank = v_bank()
                for k in range(KB):
                    inst = pe.matmul(bank, hT[:, k, P * m:P * m + P], w[k], start=k == 0, stop=k == KB - 1)
                    if last and k == 3:
                        inst.then_inc(used, 1)
                inst.then_inc(used if last else mm_v, 1)

            def heads(blocks, tiles_of, turn, modulate=False):
                pe.wait_ge(v_free, v_done.value())
                pe.wait_ge(a_free, a_done.value())
                waiting = []
                for c in range(blocks):
                    w = k512(weights(2))
                    tiles = tiles_of(c)
                    for tile in tiles:
                        columns512(w, tile, tile == tiles[-1])
                        if waiting:
                            turn(*waiting.pop())
                        waiting.append((c, tile))
                        if modulate and c and tile == tiles[0]:
                            mod_folds(2 + 2 * c)
                    if modulate:
                        mod_products(4 + 2 * c)
                turn(*waiting.pop())
                if modulate:
                    mod_folds(8)

            turn_n = [0]

            def turn_ab(c, tile):
                pe.wait_ge(rows_ready, rws.next())
                b = turn_n[0] % 2
                turn_n[0] += 1
                pe.wait_ge(a_free, a_done.value(back=3))
                bank = a_bank()
                s0, nq, _ = AB[c]["q"]
                for j in range(nq):
                    inst = transpose(bank[:, P * j:P * j + P], R[b][:, s0 + P * j:s0 + P * j + P])
                if AB[c]["k"]:
                    for j in range(2):
                        inst = transpose(bank[:, 256 + P * j:256 + P * j + P], KDUP[b][:, P * j:P * j + P])
                inst.then_inc(mm_a, 1)

            def turn_c(c, tile):
                if c >= 4:
                    return
                pe.wait_ge(rows_ready, rws.next())
                b = turn_n[0] % 2
                turn_n[0] += 1
                pe.wait_ge(a_free, a_done.value(back=3))
                bank = a_bank()
                for j in range(4):
                    inst = transpose(bank[:, P * j:P * j + P], R[b][:, P * j:P * j + P])
                inst.then_inc(mm_a, 1)

            att_n = [0]

            def attention(groups):
                pe.wait_ge(v_free, v_done.value())
                pe.wait_ge(a_free, a_done.value())
                base = att_n[0]
                att_n[0] += len(groups)

                def scores(n):
                    g = groups[n]
                    if base + n >= 2:
                        pe.wait_ge(att_e, base + n - 1)
                    s = psum[:, 2 * ((base + n) % 2):2 * ((base + n) % 2) + 2, :].rearrange("p a n -> p (a n)")
                    for u, (q, k) in enumerate(g["scores"]):
                        inst = pe.matmul(s[:, g["nk"] * u:g["nk"] * u + g["nk"]], q, k, start=True, stop=True)
                    inst.then_inc(att_s, 1)

                def turn(n):
                    pe.wait_ge(att_e, base + n + 1)
                    if base + n:
                        pe.wait_ge(att_tv, base + n)
                        pe.wait_ge(att_ta, base + n)
                    p = probs[:, (base + n) % 2, :]
                    for b in range(width(groups[n]) // P):
                        inst = transpose(psum[:, 4 + b // 4, P * (b % 4):P * (b % 4) + P], p[:, P * b:P * b + P])
                    inst.then_inc(att_t, 1)

                def values(n):
                    g = groups[n]
                    pe.wait_ge(att_tv, base + n + 1)
                    pe.wait_ge(att_ta, base + n + 1)
                    if base + n >= 2:
                        pe.wait_ge(att_o, base + n - 1)
                    pT, dv, b = probsT[:, (base + n) % 2, :], g["dv"], 0
                    o = psum[:, 6 + (base + n) % 2, :]
                    if "pv_all" in g:
                        inst = pe.matmul(o, pT[:, 0:P], g["pv_all"].rearrange("p h n -> p (h n)"), start=True, stop=True)
                    for u, vs in enumerate(g.get("pv", [])):
                        for m, vb in enumerate(vs):
                            inst = pe.matmul(o[:, dv * u:dv * u + dv], pT[:, P * b:P * b + P], vb, start=m == 0, stop=m == len(vs) - 1)
                            b += 1
                    inst.then_inc(att_pv, 1)

                scores(0)
                for n in range(len(groups)):
                    if n + 1 < len(groups):
                        scores(n + 1)
                    if n:
                        values(n - 1)
                    turn(n)
                values(len(groups) - 1)
                pe.wait_ge(att_o, att_n[0])

            def output(tiles, rows_in, gates_of=None):
                nt = len(tiles)
                pe.wait_ge(rows_ready, rws.next(rows_in))
                for k in range(KB):
                    if k % 2:
                        pe.wait_ge(a_free, a_done.value(back=3))
                        bank = a_bank()
                    else:
                        pe.wait_ge(v_free, v_done.value(back=3))
                        bank = v_bank()
                    for m in range(nt):
                        inst = transpose(bank[:, P * m:P * m + P], oA[:, m, P * k:P * k + P])
                    inst.then_inc(mm_a if k % 2 else mm_v, 1)
                if gates_of is not None:
                    gates(gates_of)
                pe.wait_ge(v_free, v_done.value())
                pe.wait_ge(a_free, a_done.value())
                for c in range(2):
                    w = k512(weights(2))
                    for m in range(nt):
                        columns512(w, m, m == nt - 1)

            def late_products(l, nt):
                s = late[l]
                loads, rows_v, rows_a, added = Tally(s["loaded"], 16), Tally(s["v"]), Tally(s["a"]), Tally(s["added"])
                chunk = [ring[:, j, :] for j in range(6)]
                up = [[chunk[2 * a + k // 4].rearrange("p (k n) -> p k n", k=4)[:, k % 4, :] for k in range(KB)] for a in range(2)]
                down = [chunk[4 + f // 2].rearrange("p (f n) -> p f n", f=2)[:, f % 2, :] for f in range(4)]
                pe.wait_ge(rounds_ready, l + 1)
                count = pe.value_load(late_rounds[0:1, 0:1], min_val=0, max_val=nt)
                per = {loads: 6, rows_v: 5, rows_a: 3, added: 2 * nt}
                with laps(pe, nt, {t: EXPERTS * n for t, n in per.items()}) as r:
                    with pe.If(count > r):
                        with laps(pe, EXPERTS, per):
                            pe.wait_ge(s["v"], rows_v.next())
                            for k in range(KB):
                                for m in range(nt):
                                    pe.matmul(psum[:, 5 + k // 4, P * (k % 4):P * (k % 4) + P], hrow[:, m, P * k:P * k + P], pick[:, 0, m, :],
                                              start=m == 0, stop=m == nt - 1)
                            for m in range(nt):
                                inst = transpose(psum[:, 0, P * m:P * m + P], share[:, 0, m, :])
                            inst.then_inc(s["product"], 1)
                            pe.wait_ge(s["loaded"], loads.next(6))
                            pe.wait_ge(s["a"], rows_a.next())
                            for bank, w in ((4, up[0]), (1, up[1])):
                                for k in range(KB):
                                    inst = pe.matmul(psum[:, bank, :], xgT[:, 0, k, :], w[k], start=k == 0, stop=k == KB - 1)
                            inst.then_inc(s["product"], 1)
                            pe.wait_ge(s["v"], rows_v.next(2))
                            for f in range(4):
                                inst = transpose(psum[:, 2, P * f:P * f + P], act_[:, P * f:P * f + P])
                            inst.then_inc(s["product"], 1)
                            pe.wait_ge(s["v"], rows_v.next())
                            for bank, h in ((7, 0), (3, 1)):
                                for f in range(4):
                                    inst = pe.matmul(psum[:, bank, :], actT[:, f, :], down[f][:, 512 * h:512 * h + 512], start=f == 0, stop=f == 3)
                            inst.then_inc(s["product"], 1)
                            pe.wait_ge(s["a"], rows_a.next(2))
                            pe.wait_ge(s["v"], rows_v.next())
                            for m in range(nt):
                                for h in range(2):
                                    inst = pe.matmul(psum[:, 2 * m + h, :], shareT[:, m, :], ySlot[:, 512 * h:512 * h + 512], start=True, stop=True)
                                    if not m and not h:
                                        inst.then_inc(s["free"], 1)
                            inst.then_inc(s["product"], 1)
                            pe.wait_ge(s["added"], added.next(2 * nt))
                    pe.end_ifs()

            def moe(l):
                nt = 4 - 2 * l
                norm(nt)
                pe.wait_ge(v_free, v_done.value())
                pe.wait_ge(a_free, a_done.value())
                pe.wait_ge(v_free, v_done.value(back=3))
                bank = v_bank()
                wr = pa("w_route", at=KB * ROUTES * l, width=KB * ROUTES).rearrange("p (k e) -> p k e", k=KB)
                for m in range(nt):
                    for k in range(KB):
                        inst = pe.matmul(bank[:, ROUTES * m:ROUTES * m + ROUTES], hT[:, k, P * m:P * m + P], wr[:, k, :],
                                         start=k == 0, stop=k == KB - 1)
                inst.then_inc(mm_v, 1)
                for m in range(nt):
                    for h in range(2):
                        pe.wait_ge(a_free, a_done.value(back=3))
                        bank = a_bank()
                        for k in range(4):
                            inst = transpose(bank[:, P * k:P * k + P], hT[:, 4 * h + k, P * m:P * m + P])
                        inst.then_inc(mm_a, 1)
                pe.wait_ge(chosen, choice.next())
                pe.wait_ge(v_free, v_done.value(back=3))
                bank = v_bank()
                for m in range(nt):
                    out = bank[:, EXPERTS * m:EXPERTS * m + EXPERTS]
                    for j in range(m):
                        pe.matmul(out, co("ones"), route[:, 11, j, 0:EXPERTS], start=j == 0, stop=False)
                    pe.matmul(out, co("before"), route[:, 11, m, 0:EXPERTS], start=m == 0, stop=True)
                for m in range(nt):
                    inst = pe.matmul(bank[:, EXPERTS * nt:EXPERTS * nt + EXPERTS], co("ones"), route[:, 11, m, 0:EXPERTS],
                                     start=m == 0, stop=m == nt - 1)
                inst.then_inc(mm_v, 1)
                pe.wait_ge(v_free, v_done.value())
                pe.wait_ge(a_free, a_done.value())

                def gather(b, h, first=False):
                    for k in range(4):
                        for m in range(nt):
                            kk = 4 * h + k
                            inst = pe.matmul(psum[:, 5 + h, P * k:P * k + P], hrow[:, m, P * kk:P * kk + P], pick[:, b, m, :],
                                             start=m == 0, stop=m == nt - 1)
                            if first and l == 0 and kk + m == 0:
                                inst.then_inc(mod_free, 1)
                    inst.then_inc(mm_a, 1)
                    a_done.n += 1

                def up(out, b):
                    for k in range(KB):
                        if k in (0, 4):
                            w = weights(2)
                        for e in range(2):
                            m = w[e].rearrange("p (k n) -> p k n", k=4)[:, k % 4, :]
                            inst = pe.matmul(out[64 * e:64 * e + 64, :], xgT[:, b, k, 64 * e:64 * e + 64], m,
                                             start=k == 0, stop=k == KB - 1)
                            if k in (3, 7):
                                inst.then_inc(used, 1)

                def add_pair():
                    pe.wait_ge(v_free, v_done.value())
                    pe.wait_ge(a_free, a_done.value())
                    for m in range(nt):
                        for h in range(2):
                            pe.wait_ge(v_free, v_done.value(back=3))
                            bank = v_bank()
                            pe.matmul(bank, shareT[:, m, :], ySlot[:, 512 * h:512 * h + 512], start=True, stop=True).then_inc(mm_v, 1)

                pe.wait_ge(pick_ready, picks.next())
                for h in range(2):
                    gather(0, h, first=True)
                base = vi[0]
                vi[0] = 0
                per_pair = 4 + 2 * nt
                tallies = {v_done: 2 * per_pair, a_done: 6, picks: 2}
                tallies.update({c: 24 // RING for c in chunk_in})
                if l == 0:
                    tallies.update({mod_in: 2, mod_out: 2})
                with laps(pe, PAIRS // 2, tallies):
                    for b in range(2):
                        pe.wait_ge(a_free, a_done.value())
                        up(psum[:, 4, :], b)
                        add_pair()
                        if l == 0 and b == 1:
                            pe.wait_ge(mod_loaded, mod_in.next(2))
                            mod_block(psum[:, 7, :], [mod_w[k // 4][:, k % 4, :] for k in range(KB)], mod_product)
                            mod_out.n += 1
                        pe.wait_ge(v_free, v_done.value(back=3))
                        bank = v_bank()
                        up(bank, b)
                        if l == 0 and b == 1:
                            pe.wait_ge(mod_taken, mod_out.value())
                            folded(psum[:, 7, :], mod_sums).then_inc(mod_product, 1)
                            mod_out.n += 1
                        pe.wait_ge(pick_ready, picks.next())
                        gather(1 - b, 0)
                        pe.wait_ge(v_free, v_done.value())
                        bank = v_bank()
                        for f in range(4):
                            inst = transpose(bank[:, P * f:P * f + P], act_[:, P * f:P * f + P])
                        inst.then_inc(mm_v, 1)
                        gather(1 - b, 1)
                        bank = v_bank()
                        for m in range(nt):
                            inst = transpose(bank[:, P * m:P * m + P], share[:, b, m, :])
                        inst.then_inc(mm_v, 1)
                        pe.wait_ge(v_free, v_done.value(back=1))
                        if l == 0 and b == 1:
                            pe.wait_ge(mod_taken, mod_out.value())
                        outs = [psum[:, 7, :], v_bank()]
                        for f in range(4):
                            if f in (0, 2):
                                w = weights(2)
                            for h in range(2):
                                for e in range(2):
                                    m = w[e].rearrange("p (k n) -> p k n", k=2)[:, f % 2, 512 * h:512 * h + 512]
                                    inst = pe.matmul(outs[h][64 * e:64 * e + 64, :], actT[:, f, 64 * e:64 * e + 64], m,
                                                     start=f == 0, stop=f == 3)
                                    if l == 0 and b == 1 and f + h + e == 0:
                                        inst.then_inc(mod_free, 1)
                                    if h and f % 2:
                                        inst.then_inc(used, 1)
                                if not h and f == 3:
                                    inst.then_inc(mm_a, 1)
                                    a_done.n += 1
                add_pair()
                vi[0] = base + PAIRS * per_pair + 2 * nt
                pe.wait_ge(pick_ready, picks.next())
                pe.wait_ge(v_free, v_done.value())
                pe.wait_ge(a_free, a_done.value())
                late_products(l, nt)

            def turn(parts):
                pe.wait_ge(rows_ready, rws.next())
                for part in parts:
                    pe.wait_ge(a_free, a_done.value(back=3))
                    bank = a_bank()
                    for j, x in enumerate(part):
                        inst = transpose(bank[0:x.shape[-1], P * j:P * j + P], x)
                    inst.then_inc(mm_a, 1)

            def project2():
                def blocks(x, w=P):
                    return [x[:, w * j:w * j + w] for j in range(x.shape[-1] // w)]

                def turned(c, m):
                    if c == 0:
                        turn([blocks(R[m])])
                    elif c == 1:
                        b = blocks(KD[m].rearrange("p b s n -> p (b s n)"))
                        turn([b[0:4], b[4:6]])
                    elif c == 2:
                        turn([blocks(KWD[m].rearrange("p b s n -> p (b s n)"))])
                    else:
                        turn([blocks(CQ[m])])

                pe.wait_ge(v_free, v_done.value())
                pe.wait_ge(a_free, a_done.value())
                waiting = []
                for c in range(4):
                    n = min(512, IN2 - 512 * c)
                    w = [x[:, 0:4 * n].rearrange("p (k n) -> p k n", k=4) for x in weights(2)]
                    for m in range(2):
                        pe.wait_ge(v_free, v_done.value(back=3))
                        bank = v_bank()
                        for k in range(KB):
                            inst = pe.matmul(bank[:, 0:n], hT[:, k, P * m:P * m + P], w[k // 4][:, k % 4, :], start=k == 0, stop=k == KB - 1)
                            if m and k == 3:
                                inst.then_inc(used, 1)
                        inst.then_inc(used if m else mm_v, 1)
                        if waiting:
                            turned(*waiting.pop())
                        waiting.append((c, m))
                turned(*waiting.pop())
                pe.wait_ge(v_free, v_done.value())
                pe.wait_ge(a_free, a_done.value())
                w = weights(1)[0][:, 0:1536].rearrange("p (k n) -> p k n", k=2)
                for m in range(2):
                    for a, b in ((0, 512), (512, 768)):
                        pe.wait_ge(v_free, v_done.value(back=3))
                        bank = v_bank()
                        for k in range(2):
                            inst = pe.matmul(bank[:, 0:b - a], cqT[:, k, P * m:P * m + P], w[:, k, a:b], start=k == 0, stop=k == 1)
                        inst.then_inc(used if m and a else mm_v, 1)
                for m in range(2):
                    b = blocks(rows[:, m, 0:768], MLA_D)
                    turn([b[0:4], b[4:8]])
                w = weights(1)[0][:, 0:1024]
                for m in range(2):
                    for j in range(2):
                        pe.wait_ge(v_free, v_done.value(back=3))
                        bank = v_bank()
                        inst = pe.matmul(bank, cqT[:, 2, P * m:P * m + P], w[:, 512 * j:512 * j + 512], start=True, stop=True)
                        inst.then_inc(used if m and j else mm_v, 1)
                for m in range(2):
                    b = blocks(rows[:, 2 + m, 0:768], MLA_D)
                    turn([b[0:4], b[4:8]])

            def compress():
                for s in range(2):
                    pe.wait_ge(rows_ready, rws.next())
                    w = weights(2)
                    pe.wait_ge(a_free, a_done.value(back=3))
                    bank = a_bank()
                    for c in range(16):
                        inst = pe.matmul(bank[0:30, 0:256], XB[:, s, c].rearrange("p g i -> p (g i)"),
                                         w[c // 8].rearrange("p (c n) -> p c n", c=8)[:, c % 8, :], start=c == 0, stop=c == 15)
                        if c % 8 == 7:
                            inst.then_inc(used, 1)
                pe.wait_ge(a_free, a_done.value())
                pe.wait_ge(v_free, v_done.value(back=3))
                bank = v_bank()
                for s in range(2):
                    for j in range(2):
                        at = 32 * (2 * s + j)
                        inst = pe.transpose(bank[:, at:at + 30], hid[0:30, s, P * j:P * j + P], ident[0:30, 0:30])
                inst.then_inc(mm_v, 1)
                pe.wait_ge(v_free, v_done.value())
                pe.wait_ge(v_free, v_done.value(back=3))
                bank = v_bank()
                k2 = pa("cmp_w2k", at=256 * layer[0], width=256).rearrange("p (j n) -> p j n", j=2)
                v2 = pa("cmp_w2v", at=P * layer[0], width=P).rearrange("p (j n) -> p j n", j=2)
                for j in range(2):
                    pe.matmul(bank[:, 0:30], k2[:, j, :], hidT[:, j, 0:30], start=j == 0, stop=j == 1)
                for j in range(2):
                    inst = pe.matmul(bank[:, 64:128], hv[:, j].rearrange("p h n -> p (h n)"), v2[:, j, :], start=j == 0, stop=j == 1)
                inst.then_inc(mm_v, 1)
                layer[0] += 1

            layer = [0]

            def mlp():
                pe.wait_ge(v_free, v_done.value())
                pe.wait_ge(a_free, a_done.value())
                for c in range(8):
                    w = k512(weights(2))
                    for b in range(2):
                        if b:
                            pe.wait_ge(v_free, v_done.value(back=3))
                            bank = v_bank()
                        else:
                            pe.wait_ge(a_free, a_done.value(back=3))
                            bank = a_bank()
                        for f in range(2):
                            at = P * (2 * b + f)
                            for k in range(KB):
                                inst = pe.matmul(bank[:, SEQ * f:SEQ * f + SEQ], w[k][:, at:at + P], hT[:, k, 0:SEQ],
                                                 start=k == 0, stop=k == KB - 1)
                                if b and f and k == 3:
                                    inst.then_inc(used, 1)
                        inst.then_inc(used if b else mm_a, 1)
                pe.wait_ge(v_free, v_done.value())
                pe.wait_ge(a_free, a_done.value())
                banks = [v_bank() for _ in range(4)]
                for c in range(16):
                    w = weights(1)[0].rearrange("p (k n) -> p k n", k=2)
                    for f in range(2):
                        for m in range(2):
                            for h in range(2):
                                inst = pe.matmul(banks[2 * m + h], aT[:, 2 * c + f, P * m:P * m + P], w[:, f, 512 * h:512 * h + 512],
                                                 start=c == 0 and f == 0, stop=c == 15 and f == 1)
                                if f and m and h:
                                    inst.then_inc(used, 1)
                                elif f and c == 15:
                                    inst.then_inc(mm_v, 1)

            all4 = [0, 1, 2, 3]
            pe.wait_ge(c_ready, 1)
            pe.wait_ge(consts_in, 16)
            for c in (0, 2):
                mod_products(c)
                mod_folds(c)
            norm(4)
            heads(3, lambda c: all4, turn_ab, modulate=True)
            attention(groups_ab())
            mod_products(10)
            mod_folds(10)
            output(all4, 0, gates_of=0)
            moe(0)
            for c in range(PAIRS // 2, MOD_BLOCKS, 2):
                mod_products(c)
                mod_folds(c)
            norm(4)
            gates(1)
            heads(6, lambda c: [2, 3] if c < 2 else all4, turn_c)
            attention(groups_c())
            output([2, 3], 2)
            moe(1)
            for l in range(DEPTH):
                norm(2)
                project2()
                compress()
                attention(groups_2())
                output([2, 3], 2)
                norm(2)
                mlp()

        @block.sync
        def _(sp):
            freed = Tally(used)
            count = [0]

            def load(src):
                slot = count[0] % RING
                if count[0] >= RING:
                    freed.n = count[0] - RING + 1
                    sp.wait_ge(used, freed.value())
                dst = ring[:, slot, 0:src.shape[1] * src.shape[2]].rearrange("p (k n) -> p k n", k=src.shape[1])
                sp.dma_start(dst, src).then_inc(loaded[slot], 16)
                count[0] += 1

            def matrix(w, cols, first=0):
                for c in range(first, cols):
                    for src in cols512(w, c):
                        load(src)

            def experts(l):
                before = count[0]
                places = Tally(mod_free)
                places.n = 1
                with sp.Fori(0, PAIRS // 2) as i:
                    freed.laps, places.laps = [(i, 24)], [(i, 1)]
                    for b in range(2):
                        for j in range(12):
                            expert = bass.ds(4 * i + 2 * b + j % 2, 1)
                            if j < 8:
                                src = t["w1" if j < 4 else "w3"][l, expert, 512 * (j // 2 % 2):512 * (j // 2 % 2) + 512, :]
                            else:
                                m = (j - 8) // 2
                                src = t["w2"][l, expert, 256 * m:256 * m + 256, :]
                            load(src.rearrange("o (k p) n -> p (o k) n", p=P))
                            if l == 0 and b == 1 and j == 3:
                                sp.wait_ge(mod_free, places.value())
                                for h in range(2):
                                    src = t["w_mod"][1, 512 * h:512 * h + 512, bass.ds(512 * i, 512)]
                                    sp.dma_start(mod_w[h], src.rearrange("(k p) n -> p k n", p=P)).then_inc(mod_loaded, 16)
                    freed.laps = []
                count[0] = before + 12 * PAIRS
                nt = 4 - 2 * l
                free = Tally(late[l]["free"])
                sp.wait_ge(rounds_ready, l + 1)
                rounds = sp.value_load(late_rounds[0:1, 0:1], min_val=0, max_val=nt)
                free.n = 1
                with laps(sp, nt, {free: EXPERTS}) as r:
                    with sp.If(rounds > r):
                        freed.n = count[0]
                        sp.wait_ge(used, freed.value())
                        with laps(sp, EXPERTS, {free: 1}) as e:
                            sp.wait_ge(late[l]["free"], free.value())
                            for j in range(6):
                                if j < 4:
                                    src = t["w1" if j < 2 else "w3"][l, bass.ds(e, 1), 512 * (j % 2):512 * (j % 2) + 512, :]
                                else:
                                    src = t["w2"][l, bass.ds(e, 1), 256 * (j - 4):256 * (j - 4) + 256, :]
                                dst = ring[:, j, :].rearrange("p (k n) -> p k n", k=4 if j < 4 else 2)
                                sp.dma_start(dst, src.rearrange("o (k p) n -> p (o k) n", p=P)).then_inc(late[l]["loaded"], 16)
                            free.n += 1
                    sp.end_ifs()
                sp.wait_ge(late[l]["free"], rounds * EXPERTS + 1)

            def project2(l):
                for c in range(4):
                    n = min(512, IN2 - 512 * c)
                    for h in range(2):
                        load(t["w_in_2"][l, 512 * h:512 * h + 512, 512 * c:512 * c + n].rearrange("(k p) n -> p k n", p=P))
                load(t["w_q_up_2"][l].rearrange("(k p) n -> p k n", p=P))
                load(t["w_kv_up_2"][l].rearrange("(k p) n -> p k n", p=P))

            def compress(l):
                for w in ("cmp_w1_k_2", "cmp_w1_v_2"):
                    for h in range(2):
                        load(t[w][l, 1024 * h:1024 * h + 1024, :].rearrange("(k p) n -> p k n", p=P))

            def mlp(l):
                matrix(t["w_ff1_2"][l], 8)
                for c in range(16):
                    load(rows256(t["w_ff2_2"][l], c))

            matrix(t["w_mod"][0], 2)
            sp.dma_start(X[:, 2:4, :], t["x"][0].rearrange("(t p) n -> p t n", p=P)).then_inc(x_in, 16)
            sp.dma_start(X[:, 0:2, :], t["ctx"][0].rearrange("(t p) n -> p t n", p=P)).then_inc(x_in, 16)
            matrix(t["w_mod"][0], 4, 2)
            for c in range(3):
                matrix(t["w_in_ab"][0], c + 1, c)
                matrix(t["w_mod"][0], 6 + 2 * c, 4 + 2 * c)
            matrix(t["w_mod"][0], 12, 10)
            matrix(t["w_out_ab"][0], 2)
            experts(0)
            matrix(t["w_mod"][1], MOD_BLOCKS, PAIRS // 2)
            matrix(t["w_in_c"][0], 6)
            matrix(t["w_out_c"][0], 2)
            experts(1)
            for l in range(DEPTH):
                project2(l)
                compress(l)
                matrix(t["w_out_2"][l], 2)
                mlp(l)
            sp.wait_ge(x_ready, 8)
            sp.dma_start(arena[:, 0:D], t["final_norm_2"].rearrange("(a n) -> a n", a=1).to_broadcast([P, D])).then_inc(final_in, 16)
            for m in range(2):
                sp.wait_ge(x_ready, 9 + m)
                sp.dma_start(t["out"][0, P * m:P * m + P, :], rows[:, m, :]).then_inc(out_done, 16)
            sp.wait_ge(out_done, 32)



def lay_out(inputs):
    g = {k: np.asarray(v) for k, v in inputs.items()}

    def by_feature(v):
        v = v.reshape(-1, P)
        return v.T

    def everywhere(v):
        return np.broadcast_to(v.reshape(1, -1), (P, v.size))

    def blocks(w):
        w = w.reshape(-1, P, w.shape[-1])
        return w.transpose(1, 0, 2).reshape(P, -1)

    cc = np.stack([g["c"][0], g["c_ctx"]], -1)
    heads = np.concatenate([g[n][0] for n in ("qn_a", "kn_a", "qn_b", "kn_b", "qn_c", "kn_c")])
    v = {
        "c": blocks(cc), "norm_mix": by_feature(g["norm_mix"]), "norm_ffn": by_feature(g["norm_ffn"]),
        "head_gain": everywhere(heads), "sink": everywhere(g["sink_a"]), "lam": everywhere(g["lam_c"]),
        "subln": by_feature(g["subln_c"]),
        "w_route": blocks(np.concatenate([g["w_group"], g["w_expert"]], -1)),
        "b_route": everywhere(np.concatenate([g["b_group"], g["b_expert"]], -1)),
        "attn_norm": by_feature(g["attn_norm_2"]), "q_norm": by_feature(g["mla_q_norm_2"]),
        "kv_norm": by_feature(g["mla_kv_norm_2"]), "b_mod": by_feature(g["b_mod"]),
        "mix_norm": by_feature(np.concatenate([g["nsa_out_norm_2"], g["mla_out_norm_2"]], -1)),
        "mlp_norm": by_feature(g["mlp_norm_2"]),
        "pos_k": by_feature(g["cmp_pos_k_2"]), "pos_v": by_feature(g["cmp_pos_v_2"]),
        "cmp_w2k": blocks(np.concatenate([g["cmp_w2_k_2"]] * 2, -1)), "cmp_w2v": blocks(g["cmp_w2_v_2"]),
    }
    for n, w in PARAMS:
        assert v[n].shape == (P, w), (n, v[n].shape, w)
    return np.ascontiguousarray(np.concatenate([v[n] for n, _ in PARAMS], 1))


WEIGHTS = ["x", "ctx", "w_mod", "w_in_ab", "w_out_ab", "w_in_c", "w_out_c", "w1", "w3", "w2",
           "w_in_2", "w_q_up_2", "w_kv_up_2", "cmp_w1_k_2", "cmp_w1_v_2", "w_out_2", "w_ff1_2", "w_ff2_2", "final_norm_2"]


def arrays_of(inputs):
    arrays = {n: np.ascontiguousarray(inputs[n]) for n in WEIGHTS}
    arrays["params"] = lay_out(inputs)
    arrays["consts"] = np.ascontiguousarray(constants())
    return arrays


def kernel(**inputs):
    import concourse.bacc as bacc
    from concourse.bass_utils import run_bass_kernel_spmd

    nc = bacc.Bacc("TRN2", target_bir_lowering=False, num_devices=1)
    arrays = arrays_of(inputs)
    t = {n: nc.dram_tensor("in_" + n, a.shape, mybir.dt.from_np(a.dtype), kind="ExternalInput").ap() for n, a in arrays.items()}
    t["out"] = nc.dram_tensor("out", (1, SEQ, D), mybir.dt.float32, kind="ExternalOutput").ap()
    build(nc, t)
    r = run_bass_kernel_spmd(nc, [{"in_" + n: a for n, a in arrays.items()}], core_ids=[0])
    return r.results[0]["out"]
```
